# Optimizing a Trainium2 kernel written in Bass

```python
import math
import jax, jax.numpy as jnp
from jax import lax
import numpy as np

D_MODEL = 1024
BATCH = 1
SEQ = 256
DEPTH = 2

GRID_W = 64
CTX_LEN = 256
EPS = 1e-6
ROPE_BASE = 10000.0
F32 = jnp.float32

ML_HEADS = 4
ML_QK = 128
ML_V = 256
ML_CHUNK = 64
ML_QKW = ML_HEADS * ML_QK
ML_W = ML_HEADS * ML_V

SSD_HEADS = 16
SSD_P = 64
SSD_N = 64
SSD_GROUPS = 2
SSD_HPG = SSD_HEADS // SSD_GROUPS
SSD_CONV = 5
SSD_CHUNK = 64
SSD_W = SSD_HEADS * SSD_P
SSD_GN = SSD_GROUPS * SSD_N
SSD_XBC = SSD_W + 2 * SSD_GN

MLA_HEADS = 8
MLA_NOPE = 64
MLA_ROPE = 32
MLA_V = 64
MLA_Q_RANK = 384
MLA_KV_RANK = 256
MLA_SCALE = (MLA_NOPE + MLA_ROPE) ** -0.5
Q_BLOCK = 128

RW_HEADS = 16
RW_N = 64
RW_DECAY_RANK = 64
RW_A_RANK = 64
RW_GATE_RANK = 128
RW_W = RW_HEADS * RW_N

N_EXPERTS = 16
N_GROUPS = 4
EXPERTS_PER_GROUP = N_EXPERTS // N_GROUPS
TOP_K = 2
EXPERT_FF = 512

AB_SPLITS = (ML_QKW, ML_QKW, ML_W, ML_W, 2 * ML_HEADS, 2 * ML_HEADS, SSD_W, SSD_XBC, 2 * SSD_HEADS)
AB_IN = sum(AB_SPLITS)
AB_OUT = ML_W + SSD_W
MLA_SPLITS = (MLA_Q_RANK, MLA_KV_RANK, MLA_ROPE)
MLA_IN = sum(MLA_SPLITS)
RW_SPLITS = (RW_W, RW_W, RW_W, 2 * RW_DECAY_RANK, 2 * RW_A_RANK, RW_GATE_RANK)
RW_IN = sum(RW_SPLITS)
CD_IN = MLA_IN + RW_IN
CD_OUT = MLA_HEADS * MLA_V + RW_W

kernel_name = "hybrid_mlstm_ssd_mla_rwkv7_grouped_moe_dit"

def rmsnorm(x, w):
    xf = x.astype(F32)
    y = xf * lax.rsqrt(jnp.mean(xf * xf, axis=-1, keepdims=True) + EPS)
    return y.astype(x.dtype) * w

def head_rmsnorm(h, w):
    hf = h.astype(F32)
    y = hf * lax.rsqrt(jnp.mean(hf * hf, axis=-1, keepdims=True) + EPS)
    return y.reshape(*h.shape[:2], -1) * w

def split_cols(p, sizes):
    return jnp.split(p, [int(i) for i in np.cumsum(sizes)[:-1]], axis=-1)

def to_heads(t, n):
    return t.reshape(*t.shape[:-1], n, t.shape[-1] // n)

def to_chunks(t, L):
    B, T = t.shape[:2]
    return jnp.moveaxis(t.reshape(B, T // L, L, *t.shape[2:]), 1, 0)

def from_chunks(t):
    nc, B, L = t.shape[:3]
    return jnp.moveaxis(t, 0, 1).reshape(B, nc * L, *t.shape[3:])

def dwconv_centred(x, w, b):
    y = lax.conv_general_dilated(x, w[:, None, :].astype(x.dtype), (1,), 'SAME',
                                 dimension_numbers=('NWC', 'WIO', 'NWC'),
                                 feature_group_count=x.shape[-1])
    return y + b

def centred_shift(x):
    prev = jnp.pad(x, ((0, 0), (1, 0), (0, 0)))[:, :-1]
    nxt = jnp.pad(x, ((0, 0), (0, 1), (0, 0)))[:, 1:]
    return 0.5 * (prev + nxt)

def axial_angles(n_rows):
    row = jnp.repeat(jnp.arange(n_rows, dtype=F32), GRID_W)
    col = jnp.tile(jnp.arange(GRID_W, dtype=F32), n_rows)
    n_freq = MLA_ROPE // 4
    inv = ROPE_BASE ** (-jnp.arange(n_freq, dtype=F32) / n_freq)
    return jnp.concatenate([row[:, None] * inv, col[:, None] * inv], axis=-1)

def apply_rope(x, ang):
    x1, x2 = jnp.split(x, 2, axis=-1)
    cos, sin = jnp.cos(ang).astype(x.dtype), jnp.sin(ang).astype(x.dtype)
    return jnp.concatenate([x1 * cos - x2 * sin, x1 * sin + x2 * cos], axis=-1)

def attend_blocked(q, k, v):
    B, S, H, d = q.shape
    qb = jnp.moveaxis(q.reshape(B, S // Q_BLOCK, Q_BLOCK, H, d), 1, 0)

    def block(qi):
        s = jnp.einsum('bqhd,bkhd->bhqk', qi, k).astype(F32)
        p = jax.nn.softmax(s, axis=-1).astype(v.dtype)
        return jnp.einsum('bhqk,bkhv->bqhv', p, v)

    return from_chunks(lax.map(block, qb))

def prefixed_bidir(scan_fn, ctx_fwd, lat_fwd, ctx_bwd, lat_bwd, init):
    flip = lambda ts: tuple(jnp.flip(t, axis=1) for t in ts)
    yc_f, st_f = scan_fn(*ctx_fwd, init)
    yl_f, _ = scan_fn(*lat_fwd, st_f)
    yc_b, st_b = scan_fn(*flip(ctx_bwd), init)
    yl_b, _ = scan_fn(*flip(lat_bwd), st_b)
    return yc_f + jnp.flip(yc_b, axis=1), yl_f + jnp.flip(yl_b, axis=1)

def mlstm_chunked(q, k, v, ig, lf, state):
    L = ML_CHUNK
    mask = jnp.tril(jnp.ones((L, L), bool))[None, :, :, None]

    def step(carry, inp):
        C, n, m = carry
        qc, kc, vc, ic, fc = inp
        b = jnp.cumsum(fc, axis=1)
        logD = jnp.where(mask, b[:, :, None, :] - b[:, None, :, :] + ic[:, None, :, :], -jnp.inf)
        inter = b + m[:, None, :]
        m_j = jnp.maximum(inter, jnp.max(logD, axis=2))
        s = jnp.einsum('bjhd,bshd->bjsh', qc, kc) * jnp.exp(logD - m_j[:, :, None, :])
        w_int = jnp.exp(inter - m_j)
        num = jnp.einsum('bjsh,bshv->bjhv', s, vc) + w_int[..., None] * jnp.einsum('bhvd,bjhd->bjhv', C, qc)
        den = jnp.sum(s, axis=2) + w_int * jnp.einsum('bhd,bjhd->bjh', n, qc)
        h = num / jnp.maximum(jnp.abs(den), jnp.exp(-m_j))[..., None]
        logE = b[:, -1:, :] - b + ic
        m_new = jnp.maximum(b[:, -1] + m, jnp.max(logE, axis=1))
        E = jnp.exp(logE - m_new[:, None, :])
        dec = jnp.exp(b[:, -1] + m - m_new)
        C = dec[..., None, None] * C + jnp.einsum('bsh,bshv,bshd->bhvd', E, vc, kc)
        n = dec[..., None] * n + jnp.einsum('bsh,bshd->bhd', E, kc)
        return (C, n, m_new), h

    state, hs = lax.scan(step, state, tuple(to_chunks(t, L) for t in (q, k, v, ig, lf)))
    return from_chunks(hs), state

def ssd_chunked(x, dt, la, bm, cm, state):
    B, T = x.shape[:2]
    L = SSD_CHUNK
    x = x.reshape(B, T, SSD_GROUPS, SSD_HPG, SSD_P)
    dt = dt.reshape(B, T, SSD_GROUPS, SSD_HPG)
    la = la.reshape(B, T, SSD_GROUPS, SSD_HPG)
    mask = jnp.tril(jnp.ones((L, L), bool))[None, :, :, None, None]

    def step(S, inp):
        xc, dtc, lac, bc, cc = inp
        b = jnp.cumsum(lac, axis=1)
        seg = jnp.exp(jnp.where(mask, b[:, :, None] - b[:, None, :], -jnp.inf))
        cb = jnp.einsum('bjgn,bsgn->bjsg', cc, bc)
        w = cb[..., None] * seg * dtc[:, None]
        y = jnp.einsum('bjsgh,bsghp->bjghp', w, xc) + jnp.exp(b)[..., None] * jnp.einsum('bghpn,bjgn->bjghp', S, cc)
        e = jnp.exp(b[:, -1:] - b) * dtc
        S = jnp.exp(b[:, -1])[..., None, None] * S + jnp.einsum('bsgh,bsghp,bsgn->bghpn', e, xc, bc)
        return S, y

    state, ys = lax.scan(step, state, tuple(to_chunks(t, L) for t in (x, dt, la, bm, cm)))
    return from_chunks(ys).reshape(B, T, SSD_HEADS, SSD_P), state

def rwkv7_scan(r, w, k, v, a, b, state):
    def step(S, inp):
        r_t, w_t, k_t, v_t, a_t, b_t = inp
        sa = jnp.einsum('bhvk,bhk->bhv', S, a_t)
        S = S * w_t[:, :, None, :] + sa[..., None] * b_t[:, :, None, :] + v_t[..., None] * k_t[:, :, None, :]
        return S, jnp.einsum('bhvk,bhk->bhv', S, r_t)

    state, ys = lax.scan(step, state, tuple(jnp.moveaxis(t, 1, 0) for t in (r, w, k, v, a, b)))
    return jnp.moveaxis(ys, 0, 1), state

def mixer_ab(u_c, u_l, w_in, w_out, ml_i_bias, ml_f_bias, ml_norm, ssd_conv_w, ssd_conv_b,
             ssd_dt_bias, ssd_a_log, ssd_d, ssd_norm, with_ctx_out):
    Bsz = u_l.shape[0]
    p_c = split_cols(u_c @ w_in, AB_SPLITS)
    p_l = split_cols(u_l @ w_in, AB_SPLITS)

    def ml_dirs(p):
        q = to_heads(p[0].astype(F32), ML_HEADS) * ML_QK ** -0.5
        k = to_heads(p[1].astype(F32), ML_HEADS)
        v = to_heads(p[2].astype(F32), ML_HEADS)
        ig = to_heads(p[4].astype(F32), 2)
        fg = to_heads(p[5].astype(F32), 2)
        return [(q, k, v, ig[..., d, :] + ml_i_bias[d], jax.nn.log_sigmoid(fg[..., d, :] + ml_f_bias[d])) for d in range(2)]

    mc_f, mc_b = ml_dirs(p_c)
    mlf, mlb = ml_dirs(p_l)
    ml_init = (jnp.zeros((Bsz, ML_HEADS, ML_V, ML_QK), F32), jnp.zeros((Bsz, ML_HEADS, ML_QK), F32),
               jnp.zeros((Bsz, ML_HEADS), F32))
    h_c, h_l = prefixed_bidir(mlstm_chunked, mc_f, mlf, mc_b, mlb, ml_init)

    def ml_out(h, p):
        return head_rmsnorm(h, ml_norm) * jax.nn.sigmoid(p[3].astype(F32))

    def ssd_dirs(p):
        xbc = jax.nn.silu(dwconv_centred(p[7], ssd_conv_w, ssd_conv_b)).astype(F32)
        xs, bm, cm = split_cols(xbc, (SSD_W, SSD_GN, SSD_GN))
        xs, bm, cm = to_heads(xs, SSD_HEADS), to_heads(bm, SSD_GROUPS), to_heads(cm, SSD_GROUPS)
        dt_raw = to_heads(p[8].astype(F32), 2)
        out = []
        for d in range(2):
            dt = jax.nn.softplus(dt_raw[..., d, :] + ssd_dt_bias[d])
            out.append((xs, dt, -dt * jnp.exp(ssd_a_log[d]), bm, cm))
        return out

    sc_f, sc_b = ssd_dirs(p_c)
    sl_f, sl_b = ssd_dirs(p_l)
    ssd_init = jnp.zeros((Bsz, SSD_GROUPS, SSD_HPG, SSD_P, SSD_N), F32)
    y_c, y_l = prefixed_bidir(ssd_chunked, sc_f, sl_f, sc_b, sl_b, ssd_init)

    def ssd_out(y, xs, p):
        y = (y + ssd_d[:, None] * xs).reshape(*y.shape[:2], SSD_W)
        return rmsnorm(y * jax.nn.silu(p[6].astype(F32)), ssd_norm)

    mix_l = jnp.concatenate([ml_out(h_l, p_l), ssd_out(y_l, sl_f[0], p_l)], axis=-1).astype(u_l.dtype) @ w_out
    mix_c = None
    if with_ctx_out:
        mix_c = jnp.concatenate([ml_out(h_c, p_c), ssd_out(y_c, sc_f[0], p_c)], axis=-1).astype(u_c.dtype) @ w_out
    return mix_c, mix_l

def mixer_cd(u_c, u_l, ang, w_in, w_out, mla_qn, mla_w_uq, mla_kvn, mla_w_ukv, rw_mu, rw_w0, rw_w2,
             rw_a0, rw_a2, rw_g2, rw_kk, rw_ka, rw_rk, rw_ln, with_ctx_out):
    Bsz, S = u_l.shape[:2]

    def project(u):
        p = u @ w_in
        p_mla, p_rw = p[..., :MLA_IN], p[..., MLA_IN:].astype(F32)
        p_rw = p_rw + rw_mu * (centred_shift(p_rw) - p_rw)
        return split_cols(p_mla, MLA_SPLITS), split_cols(p_rw, RW_SPLITS)

    (m_c, r_c), (m_l, r_l) = project(u_c), project(u_l)

    def mla_q(m, rotate):
        q = to_heads(rmsnorm(m[0], mla_qn) @ mla_w_uq, MLA_HEADS)
        q_nope, q_rope = q[..., :MLA_NOPE], q[..., MLA_NOPE:]
        if rotate:
            q_rope = apply_rope(q_rope, ang[:, None, :])
        return jnp.concatenate([q_nope, q_rope], axis=-1) * MLA_SCALE

    def mla_kv(m, rotate):
        kv = to_heads(rmsnorm(m[1], mla_kvn) @ mla_w_ukv, MLA_HEADS)
        k_nope, v = kv[..., :MLA_NOPE], kv[..., MLA_NOPE:]
        kr = apply_rope(m[2], ang) if rotate else m[2]
        k_rope = jnp.broadcast_to(kr[:, :, None, :], (*kr.shape[:2], MLA_HEADS, MLA_ROPE))
        return jnp.concatenate([k_nope, k_rope], axis=-1), v

    k_c, v_c = mla_kv(m_c, False)
    k_l, v_l = mla_kv(m_l, True)
    att_l = attend_blocked(mla_q(m_l, True), jnp.concatenate([k_c, k_l], axis=1),
                           jnp.concatenate([v_c, v_l], axis=1))

    def rw_dirs(p):
        r, k, v, w_low, a_low, _ = p
        kk = to_heads(k * rw_kk, RW_HEADS)
        kk = kk / jnp.maximum(jnp.sqrt(jnp.sum(kk * kk, axis=-1, keepdims=True)), 1e-12)
        w_low, a_low = to_heads(w_low, 2), to_heads(a_low, 2)
        out = []
        for d in range(2):
            w_log = -jax.nn.softplus(-(rw_w0[d] + jnp.tanh(w_low[..., d, :]) @ rw_w2[d])) - 0.5
            a = jax.nn.sigmoid(rw_a0[d] + a_low[..., d, :] @ rw_a2[d])
            k_d = k * (1 + (a - 1) * rw_ka)
            out.append((to_heads(r, RW_HEADS), to_heads(jnp.exp(-jnp.exp(w_log)), RW_HEADS),
                        to_heads(k_d, RW_HEADS), to_heads(v, RW_HEADS), -kk, kk * to_heads(a, RW_HEADS)))
        return out

    rc_f, rc_b = rw_dirs(r_c)
    rl_f, rl_b = rw_dirs(r_l)
    rw_init = jnp.zeros((Bsz, RW_HEADS, RW_N, RW_N), F32)
    o_c, o_l = prefixed_bidir(rwkv7_scan, rc_f, rl_f, rc_b, rl_b, rw_init)

    def rw_out(o, p, dirs):
        bonus = sum(jnp.sum(dd[0] * dd[2] * rw_rk, axis=-1, keepdims=True) * dd[3] for dd in dirs)
        y = head_rmsnorm(o, rw_ln) + bonus.reshape(*o.shape[:2], RW_W)
        return y * (jax.nn.sigmoid(p[5]) @ rw_g2)

    mix_l = jnp.concatenate([att_l.reshape(Bsz, S, -1), rw_out(o_l, r_l, (rl_f, rl_b))],
                            axis=-1).astype(u_l.dtype) @ w_out
    mix_c = None
    if with_ctx_out:
        att_c = attend_blocked(mla_q(m_c, False), k_c, v_c)
        mix_c = jnp.concatenate([att_c.reshape(Bsz, u_c.shape[1], -1), rw_out(o_c, r_c, (rc_f, rc_b))],
                                axis=-1).astype(u_c.dtype) @ w_out
    return mix_c, mix_l

def swiglu(x, wg, wu, wd):
    return (jax.nn.silu(x @ wg) * (x @ wu)) @ wd

def moe(v, router_w, router_bias, w_gate, w_up, w_down, s_gate, s_up, s_down):
    B, T, D = v.shape
    xt = v.reshape(B * T, D)
    aff = jax.nn.sigmoid((xt @ router_w).astype(F32))
    sel = (aff + router_bias).reshape(-1, N_GROUPS, EXPERTS_PER_GROUP)
    g_idx = jnp.argmax(jnp.sum(lax.top_k(sel, TOP_K)[0], axis=-1), axis=-1)
    in_group = jnp.take_along_axis(sel, g_idx[:, None, None], axis=1)[:, 0]
    _, local = lax.top_k(in_group, TOP_K)
    e_idx = g_idx[:, None] * EXPERTS_PER_GROUP + local
    w = jnp.take_along_axis(aff, e_idx, axis=-1)
    w = w / jnp.sum(w, axis=-1, keepdims=True)
    gates = jnp.einsum('nk,nke->ne', w, jax.nn.one_hot(e_idx, N_EXPERTS, dtype=F32)).astype(xt.dtype)
    out = swiglu(xt, s_gate, s_up, s_down)
    for e in range(N_EXPERTS):
        out = out + gates[:, e:e + 1] * swiglu(xt, w_gate[e], w_up[e], w_down[e])
    return out.reshape(B, T, D)

def setup_inputs(seed: int = 0) -> dict:
    key = jax.random.key(seed)
    keys = jax.random.split(key, 64)
    counter = [0]

    def nxt():
        k = keys[counter[0]]
        counter[0] += 1
        return k

    def nrm(shape, scale=1.0):
        return jax.random.normal(nxt(), shape, F32) * scale

    def unif(shape, lo, hi):
        return jax.random.uniform(nxt(), shape, F32, lo, hi)

    D = D_MODEL
    NE, NO = (DEPTH + 1) // 2, DEPTH // 2
    dt0 = jnp.exp(unif((NE, 2, SSD_HEADS), math.log(1e-3), math.log(1e-1)))
    return {
        "x": nrm((BATCH, SEQ, D)),
        "c": nrm((BATCH, D)),
        "ctx": nrm((BATCH, CTX_LEN, D)),
        "c_ctx": nrm((D,)),
        "w_mod": nrm((DEPTH, D, 6 * D), 0.5 * D ** -0.5),
        "b_mod": nrm((DEPTH, 6 * D), 0.02),
        "norm_g": 1.0 + nrm((DEPTH, 4, D), 0.05),
        "ab_w_in": nrm((NE, D, AB_IN), D ** -0.5),
        "ab_w_out": nrm((NE, AB_OUT, D), AB_OUT ** -0.5),
        "ml_i_bias": nrm((NE, 2, ML_HEADS), 0.1) - 1.0,
        "ml_f_bias": unif((NE, 2, ML_HEADS), 3.0, 6.0),
        "ml_norm": 1.0 + nrm((NE, ML_W), 0.05),
        "ssd_conv_w": nrm((NE, SSD_CONV, SSD_XBC), SSD_CONV ** -0.5),
        "ssd_conv_b": nrm((NE, SSD_XBC), 0.02),
        "ssd_dt_bias": dt0 + jnp.log(-jnp.expm1(-dt0)),
        "ssd_a_log": jnp.log(unif((NE, 2, SSD_HEADS), 1.0, 16.0)),
        "ssd_d": 1.0 + nrm((NE, SSD_HEADS), 0.1),
        "ssd_norm": 1.0 + nrm((NE, SSD_W), 0.05),
        "cd_w_in": nrm((NO, D, CD_IN), D ** -0.5),
        "cd_w_out": nrm((NO, CD_OUT, D), CD_OUT ** -0.5),
        "mla_qn": 1.0 + nrm((NO, MLA_Q_RANK), 0.05),
        "mla_w_uq": nrm((NO, MLA_Q_RANK, MLA_HEADS * (MLA_NOPE + MLA_ROPE)), MLA_Q_RANK ** -0.5),
        "mla_kvn": 1.0 + nrm((NO, MLA_KV_RANK), 0.05),
        "mla_w_ukv": nrm((NO, MLA_KV_RANK, MLA_HEADS * (MLA_NOPE + MLA_V)), MLA_KV_RANK ** -0.5),
        "rw_mu": unif((NO, RW_IN), 0.0, 1.0),
        "rw_w0": unif((NO, 2, RW_W), -6.0, -1.0),
        "rw_w2": nrm((NO, 2, RW_DECAY_RANK, RW_W), 0.1),
        "rw_a0": nrm((NO, 2, RW_W), 0.1),
        "rw_a2": nrm((NO, 2, RW_A_RANK, RW_W), 0.1),
        "rw_g2": nrm((NO, RW_GATE_RANK, RW_W), RW_GATE_RANK ** -0.5),
        "rw_kk": 0.85 + nrm((NO, RW_W), 0.05),
        "rw_ka": 1.0 + nrm((NO, RW_W), 0.05),
        "rw_rk": nrm((NO, RW_HEADS, RW_N), 0.1),
        "rw_ln": 1.0 + nrm((NO, RW_W), 0.05),
        "router_w": nrm((D, N_EXPERTS), D ** -0.5),
        "router_bias": nrm((N_EXPERTS,), 0.01),
        "exp_w_gate": nrm((DEPTH, N_EXPERTS, D, EXPERT_FF), D ** -0.5),
        "exp_w_up": nrm((DEPTH, N_EXPERTS, D, EXPERT_FF), D ** -0.5),
        "exp_w_down": nrm((DEPTH, N_EXPERTS, EXPERT_FF, D), EXPERT_FF ** -0.5),
        "sh_w_gate": nrm((DEPTH, D, EXPERT_FF), D ** -0.5),
        "sh_w_up": nrm((DEPTH, D, EXPERT_FF), D ** -0.5),
        "sh_w_down": nrm((DEPTH, EXPERT_FF, D), EXPERT_FF ** -0.5),
    }

def reference(x, c, ctx, c_ctx, w_mod, b_mod, norm_g, ab_w_in, ab_w_out, ml_i_bias, ml_f_bias, ml_norm,
              ssd_conv_w, ssd_conv_b, ssd_dt_bias, ssd_a_log, ssd_d, ssd_norm, cd_w_in, cd_w_out, mla_qn,
              mla_w_uq, mla_kvn, mla_w_ukv, rw_mu, rw_w0, rw_w2, rw_a0, rw_a2, rw_g2, rw_kk, rw_ka, rw_rk,
              rw_ln, router_w, router_bias, exp_w_gate, exp_w_up, exp_w_down, sh_w_gate, sh_w_up, sh_w_down):
    n_rows = x.shape[1] // GRID_W
    ang = axial_angles(n_rows)
    s_lat = jax.nn.silu(c)[:, None, :]
    s_ctx = jax.nn.silu(c_ctx)
    h_l, h_c = x, ctx
    for l in range(DEPTH):
        last = l == DEPTH - 1
        sh_a, sc_a, g_a, sh_f, sc_f, g_f = jnp.split(s_lat @ w_mod[l] + b_mod[l], 6, axis=-1)
        csh_a, csc_a, cg_a, csh_f, csc_f, cg_f = jnp.split(s_ctx @ w_mod[l] + b_mod[l], 6, axis=-1)
        u_l = rmsnorm(h_l, norm_g[l, 0]) * (1 + sc_a) + sh_a
        u_c = rmsnorm(h_c, norm_g[l, 0]) * (1 + csc_a) + csh_a
        i = l // 2
        if l % 2 == 0:
            y_c, y_l = mixer_ab(u_c, u_l, ab_w_in[i], ab_w_out[i], ml_i_bias[i], ml_f_bias[i], ml_norm[i],
                                ssd_conv_w[i], ssd_conv_b[i], ssd_dt_bias[i], ssd_a_log[i], ssd_d[i],
                                ssd_norm[i], not last)
        else:
            y_c, y_l = mixer_cd(u_c, u_l, ang, cd_w_in[i], cd_w_out[i], mla_qn[i], mla_w_uq[i], mla_kvn[i],
                                mla_w_ukv[i], rw_mu[i], rw_w0[i], rw_w2[i], rw_a0[i], rw_a2[i], rw_g2[i],
                                rw_kk[i], rw_ka[i], rw_rk[i], rw_ln[i], not last)
        h_l = h_l + g_a * rmsnorm(y_l, norm_g[l, 1])
        v_l = rmsnorm(h_l, norm_g[l, 2]) * (1 + sc_f) + sh_f
        moe_w = (router_w, router_bias, exp_w_gate[l], exp_w_up[l], exp_w_down[l], sh_w_gate[l], sh_w_up[l], sh_w_down[l])
        if last:
            f_l = moe(v_l, *moe_w)
        else:
            h_c = h_c + cg_a * rmsnorm(y_c, norm_g[l, 1])
            v_c = rmsnorm(h_c, norm_g[l, 2]) * (1 + csc_f) + csh_f
            f = moe(jnp.concatenate([v_c, v_l], axis=1), *moe_w)
            f_c, f_l = f[:, :v_c.shape[1]], f[:, v_c.shape[1]:]
            h_c = h_c + cg_f * rmsnorm(f_c, norm_g[l, 3])
        h_l = h_l + g_f * rmsnorm(f_l, norm_g[l, 3])
    return h_l


_drawn_inputs = setup_inputs


def setup_inputs(seed=0):
    import zlib

    import numpy as np

    out = dict(_drawn_inputs(seed))
    spreads = {}
    factors = {'ml_i_bias': 8.0,
     'mla_qn': 8.0,
     'mla_kvn': 8.0,
     'rw_a0': 12.695,
     'rw_ln': 18.976,
     'rw_w2': 4.694,
     'rw_kk': 3.695,
     'rw_rk': 3.551}
    for name, (base, spread) in spreads.items():
        noise = np.random.default_rng([zlib.crc32(name.encode()), seed]).standard_normal(out[name].shape)
        drawn = base * np.exp(spread * noise) if base else spread * noise
        out[name] = __import__('jax').numpy.asarray(drawn.astype(out[name].dtype))
    for name, factor in factors.items():
        out[name] = (out[name] * factor).astype(out[name].dtype)
    return out
```

```python
from contextlib import ExitStack

import numpy as np

import concourse.bass as bass
from concourse import mybir

F32 = mybir.dt.float32
F32R = mybir.dt.float32r
ALU = mybir.AluOpType
ACT = mybir.ActivationFunctionType
AX = mybir.AxisListType

P = 128
D = 1024
KD = D // P
NC_, NL = 256, 256
T = NC_ + NL
TT = T // P
EPS = 1e-6
MLH, MLQK, MLV = 4, 128, 256
SSH, SSP, SSN = 16, 64, 64
CONV = 5
AH, NOPE, ROPE, AV = 8, 64, 32, 64
HD = NOPE + ROPE
ASCALE = HD ** -0.5
QR, KVR = 384, 256
RH, RN = 16, 64
L = 64
NCH = T // L
NE, FF = 16, 512
LWC = float(np.exp(-0.5))
NSLOT = 3
SLOT = 4096

C_Q, C_K, C_V, C_O, C_IG, C_FG, C_Z, C_X, C_DT = 0, 512, 1024, 2048, 3072, 3080, 3088, 4112, 5392
C_MQ, C_MKV, C_MKR, C_R, C_RK, C_RV, C_LOW = 0, 384, 640, 672, 1696, 2720, 3744

VEC_PARTS = [("norm_g", 64), ("b_mod", 96), ("c", 8), ("c_ctx", 8), ("ml_norm", 8), ("ssd_norm", 8),
             ("ssd_conv_w", 50), ("ssd_conv_b", 10), ("mla_qn", 3), ("mla_kvn", 2), ("rw_mu", 27),
             ("rw_w0", 16), ("rw_a0", 16), ("rw_kk", 8), ("rw_ka", 8), ("rw_rk", 8), ("rw_ln", 8)]
VEC, _n = {}, 0
for _name, _k in VEC_PARTS:
    VEC[_name] = _n
    _n += _k
NVEC = _n
NVT = -(-NVEC // P)

OFF = {0: {0: [(128, 512)], 1: [(256, 512)], 2: [(384, 512)], 3: []},
       1: {1: [(0, 128), (256, 512)], 0: [(256, 512)], 3: [(256, 384)], 2: []}}
SPAN = {0: [(0, [(0, 512)]), (1, [(128, 512)]), (2, [(256, 512)]), (3, [(384, 512)])],
        1: [(1, [(0, 512)]), (0, [(0, 128), (256, 512)]), (3, [(256, 512)]), (2, [(256, 384)])]}


def constants():
    i = np.arange(P)
    neg = np.float32(-1e30)
    c = {"ident": np.eye(P, dtype=np.float32)}
    c["blockones"] = (i[:, None] // 64 == i[None, :] // 64).astype(np.float32)
    fwd = np.where(i[:, None] <= i[None, :], np.float32(0), neg)
    bwd = np.where(i[:, None] >= i[None, :], np.float32(0), neg)
    c["maskneg"] = np.stack([np.tile(fwd, (1, 4)), np.tile(bwd, (1, 4))], 1).astype(np.float32)
    s, t = (i % 64)[:, None], np.arange(64)[None, :]
    same = (s // 16) == (t // 16)
    m = []
    for st, inc in (((s < t), (s <= t)), ((s > t), (s >= t))):
        tr = (s > t) if st[0, 1] else (s < t)
        m.append(np.stack([st, inc, st & same, st & ~same, tr & same, tr & ~same], 1))
    c["rmask"] = np.stack(m, 1).astype(np.float32)
    c["stackid"] = (s == t).astype(np.float32)
    one = np.ones((P, 2, 8, L), np.float32)
    one[:, 0, :, 0] = 0
    one[:, 1, :, L - 1] = 0
    c["restart"] = one.reshape(P, 2, 8 * L)
    rows = NL // 64
    ang_row = np.repeat(np.arange(rows, dtype=np.float32), 64)
    ang_col = np.tile(np.arange(64, dtype=np.float32), rows)
    inv = (10000.0 ** (-np.arange(8, dtype=np.float32) / 8)).astype(np.float32)
    ang = np.concatenate([ang_row[:, None] * inv, ang_col[:, None] * inv], -1).astype(np.float32).T
    cs, sn = np.cos(ang), np.sin(ang)
    c["rope"] = np.stack([np.concatenate([cs, cs]), np.concatenate([-sn, sn])], 1).astype(np.float32)
    return {k: np.ascontiguousarray(v) for k, v in c.items()}


class Steps:

    def __init__(self, known):
        self.known, self.new, self.block, self.loop = known, {}, 0, None

    def name(self, label):
        return label if label[0] == "let go" else (self.block, label)


class Turn:

    def __init__(self, first, per):
        self.first, self.per = first, per


class Engine:

    def __init__(self, name, sem, steps):
        self.name, self.sem, self.steps = name, sem, steps
        self.n, self.waited, self.loop, self.waited_in_loop = 0, {}, None, {}

    def tick(self, *labels):
        self.n += 1
        for label in map(self.steps.name, labels):
            self.steps.new[label] = [self.name, self.n, 0, 0]
            if self.loop is not None:
                self.loop[2].append(label)
        return 1

    @property
    def now(self):
        return self.n if self.loop is None else self.loop[0] * self.per + self.n

    def step(self, ins, *labels):
        ins.then_inc(self.sem, self.tick(*labels))
        self.e.wait_ge(self.sem, self.now)
        return ins

    def wait_ge(self, sem, value):
        if sem is None:
            return
        if isinstance(value, Turn):
            if self.waited_in_loop.get(id(sem), -1) < value.first:
                self.waited_in_loop[id(sem)] = value.first
                self.e.wait_ge(sem, self.loop[0] * value.per + value.first)
        elif not isinstance(value, int) or self.waited.get(id(sem), 0) < value:
            if self.loop is None and isinstance(value, int):
                self.waited[id(sem)] = value
            self.e.wait_ge(sem, value)

    def settle(self):
        self.e.sem_inc(self.settled, 1)

    def start_loop(self, i, key, rounds):
        self.loop = (i, key, [])
        self.steps.loop = key
        self.waited_in_loop = {}
        self.loop_n, self.rounds = self.n, rounds
        self.per = self.steps.known.get(("per", self.name, key), 1)

    def end_loop(self):
        i, key, labels = self.loop
        per = self.n - self.loop_n
        self.steps.new[("per", self.name, key)] = per
        for label in labels:
            self.steps.new[label][2:] = [per, (self.rounds, key)]
        self.n += per * (self.rounds - 1)
        self.loop = self.steps.loop = None


def program(nc, A, out, known, upto=99, taps=None):
    steps = Steps(known)
    with ExitStack() as ctx:
        def sb(name, shape):
            return ctx.enter_context(nc.sbuf_tensor(name, shape, F32))

        def semaphore(name):
            return ctx.enter_context(nc.semaphore(name))

        pe_done, act_done = semaphore("tensor_steps_done"), semaphore("scalar_steps_done")
        dve_done, pool_done = semaphore("vector_steps_done"), semaphore("gpsimd_steps_done")
        done = {"pe": pe_done, "act": act_done, "dve": dve_done, "pool": pool_done}
        pe, act, dve, pool = (Engine(n, s, steps) for n, s in done.items())
        sp = Engine("sp", None, steps)
        pe.settled = dve.settled = semaphore("waits_settled")

        def at(label, back=0):
            got = steps.known.get(steps.name(label))
            if got is None or (back and steps.loop is None):
                return None, 0
            name, value, per, rounds = got
            if per and steps.loop == rounds[1]:
                assert value >= back * per
                return done[name], Turn(value - back * per, per)
            return done[name], value + (per * (rounds[0] - 1) if per else 0)

        def latest(engine, now, before=()):
            found = [at((x, d)) for x, d in now] + [at((x, d), back=1) for x, d in before]
            found = [v for s, v in found if s is done[engine]]
            return (done[engine], max(found, key=lambda v: v.first if isinstance(v, Turn) else v)) if found else (None, 0)

        weights_landed = [semaphore(f"weights_landed_{i}") for i in range(NSLOT)]
        loads_landed = semaphore("loads_landed")
        output_written = semaphore("output_written")
        loads = [0]

        def load(eng, dst, src):
            eng.dma_start(dst, src).then_inc(loads_landed, 16)
            loads[0] += 16

        def loads_done(e):
            e.e.wait_ge(loads_landed, loads[0])

        ident, ones, blockones = sb("ident", [P, P]), sb("ones", [P, P]), sb("blockones", [P, P])
        stackid = sb("stackid", [P, 64])
        vec = sb("vec", [P, NVT * P])
        mod = sb("mod", [P, 48, 2])
        moda = sb("moda", [P, 4, 8, 2])
        silc = sb("silc", [P, 8, 2])
        epsc, zeros = sb("epsc", [P, 1]), sb("zeros", [P, 1])
        h = sb("h", [P, KD, T])
        ring = sb("ring", [P, NSLOT, SLOT])
        with nc.sbuf_tensor("arena", [P, 35000], F32) as arena:
            pass
        ctx.enter_context(nc.sbuf_tensor("arena_for_experts", [P, 35000 - 20480], F32))
        parts = ctx.enter_context(nc.sbuf_tensor("parts", [P, 20480], F32R))
        ps = [ctx.enter_context(nc.psum_tensor(f"bank{i}", [P, 512], F32))[:, :] for i in range(8)]

        def region(at, *shape, rows=P):
            n = int(np.prod(shape))
            assert at + n <= 35000
            return shaped(arena[0:rows, at:at + n], shape)

        def parts_region(at, *shape):
            return shaped(parts[:, at:at + int(np.prod(shape))], shape)

        def shaped(flat, shape):
            if len(shape) == 1:
                return flat
            names = "abcd"[:len(shape)]
            return flat.rearrange(f"p ({' '.join(names)}) -> p {' '.join(names)}",
                                  **{x: y for x, y in zip(names, shape)})

        pieces, piece_at = [], {}

        def piece(key, w, r0, kt, c0, n):
            piece_at[key] = len(pieces)
            pieces.append((w[r0:r0 + kt * P, c0:c0 + n].rearrange("(k p) n -> p k n", p=P), kt, n))

        w_in = A["ab_w_in"][0]
        for m in range(12):
            piece(("mod", 0, m), A["w_mod"][0], 0, 8, m * 512, 512)
        piece("q", w_in, 0, 8, C_Q, 512)
        piece("k", w_in, 0, 8, C_K, 512)
        for j in range(2):
            piece(("v", j), w_in, 0, 8, C_V + j * 512, 512)
        piece("gates", w_in, 0, 8, C_IG, 16)
        for j in range(2):
            piece(("x", j), w_in, 0, 8, C_X + j * 512, 512)
        piece(("x", 2), w_in, 0, 8, C_X + 1024, 288)
        for j in range(2):
            piece(("o", j), w_in, 0, 8, C_O + j * 512, 512)
        for j in range(2):
            piece(("z", j), w_in, 0, 8, C_Z + j * 512, 512)
        for j in range(4):
            piece(("out", 0, j), A["ab_w_out"][0], 0, 16, j * 256, 256)

        def shared(l):
            piece(("sh", l, 0), A["sh_w_gate"][l], 0, 8, 0, 512)
            piece(("sh", l, 1), A["sh_w_up"][l], 0, 8, 0, 512)
            piece(("sh", l, 2), A["sh_w_down"][l], 0, 4, 0, 1024)
            piece_at[("experts", l)] = len(pieces)
            pieces.extend([None] * (3 * NE))

        shared(0)
        for m in range(12):
            piece(("mod", 1, m), A["w_mod"][1], 0, 8, m * 512, 512)
        w_in1 = A["cd_w_in"][0]
        piece("mq", w_in1, 0, 8, C_MQ, 384)
        piece("mkv", w_in1, 0, 8, C_MKV, 288)
        for n_, c_ in (("r", C_R), ("rk", C_RK), ("rv", C_RV)):
            for j in range(2):
                piece((n_, j), w_in1, 0, 8, c_ + j * 512, 512)
        piece("low", w_in1, 0, 8, C_LOW, 384)
        for j in range(4):
            piece(("out", 1, j), A["cd_w_out"][0], 0, 12, j * 256, 256)
        shared(1)

        def slot_view(i, kt, n):
            return ring[:, i % NSLOT, 0:kt * n].rearrange("p (k n) -> p k n", k=kt)

        def weights(key):
            i = piece_at[key]
            _, kt, n = pieces[i]
            pe.wait_ge(weights_landed[i % NSLOT], 16 * (i // NSLOT + 1))
            return slot_view(i, kt, n)

        issued = [0]

        def stream_weights(last):
            while issued[0] <= min(last + NSLOT, len(pieces) - 1) and pieces[issued[0]] is not None:
                i = issued[0]
                if i >= NSLOT:
                    sp.wait_ge(*at(("let go", i - NSLOT)))
                src, kt, n = pieces[i]
                nc.sync.dma_start(slot_view(i, kt, n), src).then_inc(weights_landed[i % NSLOT], 16)
                issued[0] += 1

        def let_go(key):
            return ("let go", piece_at[key])

        blocks = [0]

        class Stop(Exception):
            pass

        def block(pe_=None, act_=None, dve_=None, pool_=None, sp_=None, last=None):
            blocks[0] += 1
            steps.block = blocks[0]
            with nc.Block(no_gpsimd_drain=True) as b:
                if pe_:
                    @b.tensor
                    def _(e):
                        pe.e = e
                        pe_()
                if act_:
                    @b.scalar
                    def _(e):
                        act.e = e
                        act_()
                if dve_:
                    @b.vector
                    def _(e):
                        dve.e = e
                        dve_()
                if pool_:
                    @b.gpsimd
                    def _(e):
                        pool.e = e
                        pool_()
                        e.wait_ge(pool.sem, pool.n)

                @b.sync
                def _(e):
                    sp.e = e
                    if sp_:
                        sp_()
                    if last is not None:
                        stream_weights(piece_at[last])
                    if loads[0]:
                        e.wait_ge(loads_landed, loads[0])
            if taps and blocks[0] in taps:
                for name, ap in taps[blocks[0]](region, h).items():
                    o = nc.dram_tensor(name, ap.shape, F32, kind="ExternalOutput").ap()
                    with nc.Block(no_gpsimd_drain=True) as b:
                        @b.sync
                        def _(e, o=o, ap=ap):
                            e.dma_start(o, ap).then_inc(loads_landed, 16)
                            loads[0] += 16
                            e.wait_ge(loads_landed, loads[0])
            if blocks[0] >= upto:
                raise Stop

        def bank(tag, j):
            if j >= 8:
                pe.wait_ge(*at((tag, "read", j - 8)))
            return ps[j % 8]

        def whole(x):
            return x.bitcast(F32)

        def three(wh, wl, xh, xl):
            return [(wh, xh), (wh, xl), (wl, xh)]

        def mms(o, pairs):
            for n, (a, b) in enumerate(pairs):
                m = nc.tensor.matmul(o, a, b, start=n == 0, stop=n == len(pairs) - 1)
            return m

        def col(name, i):
            return vec[:, VEC[name] + i:VEC[name] + i + 1]


        def vmul(o, a, b):
            return nc.vector.tensor_tensor(o, a, b, ALU.mult)

        def vadd(o, a, b):
            return nc.vector.tensor_tensor(o, a, b, ALU.add)

        def vsub(o, a, b):
            return nc.vector.tensor_tensor(o, a, b, ALU.subtract)

        def halves(x):
            return x.rearrange("p n (s t) -> p n s t", s=2)

        def load_all():
            xin = region(0, TT, D)
            rows = region(4096, NVT, P)

            def sp_():
                for n_, t_ in (("ident", ident), ("blockones", blockones), ("stackid", stackid)):
                    load(nc.sync, t_[:], A[n_])
                for tt in range(2):
                    load(nc.sync, xin[:, tt, :], A["ctx"][0, tt * P:(tt + 1) * P, :])
                    load(nc.sync, xin[:, 2 + tt, :], A["x"][0, tt * P:(tt + 1) * P, :])
                flat = {"norm_g": "l a (r p) -> (l a r) p", "b_mod": "l (r p) -> (l r) p", "c": "l (r p) -> (l r) p",
                        "c_ctx": "(r p) -> r p", "ssd_conv_w": "l a (r p) -> (l a r) p", "rw_w0": "l a (r p) -> (l a r) p",
                        "rw_a0": "l a (r p) -> (l a r) p", "rw_rk": "l (r q) n -> (l r) (q n)"}
                for n_, k_ in VEC_PARTS:
                    pat = flat.get(n_, "l (r p) -> (l r) p")
                    kw = {"q": 2} if n_ == "rw_rk" else {"p": P}
                    src = A[n_].rearrange(pat, **kw)
                    a0 = VEC[n_]
                    at = 0
                    while at < k_:
                        r = (a0 + at) % P
                        m = min(k_ - at, P - r)
                        load(nc.sync, rows[r:r + m, (a0 + at) // P, :], src[at:at + m, :])
                        at += m

            def pool_():
                nc.gpsimd.memset(ones[:], 1.0).then_inc(pool_done, pool.tick("ones"))
                nc.gpsimd.memset(epsc[:], EPS).then_inc(pool_done, pool.tick("epsc"))

            def pe_():
                pe.wait_ge(loads_landed, loads[0])
                j = 0
                for t in range(NVT):
                    n = min(P, NVEC - t * P)
                    o = bank("load", j)
                    nc.tensor.transpose(o[:, 0:n], rows[0:n, t, :], ident[0:n, 0:n]).then_inc(pe_done, pe.tick(("vecT", t)))
                    j += 1
                for k in range(KD):
                    o = bank("load", j)
                    for tt in range(TT):
                        m = nc.tensor.transpose(o[:, tt * P:(tt + 1) * P], xin[:, tt, k * P:(k + 1) * P], ident[:])
                    m.then_inc(pe_done, pe.tick(("hT", k)))
                    j += 1

            def act_():
                for k in range(0, KD, 2):
                    act.wait_ge(*at(("hT", k)))
                    nc.scalar.activation(h[:, k, :], ps[(NVT + k) % 8][:], ACT.Copy).then_inc(act_done, act.tick(("load", "read", NVT + k)))
                act.wait_ge(*at(("load", "read", NVT - 1)))
                nc.scalar.activation(silc[:, :, 1], vec[:, VEC["c"]:VEC["c"] + 8], ACT.Silu).then_inc(act_done, act.tick())
                nc.scalar.activation(silc[:, :, 0], vec[:, VEC["c_ctx"]:VEC["c_ctx"] + 8], ACT.Silu).then_inc(act_done, act.tick())

            def dve_():
                for t in range(NVT):
                    dve.wait_ge(*at(("vecT", t)))
                    n = min(P, NVEC - t * P)
                    nc.vector.tensor_copy(vec[:, t * P:t * P + n], ps[t][:, 0:n]).then_inc(dve_done, dve.tick(("load", "read", t)))
                for k in range(1, KD, 2):
                    dve.wait_ge(*at(("hT", k)))
                    nc.vector.tensor_copy(h[:, k, :], ps[(NVT + k) % 8][:]).then_inc(dve_done, dve.tick(("load", "read", NVT + k)))

            n_loads = 3 + 4 + sum(1 for _ in load_parts())
            loads[0] = 16 * n_loads

            def sp_first():
                loads[0] = 0
                sp_()
                assert loads[0] == 16 * n_loads

            block(pe_, act_, dve_, pool_, sp_first)

        def load_parts():
            for n_, k_ in VEC_PARTS:
                at = 0
                while at < k_:
                    r = (VEC[n_] + at) % P
                    at += min(k_ - at, P - r)
                    yield n_

        def modulation(l):
            rows = region(30000, 4, 512, rows=2)

            def pe_():
                for m in range(13):
                    if m < 12:
                        w = weights(("mod", l, m))
                        pe.wait_ge(*at(("row", m - 4)))
                        mms(ps[1 + m % 4][0:2, :], [(silc[:, k, :], w[:, k, :]) for k in range(8)]).then_inc(pe_done, pe.tick(("row sums", m), let_go(("mod", l, m))))
                    if m > 0:
                        pe.wait_ge(*at(("row", m - 1)))
                        for f in range(4):
                            c0 = (4 * (m - 1) + f) * 2
                            x = nc.tensor.transpose(ps[0][:, c0:c0 + 2], rows[:, (m - 1) % 4, f * P:(f + 1) * P], ident[0:2, 0:2])
                        x.then_inc(pe_done, pe.tick(("turned", m - 1)))

            def act_():
                for m in range(12):
                    act.wait_ge(*at(("row sums", m)))
                    if m >= 4:
                        act.wait_ge(*at(("turned", m - 4)))
                    nc.scalar.activation(rows[:, m % 4], ps[1 + m % 4][0:2, :], ACT.Copy).then_inc(act_done, act.tick(("row", m)))

            def dve_():
                dve.wait_ge(*at(("turned", 11)))
                b0 = VEC["b_mod"] + 48 * l
                bias = vec[:, b0:b0 + 48].unsqueeze(2).to_broadcast([P, 48, 2])
                dve.step(vadd(mod[:], ps[0][:, 0:96].rearrange("p (m s) -> p m s", s=2), bias))
                g = [vec[:, VEC["norm_g"] + (4 * l + a) * 8:][:, 0:8].unsqueeze(2).to_broadcast([P, 8, 2])
                     for a in range(4)]
                one = nc.vector.scalar_tensor_tensor
                one(moda[:, 0], mod[:, 8:16], 1.0, g[0], ALU.add, ALU.mult).then_inc(dve_done, dve.tick())
                one(moda[:, 2], mod[:, 32:40], 1.0, g[2], ALU.add, ALU.mult).then_inc(dve_done, dve.tick())
                vmul(moda[:, 1], mod[:, 16:24], g[1]).then_inc(dve_done, dve.tick())
                vmul(moda[:, 3], mod[:, 40:48], g[3]).then_inc(dve_done, dve.tick())

            block(pe_, act_, dve_, last=("mod", l, 11))

        def rms_block(tag, src, n, cols, dim, use, sq_at, extra_pe=None):
            sq = region(sq_at, 2, T)
            inv = region(sq_at + 2 * T, T)[:, 0:cols]

            def pe_():
                for k in range(n):
                    pe.wait_ge(*at((tag, "square", k)))
                    nc.tensor.matmul(ps[0][:, 0:cols], ones[:], sq[:, k % 2, 0:cols],
                                             start=k == 0, stop=k == n - 1).then_inc(pe_done, pe.tick((tag, "summed", k)))

            def act_():
                for k in range(n):
                    if k >= 2:
                        act.wait_ge(*at((tag, "summed", k - 2)))
                    nc.scalar.activation(sq[:, k % 2, 0:cols], src(k), ACT.Square).then_inc(act_done, act.tick((tag, "square", k)))
                act.wait_ge(*at((tag, "summed", n - 1)))
                nc.scalar.activation(inv, ps[0][:, 0:cols], ACT.Sqrt, bias=epsc[:], scale=1.0 / dim).then_inc(act_done, act.tick((tag, "root")))
                if use[1]:
                    use[1](inv)

            def dve_():
                dve.wait_ge(*at((tag, "root")))
                dve.step(nc.vector.reciprocal(inv, inv), (tag, "inv"))
                use[0](inv)

            block(pe_, act_, dve_)

        def segments(c0):
            return [(s, slice(s * 256, s * 256 + 256), slice(s * 256 - c0, s * 256 + 256 - c0))
                    for s in range(2) if s * 256 >= c0]

        def modulated(tag, a, shift, dst, sq_at, c0=0):
            def dve_(inv):
                for k in range(KD):
                    for s, c, ci in segments(c0):
                        nc.vector.scalar_tensor_tensor(dst[:, k, c], h[:, k, c], moda[:, a, k, s:s + 1],
                                                                inv[:, ci], ALU.mult, ALU.mult).then_inc(dve_done, dve.tick((tag, "scaled", k, s)))

            def act_(inv):
                for k in range(KD):
                    for s, c, _ in segments(c0):
                        act.wait_ge(*at((tag, "scaled", k, s)))
                        nc.scalar.activation(dst[:, k, c], dst[:, k, c], ACT.Identity,
                                                      bias=mod[:, shift + k, s:s + 1]).then_inc(act_done, act.tick())

            rms_block(tag, lambda k: h[:, k, c0:T], KD, T - c0, D, (dve_, act_), sq_at)

        def residual(tag, a, y, sq_at, c0=0):
            def dve_(inv):
                for k in range(KD):
                    for s, c, ci in segments(c0):
                        dve.step(nc.vector.scalar_tensor_tensor(y[:, k, c], y[:, k, c], moda[:, a, k, s:s + 1],
                                                                inv[:, ci], ALU.mult, ALU.mult))
                        vadd(h[:, k, c], h[:, k, c], y[:, k, c]).then_inc(dve_done, dve.tick())

            rms_block(tag, lambda k: y[:, k, c0:T], KD, T - c0, D, (dve_, None), sq_at)

        a_mask = region(0, 2, 512)
        a_oz = region(1024, 16, T)
        a_q, a_k = region(9216, 4, T), region(11264, 4, T)
        a_v = region(13312, TT, D)
        a_xbc = region(17408, 10, 2, 260)
        a_u = region(22608, KD, T)
        a_e = region(26704, 2, 4, T)
        a_gates = region(30800, 3, T, rows=32)
        a_xs = region(9216, 10, T)
        a_cb = region(14336, 2, 4, T)
        a_rows = region(30800, 7, T, rows=32)
        a_cols = region(34400, 600)
        a_bias = a_cols[0:32, 0:8]

        def project0():
            def pe_():
                j = 0
                for key, dst in (("q", a_q), ("k", a_k)):
                    w = weights(key)
                    for f in range(4):
                        mms(bank("p0", j), [(w[:, k, f * P:(f + 1) * P], a_u[:, k, :]) for k in range(8)]).then_inc(pe_done, pe.tick(("p0", j), *((let_go(key),) if f == 3 else ())))
                        j += 1
                for i in range(2):
                    w = weights(("v", i))
                    for tt in range(TT):
                        mms(bank("p0", j), [(a_u[:, k, tt * P:(tt + 1) * P], w[:, k, :]) for k in range(8)]).then_inc(pe_done, pe.tick(("p0", j), *((let_go(("v", i)),) if tt == 3 else ())))
                        j += 1
                w = weights("gates")
                for i in range(2):
                    mms(bank("p0", j)[0:8, :], [(w[:, k, 8 * i:8 * i + 8], a_u[:, k, :]) for k in range(8)]).then_inc(pe_done, pe.tick(("p0", j), *((let_go("gates"),) if i == 1 else ())))
                    j += 1
                for i in range(3):
                    w = weights(("x", i))
                    for f in range(4 if i < 2 else 2):
                        mms(bank("p0", j), [(w[:, k, f * P:(f + 1) * P], a_u[:, k, :]) for k in range(8)]).then_inc(pe_done, pe.tick(("p0", j), *((let_go(("x", i)),) if f == 3 else ())))
                        j += 1
                mms(bank("p0", j)[0:32, :], [(w[:, k, 256:288], a_u[:, k, :]) for k in range(8)]).then_inc(pe_done, pe.tick(("p0", j), let_go(("x", 2))))
                j += 1
                for kind in "oz":
                    for i in range(2):
                        w = weights((kind, i))
                        for f in range(4):
                            mms(bank("p0", j), [(w[:, k, f * P:(f + 1) * P], a_u[:, k, :]) for k in range(8)]).then_inc(pe_done, pe.tick(("p0", j), *((let_go((kind, i)),) if f == 3 else ())))
                            j += 1

            def dve_():
                for j in range(8):
                    dve.wait_ge(*at(("p0", j)))
                    if j < 4:
                        i = nc.vector.tensor_scalar(a_q[:, j, :], ps[j][:], MLQK ** -0.5, None, ALU.mult)
                    else:
                        i = nc.vector.tensor_copy(a_k[:, j - 4, :], ps[j][:])
                    i.then_inc(dve_done, dve.tick(("p0", "read", j)))
                for j in range(8, 16, 2):
                    dve.wait_ge(*at(("p0", j)))
                    i, tt = divmod(j - 8, 4)
                    nc.vector.tensor_copy(a_v[:, tt, i * 512:(i + 1) * 512], ps[j % 8][:]).then_inc(dve_done, dve.tick(("p0", "read", j)))
                for j in range(16, 18):
                    dve.wait_ge(*at(("p0", j)))
                    nc.vector.tensor_copy(a_gates[0:8, j - 16, :], ps[j % 8][0:8, :]).then_inc(dve_done, dve.tick(("p0", "read", j)))
                for j in range(18, 28):
                    dve.wait_ge(*at(("p0", j)))
                    nc.vector.tensor_copy(a_xbc[:, j - 18, :, 2:258], ps[j % 8].rearrange("p (s t) -> p s t", s=2)).then_inc(dve_done, dve.tick(("p0", "read", j)))
                dve.wait_ge(*at(("p0", 28)))
                nc.vector.tensor_copy(a_gates[:, 2, :], ps[28 % 8][0:32, :]).then_inc(dve_done, dve.tick(("p0", "read", 28)))

            def act_():
                for j in range(9, 16, 2):
                    act.wait_ge(*at(("p0", j)))
                    i, tt = divmod(j - 8, 4)
                    nc.scalar.activation(a_v[:, tt, i * 512:(i + 1) * 512], ps[j % 8][:], ACT.Copy).then_inc(act_done, act.tick(("p0", "read", j)))
                for j in range(29, 45):
                    act.wait_ge(*at(("p0", j)))
                    nc.scalar.activation(a_oz[:, j - 29, :], ps[j % 8][:],
                                                  ACT.Sigmoid if j < 37 else ACT.Silu).then_inc(act_done, act.tick(("p0", "read", j)))

            def pool_():
                nc.gpsimd.memset(a_xbc[:, :, :, 0:2], 0.0).then_inc(pool_done, pool.tick())
                nc.gpsimd.memset(a_xbc[:, :, :, 258:260], 0.0).then_inc(pool_done, pool.tick())

            def sp_():
                load(nc.sync, a_mask, A["maskneg"])
                for i, (n_, m) in enumerate((("ml_i_bias", 8), ("ml_f_bias", 8), ("ssd_dt_bias", 32), ("ssd_a_log", 32))):
                    load(nc.sync, a_bias[0:m, i:i + 1], A[n_].rearrange("l a (h o) -> (l a h) o", o=1))
                with nc.allow_non_contiguous_dma(reason="a few words"):
                    for hf in range(2):
                        load(nc.sync, a_cols[64 * hf:64 * hf + 64, 16:24],
                             A["ssd_d"][0:1, hf::2].to_broadcast([64, 8]))

            block(pe_, act_, dve_, pool_, sp_, last=("z", 1))

        def soft(x, tmp, out, sign, tag):
            v = nc.vector
            dve.step(v.scalar_tensor_tensor(tmp[0], x, -1.0, x, ALU.mult, ALU.max), (tag, "abs"))
            dve.wait_ge(*at((tag, "exp")))
            dve.step(v.tensor_scalar(tmp[2], tmp[1], 1.0, None, ALU.add), (tag, "1+e"))
            dve.step(v.tensor_scalar(tmp[0], tmp[2], -1.0, 1e-30, ALU.add, ALU.max))
            dve.step(v.reciprocal(tmp[3], tmp[0]))
            dve.step(vmul(tmp[3], tmp[3], tmp[1]))
            dve.wait_ge(*at((tag, "ln")))
            dve.step(vmul(tmp[3], tmp[3], tmp[5]))
            dve.step(v.scalar_tensor_tensor(tmp[0], tmp[0], 1e-30, tmp[1], ALU.is_equal, ALU.mult))
            dve.step(vadd(tmp[3], tmp[3], tmp[0]))
            dve.step(v.tensor_scalar(tmp[0], x, 0.0, None, ALU.max if sign > 0 else ALU.min))
            dve.step(nc.vector.tensor_tensor(out, tmp[0], tmp[3], ALU.add if sign > 0 else ALU.subtract))

        def soft_act(tmp, tag):
            act.wait_ge(*at((tag, "abs")))
            nc.scalar.activation(tmp[1], tmp[0], ACT.Exp, scale=-1.0).then_inc(act_done, act.tick((tag, "exp")))
            act.wait_ge(*at((tag, "1+e")))
            nc.scalar.activation(tmp[5], tmp[2], ACT.Ln).then_inc(act_done, act.tick((tag, "ln")))

        def scans(src, dst_f, dst_b, op, first):
            n = src[0].shape[0]
            unit = (ones if op == ALU.add else zeros)[0:n, 0:1]
            how = (ALU.mult, ALU.add) if op == ALU.add else (ALU.add, ALU.max)
            dve.step(nc.vector.tensor_tensor_scan(dst_f, unit.to_broadcast([n, T]), src[0], first, *how))
            dve.step(nc.vector.tensor_tensor_scan(dst_b[:, 0:NC_][:, ::-1], unit.to_broadcast([n, NC_]),
                                                  src[1][:, 0:NC_][:, ::-1], first, *how))
            dve.step(nc.vector.tensor_tensor_scan(dst_b[:, NC_:T][:, ::-1], unit.to_broadcast([n, NL]),
                                                  src[1][:, NC_:T][:, ::-1], dst_b[:, 0:1], *how))

        a_negm = a_rows[0:8, 3:5]
        a_em = a_rows[0:8, 5:7]
        a_brow = a_rows[:, 3:5]
        c_g = a_cols[:, 64:128].rearrange("p (d t r) -> p d t r", d=2, t=TT)
        c_b = a_cols[:, 128:384].rearrange("p (d t r) -> p d t r", d=2, t=TT)
        c_dt = a_cols[:, 384:512].rearrange("p (t r) -> p t r", t=TT)

        def mlstm_rows():
            tmp = [a_e.rearrange("p a b c -> p (a b) c")[0:8, i, :] for i in range(8)]
            x, lf, bf, bb, gf, gb = a_gates[0:8, 0, :], tmp[4], tmp[5], tmp[6], tmp[7], a_gates[0:8, 1, :]

            def dve_():
                dve.step(nc.vector.memset(zeros[:], 0.0))
                dve.step(nc.vector.tensor_scalar(x, x, a_bias[0:8, 0:1], None, ALU.add))
                f = a_gates[0:8, 1, :]
                dve.step(nc.vector.tensor_scalar(f, f, a_bias[0:8, 1:2], None, ALU.add))
                soft(f, tmp, lf, -1, "lf")
                scans((lf, lf), bf, bb, ALU.add, 0.0)
                dve.step(vsub(gf, x, bf))
                dve.step(vsub(gb, x, bb), "g rows")
                mf, mb = a_negm[:, 0], a_negm[:, 1]
                scans((gf, gb), mf, mb, ALU.max, 0.0)
                for b, m, e in ((bf, mf, 0), (bb, mb, 1)):
                    dve.step(vadd(tmp[0], b, m))
                    dve.step(nc.vector.tensor_scalar(a_em[:, e], tmp[0], -87.0, None, ALU.max), ("m", e))
                nc.vector.tensor_scalar(a_negm, a_negm, -1.0, None, ALU.mult).then_inc(dve_done, dve.tick())
                dve.wait_ge(*at("g columns"))
                nc.vector.tensor_copy(a_cols[:, 64:128], ps[0][:, 0:64]).then_inc(dve_done, dve.tick())

            def act_():
                soft_act(tmp, "lf")
                for e in range(2):
                    act.wait_ge(*at(("m", e)))
                    nc.scalar.activation(a_em[:, e], a_em[:, e], ACT.Exp, scale=-1.0).then_inc(act_done, act.tick())

            def pe_():
                pe.wait_ge(*at("g rows"))
                for d, g in enumerate((gf, gb)):
                    for tt in range(TT):
                        m = nc.tensor.transpose(ps[0][:, (d * TT + tt) * 8:(d * TT + tt) * 8 + 8],
                                                g[:, tt * P:(tt + 1) * P], ident[0:8, 0:8])
                m.then_inc(pe_done, pe.tick("g columns"))

            block(pe_, act_, dve_)

        def exponent_tiles(it, d, n_rows, row, rows_d, off_bank, diag_bank):
            sel = ident[0:n_rows, row:row + 1].to_broadcast([n_rows, P])
            nc.tensor.matmul(off_bank, sel, rows_d, start=True, stop=True)
            nc.tensor.matmul(diag_bank, sel, rows_d, start=True, stop=False)
            nc.tensor.matmul(diag_bank, ident[:], a_mask[:, d], start=False, stop=True).then_inc(pe_done, pe.tick(("expo", it)))

        def exponentials(it, d, e, off_bank, diag_bank, bias):
            act.wait_ge(*at(("expo", it)))
            for s, _ in SPAN[d]:
                c = slice(s * P, s * P + P)
                m = nc.scalar.activation(e[:, s, c], diag_bank[:, c], ACT.Exp, bias=bias(s))
                for c0, c1 in OFF[d][s]:
                    m.then_inc(act_done, act.tick())
                    m = nc.scalar.activation(e[:, s, c0:c1], off_bank[:, c0:c1], ACT.Exp, bias=bias(s))
                m.then_inc(act_done, act.tick(("E", it, s)))

        def mlstm():
            qk = [ps[0], ps[1], ps[2], ps[2]]
            inv, tmp = region(30800, T), region(31312, T)

            def qk_cols(s, c0, c1):
                return qk[s][:, c0:c1] if s < 2 else qk[s][:, c0 - 256 + 256 * (s - 2):c1 - 256 + 256 * (s - 2)]

            def prepare(it):
                hd, d = divmod(it, 2)
                if d == 0:
                    for s in range(TT):
                        pe.wait_ge(*at(("sD", it - 1, s)))
                    for s in range(TT):
                        c0 = 0 if s < 2 else 256
                        m = nc.tensor.matmul(qk_cols(s, c0, T), a_k[:, hd, s * P:(s + 1) * P], a_q[:, hd, c0:T],
                                             start=True, stop=True)
                    m.then_inc(pe_done, pe.tick(("qk", hd)))
                pe.wait_ge(*at(("h", it - 1)))
                for s in range(TT):
                    pe.wait_ge(*at(("E", it - 1, s)))
                exponent_tiles(it, d, 8, d * MLH + hd, a_negm[:, d], ps[3], ps[4])

            def pe_():
                for it in range(2 * MLH):
                    hd, d = divmod(it, 2)
                    prepare(it)
                    for n, (s, spans) in enumerate(SPAN[d]):
                        pe.wait_ge(*at(("sD", it, s)))
                        for half in range(3):
                            w = ones[:] if half == 2 else a_v[:, s, hd * MLV + half * P:hd * MLV + half * P + P]
                            for i, (c0, c1) in enumerate(spans):
                                m = nc.tensor.matmul(ps[5 + half][:, c0:c1], w, a_e[:, it % 2, s, c0:c1], start=n == 0,
                                                     stop=n == TT - 1 and i == len(spans) - 1)
                    m.then_inc(pe_done, pe.tick(("num", it)))
                    for s in range(TT):
                        pe.wait_ge(*at(("E", it, s)))
                    row = d * MLH + hd
                    nc.tensor.matmul(ps[3], ident[0:8, row:row + 1].to_broadcast([8, P]), a_em[:, d],
                                             start=True, stop=True).then_inc(pe_done, pe.tick(("em", it)))

            def act_():
                for it in range(2 * MLH):
                    hd, d = divmod(it, 2)
                    if it >= 2:
                        act.wait_ge(*at(("num", it - 2)))
                    exponentials(it, d, a_e[:, it % 2], ps[3], ps[4],
                                 lambda s: c_g[:, d, s, d * MLH + hd:d * MLH + hd + 1])

            def dve_():
                for it in range(2 * MLH):
                    hd, d = divmod(it, 2)
                    dve.wait_ge(*at(("qk", hd)))
                    for s, spans in SPAN[d]:
                        dve.wait_ge(*at(("E", it, s)))
                        for c0, c1 in spans:
                            e = a_e[:, it % 2, s, c0:c1]
                            m = vmul(e, e, qk_cols(s, c0, c1))
                            m.then_inc(dve_done, dve.tick(("sD", it, s)))
                    dve.wait_ge(*at(("num", it)))
                    dve.step(nc.vector.tensor_scalar(inv, ps[7], -1.0, None, ALU.mult))
                    dve.step(nc.vector.tensor_tensor(inv, inv, ps[7], ALU.max))
                    dve.wait_ge(*at(("em", it)))
                    dve.step(nc.vector.tensor_tensor(inv, inv, ps[3], ALU.max))
                    dve.step(nc.vector.reciprocal(inv, inv))
                    for half in range(2):
                        o = a_u[:, 2 * hd + half, :]
                        if d == 0:
                            vmul(o, ps[5 + half], inv).then_inc(dve_done, dve.tick(("h", it)))
                        else:
                            dve.step(vmul(tmp, ps[5 + half], inv), ("h", it))
                            dve.step(vadd(o, o, tmp))

            block(pe_, act_, dve_)

        def mlstm_out():
            sq = a_e.rearrange("p a b c -> p (a b) c")
            inv = a_q

            def act_():
                for k in range(8):
                    nc.scalar.activation(sq[:, k, :], a_u[:, k, :], ACT.Square).then_inc(act_done, act.tick(("hsq", k)))
                for hd in range(MLH):
                    act.wait_ge(*at(("hsum", hd)))
                    nc.scalar.activation(inv[:, hd, :], ps[hd], ACT.Sqrt, bias=epsc[:], scale=1.0 / MLV).then_inc(act_done, act.tick(("hroot", hd)))

            def pe_():
                for hd in range(MLH):
                    pe.wait_ge(*at(("hsq", 2 * hd + 1)))
                    mms(ps[hd], [(ones[:], sq[:, 2 * hd + i, :]) for i in range(2)]).then_inc(pe_done, pe.tick(("hsum", hd)))

            def dve_():
                for hd in range(MLH):
                    dve.wait_ge(*at(("hroot", hd)))
                    dve.step(nc.vector.reciprocal(inv[:, hd, :], inv[:, hd, :]))
                    for k in (2 * hd, 2 * hd + 1):
                        dve.step(nc.vector.scalar_tensor_tensor(a_u[:, k, :], a_u[:, k, :], col("ml_norm", k),
                                                                inv[:, hd, :], ALU.mult, ALU.mult))
                        vmul(a_oz[:, k, :], a_oz[:, k, :], a_u[:, k, :]).then_inc(dve_done, dve.tick())

            block(pe_, act_, dve_)

        def ssd_rows():
            tmp = [a_e.rearrange("p a b c -> p (a b) c")[0:32, i, :] for i in range(8)]
            raw, dt, la = a_gates[:, 2, :], tmp[4], tmp[5]

            def dve_():
                dve.step(nc.vector.tensor_scalar(raw, raw, a_bias[:, 2:3], None, ALU.add))
                soft(raw, tmp, dt, 1, "dt")
                dve.wait_ge(*at("A"))
                dve.step(nc.vector.tensor_scalar(la, dt, a_bias[:, 4:5], -1.0, ALU.mult, ALU.mult))
                scans((la, la), a_brow[:, 0], a_brow[:, 1], ALU.add, 0.0)
                nc.vector.tensor_copy(tmp[6], dt).then_inc(dve_done, dve.tick("B rows"))
                for f in range(10):
                    o = halves(a_xs)[:, f]
                    for t in range(CONV):
                        x = a_xbc[:, f, :, t:t + 256]
                        w = col("ssd_conv_w", 10 * t + f)
                        if t == 0:
                            dve.step(nc.vector.tensor_scalar(o, x, w, col("ssd_conv_b", f), ALU.mult, ALU.add))
                        else:
                            dve.step(nc.vector.scalar_tensor_tensor(o, x, w, o, ALU.mult, ALU.add), ("conv", f, t))
                dve.wait_ge(*at("B columns"))
                nc.vector.tensor_scalar(a_cols[:, 128:384], ps[0][:, 0:256], -1.0, None, ALU.mult).then_inc(dve_done, dve.tick())
                nc.vector.tensor_copy(a_cols[:, 384:512], ps[0][:, 256:384]).then_inc(dve_done, dve.tick())

            def act_():
                nc.scalar.activation(a_bias[:, 4:5], a_bias[:, 3:4], ACT.Exp).then_inc(act_done, act.tick("A"))
                soft_act(tmp, "dt")
                for f in range(10):
                    act.wait_ge(*at(("conv", f, CONV - 1)))
                    nc.scalar.activation(a_xs[:, f, :], a_xs[:, f, :], ACT.Silu).then_inc(act_done, act.tick())

            def pe_():
                pe.wait_ge(*at("B rows"))
                for i, r in enumerate((a_brow[:, 0], a_brow[:, 1], tmp[6])):
                    for tt in range(TT):
                        m = nc.tensor.transpose(ps[0][:, (i * TT + tt) * 32:(i * TT + tt) * 32 + 32],
                                                r[:, tt * P:(tt + 1) * P], ident[0:32, 0:32])
                m.then_inc(pe_done, pe.tick("B columns"))

            block(pe_, act_, dve_)

        a_xt = region(22608, TT, D)

        def ssd_prepare():
            def pe_():
                j = 0
                for tt in range(TT):
                    for half in range(2):
                        o = bank("xt", j)
                        for i in range(4):
                            m = nc.tensor.transpose(o[:, i * P:(i + 1) * P], a_xs[:, 4 * half + i, tt * P:(tt + 1) * P],
                                                    ident[:])
                        m.then_inc(pe_done, pe.tick(("xt", j)))
                        j += 1
                for g in range(2):
                    r = slice(64 * g, 64 * g + 64)
                    for s in range(TT):
                        c0 = 0 if s < 2 else 256
                        mms(bank("xt", j)[:, c0:T], [(a_xs[r, 8, s * P:(s + 1) * P], a_xs[r, 9, c0:T])]).then_inc(pe_done, pe.tick(("xt", j)))
                        j += 1

            def read(e, copy, j):
                e.wait_ge(*at(("xt", j)))
                if j < 8:
                    tt, half = divmod(j, 2)
                    i = copy(a_xt[:, tt, 512 * half:512 * half + 512], ps[j % 8])
                else:
                    g, s = divmod(j - 8, 4)
                    c0 = 0 if s < 2 else 256
                    i = copy(a_cb[:, g, s, c0:T], ps[j % 8][:, c0:T])
                i.then_inc(e.sem, e.tick(("xt", "read", j)))

            def act_():
                for j in range(0, 16, 2):
                    read(act, lambda o, i: nc.scalar.activation(o, i, ACT.Copy), j)

            def dve_():
                for j in range(1, 16, 2):
                    read(dve, nc.vector.tensor_copy, j)

            block(pe_, act_, dve_)

        def ssd():
            n = 2 * SSH

            def head(it):
                hd, d = divmod(it, 2)
                return hd, d, hd // 2, hd % 2

            def pe_():
                def expo(it):
                    hd, d, _, _ = head(it)
                    if it >= 2:
                        for s in range(TT):
                            pe.wait_ge(*at(("E", it - 2, s)))
                    exponent_tiles(it, d, 32, d * SSH + hd, a_brow[:, d], ps[it % 2], ps[2 + it % 2])

                expo(0)
                for it in range(n):
                    hd, d, p, hf = head(it)
                    if it + 1 < n:
                        expo(it + 1)
                    if hf == 0 and d == 0 and p >= 2:
                        pe.wait_ge(*at(("y read", p - 2)))
                    o = ps[4 + p % 2][64 * hf:64 * hf + 64]
                    for k, (s, spans) in enumerate(SPAN[d]):
                        pe.wait_ge(*at(("W", it, s)))
                        for i, (c0, c1) in enumerate(spans):
                            m = nc.tensor.matmul(o[:, c0:c1], a_xt[:, s, hd * SSP:(hd + 1) * SSP], a_e[:, it % 2, s, c0:c1],
                                                 start=d == 0 and k == 0,
                                                 stop=d == 1 and k == TT - 1 and i == len(spans) - 1)
                    m.then_inc(pe_done, pe.tick(("y", it)))

            def act_():
                for it in range(n):
                    hd, d, _, _ = head(it)
                    if it >= 2:
                        act.wait_ge(*at(("y", it - 2)))
                    exponentials(it, d, a_e[:, it % 2], ps[it % 2], ps[2 + it % 2],
                                 lambda s: c_b[:, d, s, d * SSH + hd:d * SSH + hd + 1])

            def dve_():
                for it in range(n):
                    hd, d, p, hf = head(it)
                    for s, spans in SPAN[d]:
                        dve.wait_ge(*at(("E", it, s)))
                        for c0, c1 in spans:
                            e = a_e[:, it % 2, s, c0:c1]
                            nc.vector.scalar_tensor_tensor(
                                e, e, c_dt[:, s, d * SSH + hd:d * SSH + hd + 1], a_cb[:, hd // 8, s, c0:c1],
                                ALU.mult, ALU.mult).then_inc(dve_done, dve.tick(("W", it, s)))
                    if hf == 1 and d == 1:
                        dve.wait_ge(*at(("y", it)))
                        dve.step(nc.vector.scalar_tensor_tensor(a_xs[:, p, :], a_xs[:, p, :], a_cols[:, 16 + p:17 + p],
                                                                ps[4 + p % 2], ALU.mult, ALU.add), ("y read", p))
                        vmul(a_oz[:, 8 + p, :], a_oz[:, 8 + p, :], a_xs[:, p, :]).then_inc(dve_done, dve.tick())

            block(pe_, act_, dve_)

        def ssd_norm():
            def dve_(inv):
                for k in range(8):
                    nc.vector.scalar_tensor_tensor(a_oz[:, 8 + k, :], a_oz[:, 8 + k, :], col("ssd_norm", k),
                                                            inv, ALU.mult, ALU.mult).then_inc(dve_done, dve.tick())

            rms_block("sn", lambda k: a_oz[:, 8 + k, :], 8, T, D, (dve_, None), 26704)

        def out_projection(l, mix, kt, c0, y):
            def pe_():
                for j in range(4):
                    w = weights(("out", l, j))
                    for f in range(2):
                        mms(bank("op", 2 * j + f)[:, 0:T - c0], [(w[:, k, f * P:(f + 1) * P], mix[:, k, :]) for k in range(kt)]).then_inc(pe_done, pe.tick(("op", 2 * j + f), *((let_go(("out", l, j)),) if f == 1 else ())))

            def dve_():
                for j in range(8):
                    dve.wait_ge(*at(("op", j)))
                    nc.vector.tensor_copy(y[:, j, c0:T], ps[j][:, 0:T - c0]).then_inc(dve_done, dve.tick(("op", "read", j)))

            block(pe_, None, dve_, last=("out", l, 3))

        m_v = m_y = region(0, KD, T)
        m_gate = region(4096, NE, T)
        m_silu = region(12288, 4, T)
        m_small = region(12288, 24 * 64)
        m_rw = region(13824, KD, NE)
        m_gt = region(13952, T, rows=NE)
        p_vh, p_vl = parts_region(0, KD, T), parts_region(4096, KD, T)
        p_hh, p_hl = parts_region(8192, 4, T), parts_region(10240, 4, T)
        p_wh, p_wl = parts_region(12288, 4, 1024), parts_region(16384, 4, 1024)

        def router(l, c0):
            nt = (T - c0) // P
            t_ = [m_small[:, i * 64:i * 64 + 16 * nt] for i in range(16)]
            aff, bias, sel = t_[0], t_[1][:, 0:16], t_[2]
            grp = [t_[i].rearrange("p (t g e) -> p t g e", t=nt, g=4) for i in range(16)]
            tiny = m_small[:, 1024:1536].rearrange("p (i t g) -> p i t g", i=32, t=4)[:, :, 0:nt, :]

            def sp_():
                load(nc.sync, m_rw, A["router_w"].rearrange("(k p) e -> p k e", p=P))
                load(nc.sync, bias, A["router_bias"].rearrange("(o e) -> o e", o=1).to_broadcast([P, NE]))

            def pe_():
                pe.wait_ge(loads_landed, loads[0] + 32)
                for t in range(nt):
                    c = slice(c0 + t * P, c0 + t * P + P)
                    mms(ps[0][:, t * NE:(t + 1) * NE], [(m_v[:, k, c], m_rw[:, k, :]) for k in range(KD)]).then_inc(pe_done, pe.tick("logits"))
                pe.wait_ge(*at("gates"))
                for t in range(nt):
                    m = nc.tensor.transpose(ps[1][0:NE, t * P:(t + 1) * P], grp[4].rearrange("p t g e -> p t (g e)")[:, t, :],
                                            ident[:])
                m.then_inc(pe_done, pe.tick("gates turned"))
                pe.wait_ge(*at("gate rows"))
                for e in range(NE):
                    if e >= 6:
                        pe.wait_ge(*at(("gate read", e - 6)))
                    nc.tensor.matmul(ps[2 + e % 6][:, 0:T - c0], ident[0:NE, e:e + 1].to_broadcast([NE, P]),
                                             m_gt[:, c0:T], start=True, stop=True).then_inc(pe_done, pe.tick(("gate spread", e)))

            def act_():
                act.wait_ge(*at("logits"))
                nc.scalar.activation(aff, ps[0][:, 0:NE * nt], ACT.Sigmoid).then_inc(act_done, act.tick("affinities"))
                for k in range(KD):
                    nc.scalar.activation(p_vh[:, k, c0:T], m_v[:, k, c0:T], ACT.Copy).then_inc(act_done, act.tick(("high part", k)))
                for e in range(0, NE, 2):
                    act.wait_ge(*at(("gate spread", e)))
                    nc.scalar.activation(m_gate[:, e, c0:T], ps[2 + e % 6][:, 0:T - c0], ACT.Copy).then_inc(act_done, act.tick(("gate read", e)))

            def rank(x, out, tmp):
                dve.step(nc.vector.memset(out, 0.0))
                for i in range(4):
                    for j in range(i + 1, 4):
                        a, b = x[:, :, :, i:i + 1], x[:, :, :, j:j + 1]
                        dve.step(nc.vector.tensor_tensor(tmp, b, a, ALU.is_gt))
                        dve.step(vadd(out[:, :, :, i:i + 1], out[:, :, :, i:i + 1], tmp))
                        dve.step(nc.vector.tensor_scalar(tmp, tmp, -1.0, 1.0, ALU.mult, ALU.add))
                        dve.step(vadd(out[:, :, :, j:j + 1], out[:, :, :, j:j + 1], tmp))

            def dve_():
                v = nc.vector
                dve.wait_ge(*at("affinities"))
                dve.step(vadd(grp[2].rearrange("p t g e -> p t (g e)"), grp[0].rearrange("p t g e -> p t (g e)"),
                              bias.unsqueeze(1).to_broadcast([P, nt, NE])))
                rank(grp[2], grp[3], tiny[:, 0].unsqueeze(3))
                dve.step(v.tensor_scalar(t_[3], t_[3], 2.0, None, ALU.is_lt))
                dve.step(vmul(t_[5], t_[3], sel))
                dve.step(v.tensor_reduce(tiny[:, 1], grp[5], AX.X, ALU.add))
                rank(tiny[:, 1].unsqueeze(2), tiny[:, 2].unsqueeze(2), tiny[:, 3, :, 0:1].unsqueeze(3))
                dve.step(v.tensor_scalar(tiny[:, 2], tiny[:, 2], 1.0, None, ALU.is_lt))
                dve.step(vmul(grp[3], grp[3], tiny[:, 2].unsqueeze(3).to_broadcast([P, nt, 4, 4])))
                dve.step(vmul(t_[3], t_[3], aff))
                dve.step(v.tensor_reduce(tiny[:, 4, :, 0:1], grp[3].rearrange("p t g e -> p t (g e)"), AX.X, ALU.add))
                dve.step(v.reciprocal(tiny[:, 5, :, 0:1], tiny[:, 4, :, 0:1]))
                dve.step(vmul(grp[4].rearrange("p t g e -> p t (g e)"), grp[3].rearrange("p t g e -> p t (g e)"),
                              tiny[:, 5, :, 0:1].to_broadcast([P, nt, NE])), "gates")
                dve.wait_ge(*at("gates turned"))
                dve.step(v.tensor_copy(m_gt[:, c0:T], ps[1][0:NE, 0:T - c0]), "gate rows")
                for e in range(1, NE, 2):
                    dve.wait_ge(*at(("gate spread", e)))
                    v.tensor_copy(m_gate[:, e, c0:T], ps[2 + e % 6][:, 0:T - c0]).then_inc(dve_done, dve.tick(("gate read", e)))

            def pool_():
                for k in range(KD):
                    pool.wait_ge(*at(("high part", k)))
                    nc.gpsimd.tensor_tensor(p_vl[:, k, c0:T], m_v[:, k, c0:T], whole(p_vh[:, k, c0:T]), ALU.subtract).then_inc(pool_done, pool.tick())

            block(pe_, act_, dve_, pool_, sp_)

        def experts(l, c0):
            n = T - c0
            first = piece_at[("experts", l)]
            key = ("expert loop", l)

            def quarter(x, q):
                return x[:, q % 4, :].rearrange("p (k n) -> p k n", k=8 if q < 8 else 4)

            def landed_quarter(w, q):
                n_ = 128 if q < 8 else 256
                return w(q // 4)[:, :, (q % 4) * n_:(q % 4 + 1) * n_]

            def pe_ffn():
                for q in range(8):
                    pe.wait_ge(*at(("split", q)))
                    pe.wait_ge(*at(("out read", q), back=1))
                    wh, wl = quarter(p_wh, q), quarter(p_wl, q)
                    pairs = []
                    for k in range(KD):
                        pairs += three(wh[:, k, :], wl[:, k, :], p_vh[:, k, c0:T], p_vl[:, k, c0:T])
                    mms(ps[q][:, 0:n], pairs).then_inc(pe_done, pe.tick(("g" if q < 4 else "u", q % 4), ("used", q)))
                pe.wait_ge(*at(("silu", 3)))
                for q in range(8, 12):
                    pe.wait_ge(*at(("split", q)))
                    wh, wl = quarter(p_wh, q), quarter(p_wl, q)
                    for k in range(4):
                        pe.wait_ge(*at(("hidden", k)))
                        for i in range(2):
                            j, c = 2 * (q - 8) + i, slice(i * P, (i + 1) * P)
                            for x, (a, b) in enumerate(three(wh[:, k, c], wl[:, k, c], p_hh[:, k, 0:n], p_hl[:, k, 0:n])):
                                m = nc.tensor.matmul(ps[j][:, 0:n], a, b, start=k == 0 and x == 0, stop=k == 3 and x == 2)
                            if k == 3:
                                m.then_inc(pe_done, pe.tick(("out", j), *([("used", q)] if i else [])))

            def act_ffn(w, landed):
                def split_high(q):
                    if q % 4 == 0:
                        act.wait_ge(*landed(q // 4))
                    if q >= 4:
                        act.wait_ge(*at(("used", q - 4)))
                    else:
                        act.wait_ge(*at(("used", q + 8), back=1))
                    nc.scalar.activation(quarter(p_wh, q), landed_quarter(w, q), ACT.Copy).then_inc(act_done, act.tick(("high", q)))

                for q in range(4):
                    split_high(q)
                for f in range(4):
                    act.wait_ge(*at(("g", f)))
                    nc.scalar.activation(m_silu[:, f, 0:n], ps[f][:, 0:n], ACT.Silu).then_inc(act_done, act.tick(("silu", f)))
                    split_high(4 + f)
                for q in range(8, 12):
                    split_high(q)

            def pool_ffn(w, freed):
                for q in range(12):
                    pool.wait_ge(*at(("high", q)))
                    nc.gpsimd.tensor_tensor(quarter(p_wl, q), landed_quarter(w, q), whole(quarter(p_wh, q)), ALU.subtract).then_inc(pool_done, pool.tick(("split", q), *([freed(q // 4)] if q % 4 == 3 else [])))

            def dve_ffn(gate):
                for f in range(4):
                    dve.wait_ge(*at(("silu", f)))
                    dve.wait_ge(*at(("u", f)))
                    t_ = m_silu[:, f, 0:n]
                    dve.step(vmul(t_, ps[4 + f][:, 0:n], t_))
                    if gate is not None:
                        dve.step(vmul(t_, t_, gate))
                    dve.step(nc.vector.tensor_copy(p_hh[:, f, 0:n], t_))
                    vsub(p_hl[:, f, 0:n], t_, whole(p_hh[:, f, 0:n])).then_inc(dve_done, dve.tick(("hidden", f)))
                for j in range(8):
                    dve.wait_ge(*at(("out", j)))
                    y = m_y[:, j, c0:T]
                    if gate is None:
                        nc.vector.tensor_copy(y, ps[j][:, 0:n]).then_inc(dve_done, dve.tick(("out read", j)))
                    else:
                        vadd(y, y, ps[j][:, 0:n]).then_inc(dve_done, dve.tick(("out read", j)))

            shapes = [(8, 512), (8, 512), (4, 1024)]
            names = ("exp_w_gate", "exp_w_up", "exp_w_down")

            def load_expert(e, k):
                src = A[names[k]][l, bass.ds(e, 1)].rearrange("o (k p) n -> p (o k) n", p=P)
                s = (first + k) % NSLOT
                nc.sync.dma_start(slot_view(s, *shapes[k]), src).then_inc(weights_landed[s], 16)

            def sp_first():
                stream_weights(piece_at[("sh", l, 2)])
                for k in range(3):
                    sp.wait_ge(*at(("let go", first + k - NSLOT)))
                    load_expert(0, k)
                issued[0] += 3 * NE

            def shared_w(k):
                return slot_view(first - 3 + k, *shapes[k])

            def shared_landed(k):
                i = first - 3 + k
                return weights_landed[i % NSLOT], 16 * (i // NSLOT + 1)

            block(pe_ffn, lambda: act_ffn(shared_w, shared_landed), lambda: dve_ffn(None),
                  lambda: pool_ffn(shared_w, lambda k: let_go(("sh", l, k))), sp_first)

            def looped(engine, lo, body):
                with engine.e.Fori(lo, NE) as e:
                    engine.start_loop(e, key, NE)
                    body(e)
                    engine.end_loop()

            def expert_w(k):
                return slot_view(first + k, *shapes[k])

            def act_loop(e):
                act_ffn(expert_w, lambda k: (weights_landed[(first + k) % NSLOT], e * 16 + 16 * ((first + k) // NSLOT + 1)))

            def pool_loop(e):
                pool_ffn(expert_w, lambda k: ("let go", first + 3 * NE - NSLOT + k))

            def sp_loop(e):
                for k in range(3):
                    sp.wait_ge(*at(("let go", first + 3 * NE - NSLOT + k), back=1))
                    load_expert(e, k)

            def sp_all():
                looped(sp, 1, sp_loop)
                if issued[0] < len(pieces):
                    stream_weights(issued[0] - 1)

            block(lambda: looped(pe, 0, lambda e: pe_ffn()), lambda: looped(act, 0, act_loop),
                  lambda: looped(dve, 0, lambda e: dve_ffn(m_gate[:, bass.ds(e, 1), c0:T].rearrange("p o t -> p (o t)"))),
                  lambda: looped(pool, 0, pool_loop), sp_all)

        def moe(l, c0):
            modulated("v", 2, 24, m_v, 12288, c0)
            router(l, c0)
            experts(l, c0)
            residual("r", 3, m_y, 12288, c0)

        b_rope = region(0, 2, NL)
        b_rmask = region(512, 2, 6, L)
        b_restart = region(1280, 2, 8 * L)
        b_w2, b_a2, b_g2 = region(2304, D), region(3328, D), region(4352, D)
        b_r, b_k, b_v = region(5376, KD, NL), region(7424, KD, T), region(11520, KD, T)
        b_kk = region(15616, KD, T)
        b_mix = region(19712, 12, NL)
        b_att, b_y = b_mix[:, 0:4, :], b_mix[:, 4:12, :]
        b_tw, b_al, b_gl = region(22784, T), region(23296, T), region(23808, NL)
        b_u = region(28416, KD, T)
        n_q, n_kv = region(5376, 3, NL), region(6144, 2, T)
        n_kr = region(7168, 2, T)
        n_uq, n_uqs, n_ukv = region(8192, 3, AH * HD), region(10496, 3, AH * ROPE), region(11264, 2, D)
        n_kh, n_vt = region(13312, AH, T), region(17408, TT, AH * AV)
        n_qh = region(24064, AH, NL)
        n_p, n_pt = region(26112, 2, T), region(27136, 2, T)
        n_krs = region(28160, KD, ROPE)
        n_stat = region(34600, 4, 16)
        lat = slice(NC_, T)

        def swap(dst, src, e, label):
            nc.gpsimd.tensor_copy(dst[..., 0:16], src[..., 16:32]).then_inc(e.sem, e.tick())
            return nc.gpsimd.tensor_copy(dst[..., 16:32], src[..., 0:16]).then_inc(e.sem, e.tick(label))

        def project_mla():
            i_kv = piece_at["mkv"]

            def pe_():
                w = weights("mq")
                for f in range(3):
                    mms(ps[f][:, 0:NL], [(w[:, k, f * P:(f + 1) * P], b_u[:, k, lat]) for k in range(KD)]).then_inc(pe_done, pe.tick(("q", f), *((let_go("mq"),) if f == 2 else ())))
                w = weights("mkv")
                for f in range(2):
                    mms(ps[3 + f], [(w[:, k, f * P:(f + 1) * P], b_u[:, k, :]) for k in range(KD)]).then_inc(pe_done, pe.tick(("kv", f)))
                mms(ps[5][64:96, :], [(w[:, k, 256:288], b_u[:, k, :]) for k in range(KD)])
                pe.wait_ge(*at("kr swapped"))
                mms(ps[6][64:96, :], [(n_krs[:, k, :], b_u[:, k, :]) for k in range(KD)]).then_inc(pe_done, pe.tick("kr", let_go("mkv")))

            def pool_():
                _, kt, n = pieces[i_kv]
                pool.wait_ge(weights_landed[i_kv % NSLOT], 16 * (i_kv // NSLOT + 1))
                swap(n_krs, slot_view(i_kv, kt, n)[:, :, 256:288], pool, "kr swapped")
                pool.wait_ge(loads_landed, loads[0] + 16 * 5)
                for k in range(3):
                    dst = n_uqs[:, k, :].rearrange("p (h r) -> p h r", h=AH)
                    src = n_uq[:, k, :].rearrange("p (h x) -> p h x", h=AH)[:, :, NOPE:HD]
                    swap(dst, src, pool, "uq swapped")

            def act_():
                for f in range(3):
                    act.wait_ge(*at(("q", f)))
                    nc.scalar.activation(n_q[:, f, :], ps[f][:, 0:NL], ACT.Copy).then_inc(act_done, act.tick())

            def dve_():
                for f in range(2):
                    dve.wait_ge(*at(("kv", f)))
                    nc.vector.tensor_copy(n_kv[:, f, :], ps[3 + f]).then_inc(dve_done, dve.tick())
                dve.wait_ge(*at("kr"))
                dve.wait_ge(loads_landed, loads[0] + 16 * 5)
                r = slice(64, 96)
                nc.vector.tensor_copy(n_kr[r, 0, 0:NC_], ps[5][r, 0:NC_]).then_inc(dve_done, dve.tick())
                vmul(n_kr[r, 0, lat], ps[5][r, lat], b_rope[r, 0, :]).then_inc(dve_done, dve.tick())
                dve.step(vmul(n_kr[r, 1, lat], ps[6][r, lat], b_rope[r, 1, :]))
                vadd(n_kr[r, 0, lat], n_kr[r, 0, lat], n_kr[r, 1, lat]).then_inc(dve_done, dve.tick())

            def sp_():
                load(nc.sync, b_rope[64:96], A["rope"])
                load(nc.sync, n_uq, A["mla_w_uq"][0].rearrange("(k p) n -> p k n", p=P))
                load(nc.sync, n_ukv, A["mla_w_ukv"][0].rearrange("(k p) n -> p k n", p=P))
                load(nc.sync, b_rmask, A["rmask"])
                load(nc.sync, b_restart, A["restart"])

            block(pe_, act_, dve_, pool_, sp_, last="mkv")

        def norm_latent(tag, x, n, cols, dim, gain):
            def dve_(inv):
                for k in range(n):
                    nc.vector.scalar_tensor_tensor(x[:, k, :], x[:, k, :], col(gain, k), inv, ALU.mult,
                                                            ALU.mult).then_inc(dve_done, dve.tick())

            rms_block(tag, lambda k: x[:, k, :], n, cols, dim, (dve_, None), 13312)

        def attention_heads():
            r = slice(64, 96)
            ukv = n_ukv.rearrange("p k (h x) -> p k h x", h=AH)
            tmp = n_p

            def pe_():
                for hd in range(AH):
                    o = bank("ah", 2 * hd)
                    mms(o[0:HD, 0:NL], [(n_uq[:, k, hd * HD:(hd + 1) * HD], n_q[:, k, :]) for k in range(3)])
                    mms(o[r, NL:T], [(n_uqs[:, k, hd * ROPE:(hd + 1) * ROPE], n_q[:, k, :]) for k in range(3)]).then_inc(pe_done, pe.tick(("ah", 2 * hd)))
                    mms(bank("ah", 2 * hd + 1)[0:64, :], [(ukv[:, k, hd, 0:64], n_kv[:, k, :]) for k in range(2)]).then_inc(pe_done, pe.tick(("ah", 2 * hd + 1)))
                for tt in range(TT):
                    mms(bank("ah", 16 + tt), [(n_kv[:, k, tt * P:(tt + 1) * P], ukv[:, k, :, 64:128]) for k in range(2)]).then_inc(pe_done, pe.tick(("ah", 16 + tt)))

            def dve_():
                for hd in range(AH):
                    dve.wait_ge(*at(("ah", 2 * hd)))
                    o, t = ps[(2 * hd) % 8], tmp[r, hd % 2, 0:NL]
                    one = nc.vector.scalar_tensor_tensor
                    nc.vector.tensor_scalar(n_qh[0:64, hd, :], o[0:64, 0:NL], ASCALE, None, ALU.mult).then_inc(dve_done, dve.tick())
                    one(t, o[r, 0:NL], ASCALE, b_rope[r, 0, :], ALU.mult, ALU.mult).then_inc(dve_done, dve.tick())
                    dve.step(one(n_qh[r, hd, :], o[r, NL:T], ASCALE, b_rope[r, 1, :], ALU.mult, ALU.mult),
                             ("ah", "read", 2 * hd))
                    vadd(n_qh[r, hd, :], n_qh[r, hd, :], t).then_inc(dve_done, dve.tick())

            def act_():
                for hd in range(AH):
                    act.wait_ge(*at(("ah", 2 * hd + 1)))
                    nc.scalar.activation(n_kh[0:64, hd, :], ps[(2 * hd + 1) % 8][0:64, :], ACT.Copy).then_inc(act_done, act.tick(("ah", "read", 2 * hd + 1)))
                for tt in range(TT):
                    act.wait_ge(*at(("ah", 16 + tt)))
                    nc.scalar.activation(n_vt[:, tt, :], ps[(16 + tt) % 8], ACT.Copy).then_inc(act_done, act.tick(("ah", "read", 16 + tt)))

            def pool_():
                for hd in range(AH):
                    nc.gpsimd.tensor_copy(n_kh[r, hd, :], n_kr[r, 0, :]).then_inc(pool_done, pool.tick())

            block(pe_, act_, dve_, pool_)

        def attention():
            n = 2 * AH
            neg, total, inv = n_stat[:, 0], n_stat[:, 1], n_stat[:, 2]

            def pe_():
                def scores(j):
                    hd, jt = divmod(j, 2)
                    pe.wait_ge(*at(("P", j - 2)))
                    mms(ps[j % 2], [(n_qh[0:HD, hd, jt * P:(jt + 1) * P], n_kh[0:HD, hd, :])]).then_inc(pe_done, pe.tick(("scores", j)))

                scores(0)
                for j in range(n):
                    hd, jt = divmod(j, 2)
                    if j + 1 < n:
                        scores(j + 1)
                    pe.wait_ge(*at(("Pn", j)))
                    pe.wait_ge(*at(("PT", j - 2)))
                    for s in range(TT):
                        m = nc.tensor.transpose(ps[2 + j % 2][:, s * P:(s + 1) * P], n_p[:, j % 2, s * P:(s + 1) * P],
                                                ident[:])
                    m.then_inc(pe_done, pe.tick(("turned", j)))
                    pe.wait_ge(*at(("PT", j)))
                    if hd % 2 == 0 and jt == 0:
                        pe.wait_ge(*at(("att read", hd // 2 - 2)))
                    rows = slice(64 * (hd % 2), 64 * (hd % 2) + 64)
                    mms(ps[4 + (hd // 2) % 2][rows, jt * P:(jt + 1) * P], [(n_vt[:, s, hd * AV:(hd + 1) * AV], n_pt[:, j % 2, s * P:(s + 1) * P]) for s in range(TT)]).then_inc(pe_done, pe.tick(("O", j)))

            def dve_():
                for j in range(n):
                    dve.wait_ge(*at(("scores", j)))
                    nc.vector.tensor_reduce(neg[:, j:j + 1], ps[j % 2], AX.X, ALU.max, negate=True).then_inc(dve_done, dve.tick(("max", j)))
                    dve.wait_ge(*at(("P", j)))
                    dve.step(nc.vector.reciprocal(inv[:, j:j + 1], total[:, j:j + 1]))
                    nc.vector.tensor_scalar(n_p[:, j % 2, :], n_p[:, j % 2, :], inv[:, j:j + 1], None, ALU.mult).then_inc(dve_done, dve.tick(("Pn", j)))
                    if j % 4 == 3:
                        dve.wait_ge(*at(("O", j)))
                        nc.vector.tensor_copy(b_att[:, j // 4, :], ps[4 + (j // 4) % 2][:, 0:NL]).then_inc(dve_done, dve.tick(("att read", j // 4)))

            def act_():
                def turn(j):
                    act.wait_ge(*at(("turned", j)))
                    act.wait_ge(*at(("O", j - 2)))
                    nc.scalar.activation(n_pt[:, j % 2, :], ps[2 + j % 2], ACT.Copy).then_inc(act_done, act.tick(("PT", j)))

                for j in range(n):
                    act.wait_ge(*at(("max", j)))
                    act.wait_ge(*at(("turned", j - 2)))
                    nc.scalar.activation(n_p[:, j % 2, :], ps[j % 2], ACT.Exp, bias=neg[:, j:j + 1],
                                                  accum_out=total[:, j:j + 1]).then_inc(act_done, act.tick(("P", j)))
                    turn(j)

            block(pe_, act_, dve_)

        def project_rwkv():
            raw = region(32512, 2, 2, 258)
            tmp = region(33544, T)
            jobs = [(("r", j // 4), j % 4, b_r[:, j, :], j) for j in range(8)]
            jobs += [(("rk", j // 4), j % 4, b_k[:, j, :], 8 + j) for j in range(8)]
            jobs += [(("rv", j // 4), j % 4, b_v[:, j, :], 16 + j) for j in range(8)]
            jobs += [("low", 0, b_tw, 24), ("low", 1, b_al, 25), ("low", 2, b_gl, 26)]

            def pe_():
                for j, (key, f, _, _) in enumerate(jobs):
                    w = weights(key) if f == 0 else w
                    last = f == (2 if key == "low" else 3)
                    mms(bank("rw", j), [(w[:, k, f * P:(f + 1) * P], b_u[:, k, :]) for k in range(KD)]).then_inc(pe_done, pe.tick(("rw", j), *((let_go(key),) if last else ())))

            def pool_():
                nc.gpsimd.memset(raw[:, :, :, 0:1], 0.0).then_inc(pool_done, pool.tick("pads"))
                nc.gpsimd.memset(raw[:, :, :, 257:258], 0.0).then_inc(pool_done, pool.tick("pads"))

            def act_():
                for j in range(len(jobs)):
                    act.wait_ge(*at(("rw", j)))
                    act.wait_ge(*at(("mixed", j - 2)))
                    nc.scalar.activation(raw[:, j % 2, :, 1:257], ps[j % 8].rearrange("p (s t) -> p s t", s=2),
                                                  ACT.Copy).then_inc(act_done, act.tick(("rw", "read", j)))
                act.wait_ge(*at(("mixed", 26)))
                nc.scalar.activation(b_tw, b_tw, ACT.Tanh).then_inc(act_done, act.tick())
                nc.scalar.activation(b_gl, b_gl, ACT.Sigmoid).then_inc(act_done, act.tick())

            def dve_():
                dve.wait_ge(*at("pads"))
                for j, (_, _, dst, m) in enumerate(jobs):
                    dve.wait_ge(*at(("rw", "read", j)))
                    s = slice(1, 2) if dst.shape[-1] == NL else slice(0, 2)
                    x, n = raw[:, j % 2, s], s.stop - s.start
                    t, o = (y.rearrange("p (s t) -> p s t", s=n) for y in (tmp[:, 0:256 * n], dst))
                    one = nc.vector.scalar_tensor_tensor
                    dve.step(vadd(t, x[:, :, 0:256], x[:, :, 2:258]))
                    dve.step(one(t, t, 0.5, x[:, :, 1:257], ALU.mult, ALU.subtract))
                    dve.step(one(o, t, col("rw_mu", m), x[:, :, 1:257], ALU.mult, ALU.add), ("mixed", j))

            def sp_():
                load(nc.sync, b_w2, A["rw_w2"].rearrange("l a r n -> (l a r) n"))
                load(nc.sync, b_a2, A["rw_a2"].rearrange("l a r n -> (l a r) n"))
                load(nc.sync, b_g2, A["rw_g2"].rearrange("l r n -> (l r) n"))

            def sp_all():
                sp_()
                stream_weights(piece_at["low"] - NSLOT)

            block(pe_, act_, dve_, pool_, sp_all)

        def key_norms():
            sq, root = region(24064, 2, T), region(25088, 2, T)

            def act_():
                for k in range(KD):
                    act.wait_ge(*at(("kx", k)))
                    act.wait_ge(*at(("ksum", k - 2)))
                    nc.scalar.activation(sq[:, k % 2, :], b_kk[:, k, :], ACT.Square).then_inc(act_done, act.tick(("ksq", k)))
                    act.wait_ge(*at(("ksum", k)))
                    act.wait_ge(*at(("kn", k - 2)))
                    nc.scalar.activation(root[:, k % 2, :], ps[k % 2], ACT.Sqrt).then_inc(act_done, act.tick(("kroot", k)))

            def pe_():
                for k in range(KD):
                    pe.wait_ge(*at(("ksq", k)))
                    pe.wait_ge(*at(("kroot", k - 2)))
                    mms(ps[k % 2], [(blockones[:], sq[:, k % 2, :])]).then_inc(pe_done, pe.tick(("ksum", k)))

            def dve_():
                for k in range(KD):
                    nc.vector.tensor_scalar(b_kk[:, k, :], b_k[:, k, :], col("rw_kk", k), None, ALU.mult).then_inc(dve_done, dve.tick(("kx", k)))
                for k in range(KD):
                    dve.wait_ge(*at(("kroot", k)))
                    x = root[:, k % 2, :]
                    dve.step(nc.vector.tensor_scalar(x, x, 1e-12, None, ALU.max))
                    dve.step(nc.vector.reciprocal(x, x))
                    vmul(b_kk[:, k, :], b_kk[:, k, :], x).then_inc(dve_done, dve.tick(("kn", k)))

            block(pe_, act_, dve_)

        ringflat = ring[:].rearrange("p s n -> p (s n)")


        def staging(d):
            def at(i, n=8 * L):
                if d == 0 and i >= 20:
                    return h[:, :, (i - 20) * L:(i - 19) * L]
                a = 512 * i
                flat = arena[:, 24064 + a:24064 + a + n] if d == 0 else ringflat[:, a:a + n]
                return flat.rearrange("p (h t) -> p h t", t=L)

            s = {n_: at(i) for i, n_ in enumerate(
                ("a", "r", "vt", "Ot", "RB", "RK", "D", "Dt", "D2", "D2t", "T", "Q", "S",
                 "sw", "G", "A", "t", "Pinv", "bend", "v", "AK", "bt", "kt"))}
            s.update(Pexc=s["sw"], next_a=s["sw"], Pinc=s["G"], next_r=s["G"], b=s["A"], k=s["t"], kend=s["Pinv"])
            s.update(D4=s["D"], D4t=s["Dt"], D8t=s["D2t"], N=s["D"], Nt=s["Dt"], Tdt=s["D2"], W=s["D"], U=s["Dt"], M=s["Ot"])
            flat = arena[:, 34304:34448] if d == 0 else ringflat[:, 11776:11920]
            s["low"] = flat[:, 0:2 * L].rearrange("p (h t) -> p h t", t=L)
            s["end"], s["next_end"] = flat[:, 2 * L:2 * L + 8], flat[:, 2 * L + 8:2 * L + 16]
            return s

        st = [staging(0), staging(1)]

        def products(seg, main, front):
            p = []
            if main:
                p += [("bt", (), ("bend",), "bend"), ("kt", (), ("kend",), "kend"), ("vt", (), ("v",), "v"),
                      ("X", ("a",), ("b",), [("b", "a")]), ("Xt", (), (), [("a", "b")]), ("AK", (), ("k",), [("k", "a")])]
                if seg == 1:
                    p += [("RB", ("r",), (), [("b", "r")]), ("RK", (), (), [("k", "r")])]
            if front:
                p += [("z", ("low",), (), None), ("za", (), (), None)]
            if main:
                p += [("D2", ("D", "Dt"), (), [("Dt", "D")]), ("D2t", (), (), [("D", "Dt")]),
                      ("T2", ("T1", "D2", "D2t"), (), [("D2t", "T")]), ("D4", (), (), [("D2t", "D2")]),
                      ("D4t", (), (), [("D2", "D2t")]), ("T4", ("T2", "D4t", "D4"), (), [("D4t", "T")]),
                      ("D8t", (), (), [("D4", "D4t")]), ("T8", ("T4", "D8t"), (), [("D8t", "T")]),
                      ("N", ("T8", "Ot"), (), [("Ot", "T")]), ("Nt", (), (), [("T", "Ot")]), ("Tdt", (), (), "T"),
                      ("N2", ("N", "Nt"), (), [("Nt", "N")]), ("NQ", ("Q1",), (), [("Nt", "Q")]),
                      ("M", ("Q2", "Tdt"), (), [("Tdt", "Q")]),
                      ("W", ("AK", "vt"), ("S",), [("a", "S"), ("AK", "vt")]), ("U", ("M", "W"), (), [("M", "W")])]
                if seg == 1:
                    p += [("Y", ("U", "RB", "RK"), (), [("S", "r"), ("U", "RB"), ("vt", "RK")])]
                p += [("S", ("U", "bt", "kt"), (), [("bt", "U"), ("kt", "vt")])]
            return p

        def rwkv(key, main, front, rounds=1):
            seg, main_chunk = main or (None, None)
            next_seg, front_chunk = front or (None, None)
            prods = products(seg, main is not None, front is not None)
            order = [x[0] for x in prods]

            def bank_of(d, n_):
                return ps[4 * d + order.index(n_) % 4]

            def view(d, n_):
                return bank_of(d, n_).rearrange("p (h t) -> p h t", t=L)

            def chunk(x, seg, j, d, base=0):
                first_col = seg * 256 + (j * L if d == 0 else 192 - j * L) - base
                return x[:, :, bass.ds(first_col, L)]

            def pe_round(i):
                for j, (n_, now, last, pairs) in enumerate(prods):
                    for d in range(2):
                        now_, last_ = [(x, d) for x in now], [(x, d) for x in last]
                        if j >= 4:
                            now_.append((order[j - 4] + " read", d))
                        else:
                            last_.append(([x for k, x in enumerate(order) if k % 4 == j][-1] + " read", d))
                        pe.wait_ge(*latest("act", now_, last_))
                        pe.wait_ge(*latest("dve", now_, last_))
                        pe.settle()
                        o = bank_of(d, n_)
                        if pairs is None:
                            w = b_w2 if n_ == "z" else b_a2
                            rows = slice(64 * d, 64 * d + 64)
                            for f in range(KD):
                                m = nc.tensor.matmul(o[:, f * L:(f + 1) * L], w[rows, f * P:(f + 1) * P],
                                                     st[d]["low"][rows, 0 if n_ == "z" else 1, :], start=True, stop=True)
                        elif isinstance(pairs, str):
                            for p in range(4):
                                m = nc.tensor.transpose(o[:, p * P:(p + 1) * P],
                                                        st[d][pairs][:, 2 * p:2 * p + 2, :].rearrange("p h t -> p (h t)"), ident[:])
                        else:
                            for p in range(8):
                                for hf in range(2):
                                    rows = slice(64 * hf, 64 * hf + 64)
                                    for q, (a, b) in enumerate(pairs):
                                        m = nc.tensor.matmul(o[rows, p * L:(p + 1) * L], st[d][a][rows, p, :], st[d][b][rows, p, :],
                                                             start=q == 0, stop=q == len(pairs) - 1)
                        m.then_inc(pe_done, pe.tick((n_ + " product", d)))

            def act_round(i):
                def fn(d, label, o, x, f=ACT.Copy, **kw):
                    nc.scalar.activation(o, x, f, **kw).then_inc(act_done, act.tick((label, d)))

                def turn(n_, last=None):
                    for d in range(2):
                        act.wait_ge(*at(((last or n_) + " product", d)))
                        nc.scalar.activation(st[d][n_], view(d, n_), ACT.Copy).then_inc(
                            act_done, act.tick((n_, d), (n_ + " read", d)))

                def regroup(n_):
                    for d in range(2):
                        act.wait_ge(*at((n_ + " product", d)))
                        o = bank_of(d, n_).rearrange("p (q h t) -> p q h t", q=4, h=2)
                        dst = st[d][n_].rearrange("p (q h) t -> p q h t", h=2)
                        for odd in range(2):
                            for hf in range(2):
                                m = nc.scalar.activation(dst[64 * hf:64 * hf + 64, :, odd, :], o[64 * odd:64 * odd + 64, :, hf, :], ACT.Copy)
                                m.then_inc(act_done, act.tick(*([(n_, d), (n_ + " read", d)] if odd and hf else [])))

                if main:
                    for d in range(2):
                        act.wait_ge(*at(("S read", d), back=1))
                        fn(d, "a", st[d]["a"], st[d]["next_a"])
                        if seg == 1:
                            fn(d, "r", st[d]["r"], st[d]["next_r"])
                        fn(d, "end", st[d]["end"], st[d]["next_end"])
                if front:
                    j = front_chunk(i)
                    for d in range(2):
                        c = next_seg * 256 + (j * L if d == 0 else 192 - j * L)
                        act.wait_ge(*at(("za product", d), back=1))
                        nc.scalar.activation(st[d]["low"][:, 0, :], b_tw[:, bass.ds(c, L)], ACT.Copy).then_inc(act_done, act.tick())
                        fn(d, "low", st[d]["low"][:, 1, :], b_al[:, bass.ds(c, L)])
                if main:
                    regroup("bt")
                    regroup("kt")
                    regroup("vt")
                if front:
                    for d in range(2):
                        fn(d, "v", st[d]["v"], chunk(b_v, next_seg, j, d))
                if main:
                    turn("D2")
                    turn("D2t")
                if front:
                    for d in range(2):
                        s = st[d]
                        act.wait_ge(*at(("z+w0", d)))
                        fn(d, "tanh w", s["sw"], s["sw"], ACT.Tanh, scale=0.5)
                        act.wait_ge(*at(("a+a0", d)))
                        fn(d, "tanh a", s["A"], s["A"], ACT.Tanh, scale=0.5)
                if main:
                    turn("D4", last="D4t")
                    turn("D4t")
                if front:
                    for d in range(2):
                        s = st[d]
                        act.wait_ge(*at(("G-sw", d)))
                        fn(d, "Pinv", s["Pinv"], s["G"], ACT.Exp, scale=LWC)
                        fn(d, "Pinc", s["Pinc"], s["G"], ACT.Exp, scale=-LWC)
                        fn(d, "Pexc", s["Pexc"], s["Pexc"], ACT.Exp, scale=-LWC)
                if main:
                    turn("D8t")
                    turn("N")
                    turn("Nt")
                    regroup("Tdt")
                    turn("M")
                    turn("W")
                    turn("U")

            def dve_round(i):
                v = nc.vector

                def go(ins, d, *names, settle=False):
                    dve.step(ins, *[(n_, d) for n_ in names])
                    if settle:
                        dve.settle()

                def across(name, k):
                    c = VEC[name] + k
                    return vec[:, c:c + 8].unsqueeze(2).to_broadcast([P, 8, L])

                def mask(d, k):
                    return b_rmask[:, d, k, :].unsqueeze(1).to_broadcast([P, 8, L])

                def front_1():
                    for d in range(2):
                        s = st[d]
                        dve.wait_ge(*at(("z product", d)))
                        go(vadd(s["sw"], view(d, "z"), across("rw_w0", 8 * d)), d, "z+w0", "z read")
                        dve.wait_ge(*at(("za product", d)))
                        go(vadd(s["A"], view(d, "za"), across("rw_a0", 8 * d)), d, "a+a0", "za read")

                def front_2():
                    for d in range(2):
                        s = st[d]
                        dve.wait_ge(*at(("tanh w", d)))
                        go(v.tensor_scalar(s["sw"], s["sw"], 0.5, 0.5, ALU.mult, ALU.add), d, "sw")
                        flat = [x.rearrange("p h t -> p (h t)") for x in (s["G"], b_restart[:, d].rearrange(
                            "p (h t) -> p h t", t=L), s["sw"])]
                        if d:
                            flat = [x[:, ::-1] for x in flat]
                        go(v.tensor_tensor_scan(flat[0], flat[1], flat[2], 0.0, ALU.mult, ALU.add), d, "G")
                        go(vsub(s["Pexc"], s["G"], s["sw"]), d, "G-sw")

                def front_3():
                    for d in range(2):
                        s, j = st[d], front_chunk(i)
                        dve.wait_ge(*at(("tanh a", d)))
                        go(v.tensor_scalar(s["A"], s["A"], 0.5, 0.5, ALU.mult, ALU.add), d, "A")
                        go(vmul(s["t"], s["A"], across("rw_ka", 0)), d)
                        go(vadd(s["t"], s["t"], ka1.unsqueeze(2).to_broadcast([P, 8, L])), d, settle=True)
                        go(vmul(s["t"], s["t"], chunk(b_k, next_seg, j, d)), d, settle=True)
                        go(vmul(s["A"], s["A"], chunk(b_kk, next_seg, j, d)), d)

                def front_4():
                    for d in range(2):
                        s = st[d]
                        dve.wait_ge(*at(("Pexc", d)))
                        go(vmul(s["k"], s["t"], s["Pinv"]), d, "k")
                        go(vmul(s["b"], s["A"], s["Pinv"]), d, "b")
                        go(v.tensor_copy(s["next_end"], s["Pinc"][:, :, (L - 1) * (1 - d)]), d)
                        end = s["next_end"].unsqueeze(2).to_broadcast([P, 8, L])
                        go(vmul(s["bend"], s["b"], end), d, "bend")
                        go(vmul(s["kend"], s["k"], end), d, "kend")

                def front_5():
                    for d in range(2):
                        s, j = st[d], front_chunk(i)
                        go(v.tensor_scalar(s["Pexc"], s["Pexc"], -1.0, None, ALU.mult), d, settle=True)
                        go(vmul(s["next_a"], s["Pexc"], chunk(b_kk, next_seg, j, d)), d, settle=True)
                        if next_seg == 1:
                            go(vmul(s["next_r"], s["Pinc"], chunk(b_r, 1, j, d, NC_)), d)

                def add_power(n_):
                    for d in range(2):
                        s = st[d]
                        dve.wait_ge(*at((n_ + " product", d)))
                        go(vadd(s["T"], s["T"], view(d, n_)), d, n_, n_ + " read")

                if main:
                    sid = stackid[:].unsqueeze(1).to_broadcast([P, 8, L])
                    for d in range(2):
                        s = st[d]
                        dve.wait_ge(*at(("X product", d)))
                        go(vmul(s["D"], view(d, "X"), mask(d, 2)), d, "D", "X read")
                        dve.wait_ge(*at(("Xt product", d)))
                        go(vmul(s["Dt"], view(d, "Xt"), mask(d, 4)), d, "Dt")
                    for d in range(2):
                        s = st[d]
                        go(vadd(s["T"], s["D"], sid), d, "T1")
                        go(vmul(s["Ot"], view(d, "Xt"), mask(d, 5)), d, "Ot", "Xt read")
                    for d in range(2):
                        s = st[d]
                        dve.wait_ge(*at(("AK product", d)))
                        go(vmul(s["AK"], view(d, "AK"), mask(d, 0)), d, "AK", "AK read")
                        if seg == 1:
                            dve.wait_ge(*at(("RB product", d)))
                            go(vmul(s["RB"], view(d, "RB"), mask(d, 1)), d, "RB", "RB read")
                            dve.wait_ge(*at(("RK product", d)))
                            go(vmul(s["RK"], view(d, "RK"), mask(d, 1)), d, "RK", "RK read")
                if front:
                    front_1()
                if main:
                    add_power("T2")
                if front:
                    front_2()
                if main:
                    add_power("T4")
                if front:
                    front_3()
                if main:
                    add_power("T8")
                if front:
                    front_4()
                if main:
                    for d in range(2):
                        s = st[d]
                        dve.wait_ge(*at(("N2 product", d)))
                        go(vadd(s["Q"], view(d, "N2"), sid), d, "Q1", "N2 read")
                    for d in range(2):
                        s = st[d]
                        dve.wait_ge(*at(("NQ product", d)))
                        go(vadd(s["Q"], s["Q"], view(d, "NQ")), d, "Q2", "NQ read")
                if front:
                    front_5()
                if main:
                    for d in range(2):
                        if seg == 1:
                            dve.wait_ge(*at(("Y product", d)))
                            dve.settle()
                            y = chunk(b_y, 1, main_chunk(i), d, NC_)
                            go(vadd(y, y, view(d, "Y")), d, "Y read")
                    for d in range(2):
                        s = st[d]
                        end = s["end"].unsqueeze(2).to_broadcast([P, 8, L])
                        dve.wait_ge(*at(("end", d)))
                        dve.wait_ge(*at(("S product", d)))
                        go(vmul(s["S"], s["S"], end), d)
                        go(vadd(s["S"], s["S"], view(d, "S")), d, "S", "S read")

            def looped(engine, body):
                if rounds == 1:
                    return body(0)
                with engine.e.Fori(0, rounds) as i:
                    engine.start_loop(i, key, rounds)
                    body(i)
                    engine.end_loop()

            block(lambda: looped(pe, pe_round), lambda: looped(act, act_round), lambda: looped(dve, dve_round))

        def rwkv_chunks():
            n = NC_ // L
            rwkv("first front", None, (0, lambda i: 0))
            rwkv("context", (0, lambda i: i), (0, lambda i: i + 1), n - 1)
            rwkv("last of context", (0, lambda i: n - 1), (1, lambda i: 0))
            rwkv("latents", (1, lambda i: i), (1, lambda i: i + 1), n - 1)
            rwkv("last of latents", (1, lambda i: n - 1), None)

        ka1 = region(34584, 8)

        def rwkv_start():
            def dve_():
                nc.vector.tensor_scalar(ka1, vec[:, VEC["rw_ka"]:VEC["rw_ka"] + 8], -1.0, 1.0, ALU.mult, ALU.add).then_inc(dve_done, dve.tick())
                nc.vector.memset(b_y, 0.0).then_inc(dve_done, dve.tick())
                for d in range(2):
                    nc.vector.memset(st[d]["S"], 0.0).then_inc(dve_done, dve.tick())

            block(None, None, dve_)

        def rwkv_out():
            asum, bonus, inv, sq = (region(24064 + 2048 * i, KD, NL) for i in range(4))

            def pe_():
                for f in range(KD):
                    for d in range(2):
                        r = slice(64 * d, 64 * d + 64)
                        mms(bank("ro", 2 * f + d)[:, 0:NL], [(b_a2[r, f * P:(f + 1) * P], b_al[r, lat])]).then_inc(pe_done, pe.tick(("ro", 2 * f + d)))
                for f in range(KD):
                    pe.wait_ge(*at(("rk sum operand", f)))
                    pe.wait_ge(*at(("y square", f)))
                    o = bank("ro", 16 + f)
                    nc.tensor.matmul(o[:, 0:NL], blockones[:], asum[:, f, :], start=True, stop=True)
                    nc.tensor.matmul(o[:, NL:T], blockones[:], sq[:, f, :], start=True, stop=True).then_inc(pe_done, pe.tick(("ro", 16 + f)))
                for f in range(KD):
                    mms(bank("ro", 24 + f)[:, 0:NL], [(b_g2[:, f * P:(f + 1) * P], b_gl)]).then_inc(pe_done, pe.tick(("ro", 24 + f)))

            def act_():
                for f in range(KD):
                    for d in range(2):
                        j = 2 * f + d
                        act.wait_ge(*at(("ro", j)))
                        nc.scalar.activation((asum, bonus)[d][:, f, :], ps[j % 8][:, 0:NL], ACT.Sigmoid,
                                                      bias=col("rw_a0", 8 * d + f)).then_inc(act_done, act.tick(("ro", "read", j)))
                for f in range(KD):
                    nc.scalar.activation(sq[:, f, :], b_y[:, f, :], ACT.Square).then_inc(act_done, act.tick(("y square", f)))
                for f in range(KD):
                    act.wait_ge(*at(("ro", 16 + f)))
                    nc.scalar.activation(inv[:, f, :], ps[f][:, NL:T], ACT.Sqrt, bias=epsc[:], scale=1.0 / RN).then_inc(act_done, act.tick(("y root", f)))

            def dve_():
                one = nc.vector.scalar_tensor_tensor
                dve.step(nc.vector.tensor_scalar(ka2, ka1, 2.0, None, ALU.mult))
                for f in range(KD):
                    a = asum[:, f, :]
                    dve.wait_ge(*at(("ro", "read", 2 * f + 1)))
                    dve.step(vadd(a, a, bonus[:, f, :]))
                    dve.step(nc.vector.tensor_scalar(a, a, col("rw_ka", f), ka2[:, f:f + 1], ALU.mult, ALU.add))
                    dve.step(vmul(a, a, b_k[:, f, lat]))
                    dve.step(one(a, a, col("rw_rk", f), b_r[:, f, :], ALU.mult, ALU.mult), ("rk sum operand", f))
                for f in range(KD):
                    dve.wait_ge(*at(("ro", 16 + f)))
                    dve.wait_ge(*at(("y root", f)))
                    dve.step(vmul(bonus[:, f, :], b_v[:, f, lat], ps[f][:, 0:NL]))
                    dve.step(nc.vector.reciprocal(inv[:, f, :], inv[:, f, :]), ("ro", "read", 16 + f))
                    dve.step(one(b_y[:, f, :], b_y[:, f, :], col("rw_ln", f), inv[:, f, :], ALU.mult, ALU.mult))
                    dve.step(vadd(b_y[:, f, :], b_y[:, f, :], bonus[:, f, :]))
                for f in range(KD):
                    dve.wait_ge(*at(("ro", 24 + f)))
                    vmul(b_y[:, f, :], b_y[:, f, :], ps[f][:, 0:NL]).then_inc(dve_done, dve.tick(("ro", "read", 24 + f)))

            block(pe_, act_, dve_, None, lambda: stream_weights(piece_at["low"]))

        ka2 = region(34592, 8)

        def write_out():
            o = region(0, 2, D)

            def pe_():
                for tt in range(2):
                    for half in range(2):
                        j = 2 * tt + half
                        for k in range(4):
                            m = nc.tensor.transpose(ps[j][:, k * P:(k + 1) * P],
                                                    h[:, 4 * half + k, NC_ + tt * P:NC_ + (tt + 1) * P], ident[:])
                        m.then_inc(pe_done, pe.tick(("turned", j)))

            def dve_():
                for j in range(4):
                    dve.wait_ge(*at(("turned", j)))
                    nc.vector.tensor_copy(o[:, j // 2, 512 * (j % 2):512 * (j % 2) + 512], ps[j]).then_inc(dve_done, dve.tick(("copied", j)))

            def sp_():
                for tt in range(2):
                    sp.wait_ge(*at(("copied", 2 * tt + 1)))
                    nc.sync.dma_start(out[0, tt * P:(tt + 1) * P, :], o[:, tt, :]).then_inc(output_written, 16)
                sp.wait_ge(output_written, 32)

            block(pe_, None, dve_, None, sp_)

        try:
            load_all()
            modulation(0)
            modulated("u", 0, 0, a_u, 26704)
            project0()
            mlstm_rows()
            mlstm()
            mlstm_out()
            ssd_rows()
            ssd_prepare()
            ssd()
            ssd_norm()
            a_y = region(9216, KD, T)
            out_projection(0, a_oz, 16, 0, a_y)
            residual("r", 1, a_y, 14336)
            moe(0, 0)
            modulation(1)
            modulated("u", 0, 0, b_u, 0)
            project_mla()
            norm_latent("nq", n_q, 3, NL, QR, "mla_qn")
            norm_latent("nkv", n_kv, 2, T, KVR, "mla_kvn")
            attention_heads()
            attention()
            project_rwkv()
            key_norms()
            rwkv_start()
            rwkv_chunks()
            rwkv_out()
            b_out = region(24064, KD, T)
            out_projection(1, b_mix, 12, NC_, b_out)
            residual("r", 1, b_out, 0, NC_)
            moe(1, NC_)
            write_out()
        except Stop:
            pass
    return steps.new


_INS = ['x', 'c', 'ctx', 'c_ctx', 'w_mod', 'b_mod', 'norm_g', 'ab_w_in', 'ab_w_out', 'ml_i_bias', 'ml_f_bias', 'ml_norm',
        'ssd_conv_w', 'ssd_conv_b', 'ssd_dt_bias', 'ssd_a_log', 'ssd_d', 'ssd_norm', 'cd_w_in', 'cd_w_out', 'mla_qn',
        'mla_w_uq', 'mla_kvn', 'mla_w_ukv', 'rw_mu', 'rw_w0', 'rw_w2', 'rw_a0', 'rw_a2', 'rw_g2', 'rw_kk', 'rw_ka', 'rw_rk',
        'rw_ln', 'router_w', 'router_bias', 'exp_w_gate', 'exp_w_up', 'exp_w_down', 'sh_w_gate', 'sh_w_up', 'sh_w_down']


def kernel(**inputs):
    import concourse.bacc as _bacc
    from concourse.bass_utils import run_bass_kernel_spmd as _run

    arrays = {f"in_{n}_dram": np.ascontiguousarray(inputs[n]) for n in _INS}
    arrays.update({f"in_{n}_dram": a for n, a in constants().items()})

    def build(known):
        nc = _bacc.Bacc("TRN2", target_bir_lowering=False, num_devices=1)
        args = {n[3:-5]: nc.dram_tensor(n, a.shape, mybir.dt.from_np(a.dtype), kind="ExternalInput").ap()
                for n, a in arrays.items()}
        out = nc.dram_tensor("out_0_dram", (1, NL, D), F32, kind="ExternalOutput").ap()
        return nc, program(nc, args, out, known)

    _, known = build({})
    nc, _ = build(known)
    r = _run(nc, [arrays], core_ids=[0])
    return r.results[0]["out_0_dram"]
```

```python
from contextlib import ExitStack

import numpy as np

import concourse.bass as bass
from concourse import mybir

F32 = mybir.dt.float32
F32R = mybir.dt.float32r
ALU = mybir.AluOpType
ACT = mybir.ActivationFunctionType
AX = mybir.AxisListType

P = 128
D = 1024
KD = D // P
NC_, NL = 256, 256
T = NC_ + NL
TT = T // P
EPS = 1e-6
MLH, MLQK, MLV = 4, 128, 256
SSH, SSP, SSN = 16, 64, 64
CONV = 5
AH, NOPE, ROPE, AV = 8, 64, 32, 64
HD = NOPE + ROPE
ASCALE = HD ** -0.5
QR, KVR = 384, 256
RH, RN = 16, 64
L = 64
NCH = T // L
NE, FF = 16, 512
LWC = float(np.exp(-0.5))
NSLOT = 3
SLOT = 4096
PARTS = 14520

C_Q, C_K, C_V, C_O, C_IG, C_FG, C_Z, C_X, C_DT = 0, 512, 1024, 2048, 3072, 3080, 3088, 4112, 5392
C_MQ, C_MKV, C_MKR, C_R, C_RK, C_RV, C_LOW = 0, 384, 640, 672, 1696, 2720, 3744

VEC_PARTS = [("norm_g", 64), ("b_mod", 96), ("c", 8), ("c_ctx", 8), ("ml_norm", 8), ("ssd_norm", 8),
             ("ssd_conv_w", 50), ("ssd_conv_b", 10), ("mla_qn", 3), ("mla_kvn", 2), ("rw_mu", 27),
             ("rw_w0", 16), ("rw_a0", 16), ("rw_kk", 8), ("rw_ka", 8), ("rw_rk", 8), ("rw_ln", 8)]
VEC, _n = {}, 0
for _name, _k in VEC_PARTS:
    VEC[_name] = _n
    _n += _k
NVEC = _n
NVT = -(-NVEC // P)

OFF = {0: {0: [(128, 512)], 1: [(256, 512)], 2: [(384, 512)], 3: []},
       1: {1: [(0, 128), (256, 512)], 0: [(256, 512)], 3: [(256, 384)], 2: []}}
SPAN = {0: [(0, [(0, 512)]), (1, [(128, 512)]), (2, [(256, 512)]), (3, [(384, 512)])],
        1: [(1, [(0, 512)]), (0, [(0, 128), (256, 512)]), (3, [(256, 512)]), (2, [(256, 384)])]}


def constants():
    i = np.arange(P)
    neg = np.float32(-1e30)
    c = {"ident": np.eye(P, dtype=np.float32)}
    c["blockones"] = (i[:, None] // 64 == i[None, :] // 64).astype(np.float32)
    fwd = np.where(i[:, None] <= i[None, :], np.float32(0), neg)
    bwd = np.where(i[:, None] >= i[None, :], np.float32(0), neg)
    c["maskneg"] = np.stack([np.tile(fwd, (1, 4)), np.tile(bwd, (1, 4))], 1).astype(np.float32)
    s, t = (i % 64)[:, None], np.arange(64)[None, :]
    same = (s // 16) == (t // 16)
    m = []
    for st, inc in (((s < t), (s <= t)), ((s > t), (s >= t))):
        tr = (s > t) if st[0, 1] else (s < t)
        m.append(np.stack([st, inc, st & same, st & ~same, tr & same, tr & ~same], 1))
    c["rmask"] = np.stack(m, 1).astype(np.float32)
    c["stackid"] = (s == t).astype(np.float32)
    one = np.ones((P, 2, 8, L), np.float32)
    one[:, 0, :, 0] = 0
    one[:, 1, :, L - 1] = 0
    c["restart"] = one.reshape(P, 2, 8 * L)
    rows = NL // 64
    ang_row = np.repeat(np.arange(rows, dtype=np.float32), 64)
    ang_col = np.tile(np.arange(64, dtype=np.float32), rows)
    inv = (10000.0 ** (-np.arange(8, dtype=np.float32) / 8)).astype(np.float32)
    ang = np.concatenate([ang_row[:, None] * inv, ang_col[:, None] * inv], -1).astype(np.float32).T
    cs, sn = np.cos(ang), np.sin(ang)
    c["rope"] = np.stack([np.concatenate([cs, cs]), np.concatenate([-sn, sn])], 1).astype(np.float32)
    return {k: np.ascontiguousarray(v) for k, v in c.items()}


class Steps:

    def __init__(self, known):
        self.known, self.new, self.block, self.loop = known, {}, 0, None

    def name(self, label):
        return label if label[0] == "let go" else (self.block, label)


class Turn:

    def __init__(self, first, per):
        self.first, self.per = first, per


class Engine:

    def __init__(self, name, sem, steps):
        self.name, self.sem, self.steps = name, sem, steps
        self.n, self.waited, self.loop, self.waited_in_loop = 0, {}, None, {}

    def tick(self, *labels):
        self.n += 1
        for label in map(self.steps.name, labels):
            self.steps.new[label] = [self.name, self.n, 0, 0]
            if self.loop is not None:
                self.loop[2].append(label)
        return 1

    @property
    def now(self):
        return self.n if self.loop is None else self.loop[0] * self.per + self.n

    def step(self, ins, *labels):
        ins.then_inc(self.sem, self.tick(*labels))
        self.e.wait_ge(self.sem, self.now)
        return ins

    def wait_ge(self, sem, value):
        if sem is None:
            return
        if isinstance(value, Turn):
            if self.waited_in_loop.get(id(sem), -1) < value.first:
                self.waited_in_loop[id(sem)] = value.first
                self.e.wait_ge(sem, self.loop[0] * value.per + value.first)
        elif not isinstance(value, int) or self.waited.get(id(sem), 0) < value:
            if self.loop is None and isinstance(value, int):
                self.waited[id(sem)] = value
            self.e.wait_ge(sem, value)

    def settle(self):
        self.e.sem_inc(self.settled, 1)

    def start_loop(self, i, key, rounds):
        self.loop = (i, key, [])
        self.steps.loop = key
        self.waited_in_loop = {}
        self.loop_n, self.rounds = self.n, rounds
        self.per = self.steps.known.get(("per", self.name, key), 1)

    def end_loop(self):
        i, key, labels = self.loop
        per = self.n - self.loop_n
        self.steps.new[("per", self.name, key)] = per
        for label in labels:
            self.steps.new[label][2:] = [per, (self.rounds, key)]
        self.n += per * (self.rounds - 1)
        self.loop = self.steps.loop = None


def program(nc, A, out, known):
    steps = Steps(known)
    with ExitStack() as ctx:
        def sb(name, shape):
            return ctx.enter_context(nc.sbuf_tensor(name, shape, F32))

        def semaphore(name):
            return ctx.enter_context(nc.semaphore(name))

        pe_done, act_done = semaphore("tensor_steps_done"), semaphore("scalar_steps_done")
        dve_done, pool_done = semaphore("vector_steps_done"), semaphore("gpsimd_steps_done")
        done = {"pe": pe_done, "act": act_done, "dve": dve_done, "pool": pool_done}
        pe, act, dve, pool = (Engine(n, s, steps) for n, s in done.items())
        sp = Engine("sp", None, steps)
        pe.settled = dve.settled = semaphore("waits_settled")

        def at(label, back=0):
            got = steps.known.get(steps.name(label))
            if got is None or (back and steps.loop is None):
                return None, 0
            name, value, per, rounds = got
            if per and steps.loop == rounds[1]:
                assert value >= back * per
                return done[name], Turn(value - back * per, per)
            return done[name], value + (per * (rounds[0] - 1) if per else 0)

        def latest(engine, now, before=()):
            found = [at((x, d)) for x, d in now] + [at((x, d), back=1) for x, d in before]
            found = [v for s, v in found if s is done[engine]]
            return (done[engine], max(found, key=lambda v: v.first if isinstance(v, Turn) else v)) if found else (None, 0)

        weights_landed = [semaphore(f"weights_landed_{i}") for i in range(NSLOT)]
        loads_landed = semaphore("loads_landed")
        output_written = semaphore("output_written")
        loads = [0]

        def load(eng, dst, src):
            eng.dma_start(dst, src).then_inc(loads_landed, 16)
            loads[0] += 16

        def loads_done(e):
            e.e.wait_ge(loads_landed, loads[0])

        ident, ones, blockones = sb("ident", [P, P]), sb("ones", [P, P]), sb("blockones", [P, P])
        stackid = sb("stackid", [P, 64])
        vec = sb("vec", [P, NVT * P])
        mod = sb("mod", [P, 48, 2])
        moda = sb("moda", [P, 4, 8, 2])
        silc = sb("silc", [P, 8, 2])
        epsc, zeros = sb("epsc", [P, 1]), sb("zeros", [P, 1])
        h = sb("h", [P, KD, T])
        scratch = sb("scratch", [P, T])
        gate_rows = scratch[0:NE, :]
        ring = sb("ring", [P, NSLOT, SLOT])
        with nc.sbuf_tensor("arena", [P, 35000], F32) as arena:
            pass
        ctx.enter_context(nc.sbuf_tensor("arena_for_experts", [P, PARTS], F32))
        parts = ctx.enter_context(nc.sbuf_tensor("parts", [P, 35000 - PARTS], F32R))
        ps = [ctx.enter_context(nc.psum_tensor(f"bank{i}", [P, 512], F32))[:, :] for i in range(8)]

        def region(at, *shape, rows=P):
            n = int(np.prod(shape))
            assert at + n <= 35000
            return shaped(arena[0:rows, at:at + n], shape)

        def parts_region(at, *shape):
            return shaped(parts[:, at:at + int(np.prod(shape))], shape)

        def shaped(flat, shape):
            if len(shape) == 1:
                return flat
            names = "abcd"[:len(shape)]
            return flat.rearrange(f"p ({' '.join(names)}) -> p {' '.join(names)}",
                                  **{x: y for x, y in zip(names, shape)})

        pieces, piece_at = [], {}

        def piece(key, w, r0, kt, c0, n):
            piece_at[key] = len(pieces)
            pieces.append((w[r0:r0 + kt * P, c0:c0 + n].rearrange("(k p) n -> p k n", p=P), kt, n))

        w_in = A["ab_w_in"][0]
        for m in range(12):
            piece(("mod", 0, m), A["w_mod"][0], 0, 8, m * 512, 512)
        piece("gates", w_in, 0, 8, C_IG, 16)
        piece(("x", 2), w_in, 0, 8, C_X + 1024, 288)
        for j in range(2):
            piece(("x", j), w_in, 0, 8, C_X + j * 512, 512)
        piece("q", w_in, 0, 8, C_Q, 512)
        piece("k", w_in, 0, 8, C_K, 512)
        for j in range(2):
            piece(("v", j), w_in, 0, 8, C_V + j * 512, 512)
        for j in range(2):
            piece(("o", j), w_in, 0, 8, C_O + j * 512, 512)
        for j in range(2):
            piece(("z", j), w_in, 0, 8, C_Z + j * 512, 512)
        for j in range(4):
            piece(("out", 0, j), A["ab_w_out"][0], 0, 16, j * 256, 256)

        def shared(l):
            piece(("sh", l, 0), A["sh_w_gate"][l], 0, 8, 0, 512)
            piece(("sh", l, 1), A["sh_w_up"][l], 0, 8, 0, 512)
            piece(("sh", l, 2), A["sh_w_down"][l], 0, 4, 0, 1024)
            piece_at[("experts", l)] = len(pieces)
            pieces.extend([None] * (3 * NE))

        shared(0)
        for m in range(12):
            piece(("mod", 1, m), A["w_mod"][1], 0, 8, m * 512, 512)
        w_in1 = A["cd_w_in"][0]
        piece("mq", w_in1, 0, 8, C_MQ, 384)
        piece("mkv", w_in1, 0, 8, C_MKV, 288)
        for n_, c_ in (("r", C_R), ("rk", C_RK), ("rv", C_RV)):
            for j in range(2):
                piece((n_, j), w_in1, 0, 8, c_ + j * 512, 512)
        piece("low", w_in1, 0, 8, C_LOW, 384)
        for j in range(4):
            piece(("out", 1, j), A["cd_w_out"][0], 0, 12, j * 256, 256)
        shared(1)

        def slot_view(i, kt, n):
            return ring[:, i % NSLOT, 0:kt * n].rearrange("p (k n) -> p k n", k=kt)

        def weights(key):
            i = piece_at[key]
            _, kt, n = pieces[i]
            pe.wait_ge(weights_landed[i % NSLOT], 16 * (i // NSLOT + 1))
            return slot_view(i, kt, n)

        issued = [0]

        def stream_weights(last):
            while issued[0] <= min(last + NSLOT, len(pieces) - 1) and pieces[issued[0]] is not None:
                i = issued[0]
                if i >= NSLOT:
                    sp.wait_ge(*at(("let go", i - NSLOT)))
                src, kt, n = pieces[i]
                nc.sync.dma_start(slot_view(i, kt, n), src).then_inc(weights_landed[i % NSLOT], 16)
                issued[0] += 1

        def let_go(key):
            return ("let go", piece_at[key])

        blocks = [0]

        def block(pe_=None, act_=None, dve_=None, pool_=None, sp_=None, last=None):
            blocks[0] += 1
            steps.block = blocks[0]
            with nc.Block(no_gpsimd_drain=True) as b:
                if pe_:
                    @b.tensor
                    def _(e):
                        pe.e = e
                        pe_()
                if act_:
                    @b.scalar
                    def _(e):
                        act.e = e
                        act_()
                if dve_:
                    @b.vector
                    def _(e):
                        dve.e = e
                        dve_()
                if pool_:
                    @b.gpsimd
                    def _(e):
                        pool.e = e
                        pool_()
                        e.wait_ge(pool.sem, pool.n)

                @b.sync
                def _(e):
                    sp.e = e
                    if sp_:
                        sp_()
                    if last is not None:
                        stream_weights(piece_at[last])
                    if loads[0]:
                        e.wait_ge(loads_landed, loads[0])

        def bank(tag, j):
            if j >= 8:
                pe.wait_ge(*at((tag, "read", j - 8)))
            return ps[j % 8]

        def whole(x):
            return x.bitcast(F32)

        def three(wh, wl, xh, xl):
            return [(wh, xh), (wh, xl), (wl, xh)]

        def mms(o, pairs, first=True, last=True):
            for n, (a, b) in enumerate(pairs):
                m = nc.tensor.matmul(o, a, b, start=first and n == 0, stop=last and n == len(pairs) - 1)
            return m

        def col(name, i):
            return vec[:, VEC[name] + i:VEC[name] + i + 1]


        def vmul(o, a, b):
            return nc.vector.tensor_tensor(o, a, b, ALU.mult)

        def vadd(o, a, b):
            return nc.vector.tensor_tensor(o, a, b, ALU.add)

        def vsub(o, a, b):
            return nc.vector.tensor_tensor(o, a, b, ALU.subtract)

        def halves(x):
            return x.rearrange("p n (s t) -> p n s t", s=2)

        def load_all():
            xin = region(0, TT, D)
            rows = region(4096, NVT, P)

            def sp_():
                for n_, t_ in (("ident", ident), ("blockones", blockones), ("stackid", stackid)):
                    load(nc.sync, t_[:], A[n_])
                for tt in range(2):
                    load(nc.sync, xin[:, tt, :], A["ctx"][0, tt * P:(tt + 1) * P, :])
                    load(nc.sync, xin[:, 2 + tt, :], A["x"][0, tt * P:(tt + 1) * P, :])
                flat = {"norm_g": "l a (r p) -> (l a r) p", "b_mod": "l (r p) -> (l r) p", "c": "l (r p) -> (l r) p",
                        "c_ctx": "(r p) -> r p", "ssd_conv_w": "l a (r p) -> (l a r) p", "rw_w0": "l a (r p) -> (l a r) p",
                        "rw_a0": "l a (r p) -> (l a r) p", "rw_rk": "l (r q) n -> (l r) (q n)"}
                for n_, k_ in VEC_PARTS:
                    pat = flat.get(n_, "l (r p) -> (l r) p")
                    kw = {"q": 2} if n_ == "rw_rk" else {"p": P}
                    src = A[n_].rearrange(pat, **kw)
                    a0 = VEC[n_]
                    at = 0
                    while at < k_:
                        r = (a0 + at) % P
                        m = min(k_ - at, P - r)
                        load(nc.sync, rows[r:r + m, (a0 + at) // P, :], src[at:at + m, :])
                        at += m

            def pool_():
                nc.gpsimd.memset(ones[:], 1.0).then_inc(pool_done, pool.tick("ones"))
                nc.gpsimd.memset(epsc[:], EPS).then_inc(pool_done, pool.tick("epsc"))

            def pe_():
                pe.wait_ge(loads_landed, loads[0])
                j = 0
                for t in range(NVT):
                    n = min(P, NVEC - t * P)
                    o = bank("load", j)
                    nc.tensor.transpose(o[:, 0:n], rows[0:n, t, :], ident[0:n, 0:n]).then_inc(pe_done, pe.tick(("vecT", t)))
                    j += 1
                for k in range(KD):
                    o = bank("load", j)
                    for tt in range(TT):
                        m = nc.tensor.transpose(o[:, tt * P:(tt + 1) * P], xin[:, tt, k * P:(k + 1) * P], ident[:])
                    m.then_inc(pe_done, pe.tick(("hT", k)))
                    j += 1

            def act_():
                for k in range(0, KD, 2):
                    act.wait_ge(*at(("hT", k)))
                    nc.scalar.activation(h[:, k, :], ps[(NVT + k) % 8][:], ACT.Copy).then_inc(act_done, act.tick(("load", "read", NVT + k)))
                act.wait_ge(*at(("load", "read", NVT - 1)))
                nc.scalar.activation(silc[:, :, 1], vec[:, VEC["c"]:VEC["c"] + 8], ACT.Silu).then_inc(act_done, act.tick())
                nc.scalar.activation(silc[:, :, 0], vec[:, VEC["c_ctx"]:VEC["c_ctx"] + 8], ACT.Silu).then_inc(act_done, act.tick())

            def dve_():
                for t in range(NVT):
                    dve.wait_ge(*at(("vecT", t)))
                    n = min(P, NVEC - t * P)
                    nc.vector.tensor_copy(vec[:, t * P:t * P + n], ps[t][:, 0:n]).then_inc(dve_done, dve.tick(("load", "read", t)))
                for k in range(1, KD, 2):
                    dve.wait_ge(*at(("hT", k)))
                    nc.vector.tensor_copy(h[:, k, :], ps[(NVT + k) % 8][:]).then_inc(dve_done, dve.tick(("load", "read", NVT + k)))

            n_loads = 3 + 4 + sum(1 for _ in load_parts())
            loads[0] = 16 * n_loads

            def sp_first():
                loads[0] = 0
                sp_()
                assert loads[0] == 16 * n_loads

            block(pe_, act_, dve_, pool_, sp_first)

        def load_parts():
            for n_, k_ in VEC_PARTS:
                at = 0
                while at < k_:
                    r = (VEC[n_] + at) % P
                    at += min(k_ - at, P - r)
                    yield n_

        def modulation(l):
            rows = region(30000, 4, 512, rows=2)

            def pe_():
                for m in range(13):
                    if m < 12:
                        w = weights(("mod", l, m))
                        pe.wait_ge(*at(("row", m - 4)))
                        mms(ps[1 + m % 4][0:2, :], [(silc[:, k, :], w[:, k, :]) for k in range(8)]).then_inc(pe_done, pe.tick(("row sums", m), let_go(("mod", l, m))))
                    if m > 0:
                        pe.wait_ge(*at(("row", m - 1)))
                        for f in range(4):
                            c0 = (4 * (m - 1) + f) * 2
                            x = nc.tensor.transpose(ps[0][:, c0:c0 + 2], rows[:, (m - 1) % 4, f * P:(f + 1) * P], ident[0:2, 0:2])
                        x.then_inc(pe_done, pe.tick(("turned", m - 1)))

            def act_():
                for m in range(12):
                    act.wait_ge(*at(("row sums", m)))
                    if m >= 4:
                        act.wait_ge(*at(("turned", m - 4)))
                    nc.scalar.activation(rows[:, m % 4], ps[1 + m % 4][0:2, :], ACT.Copy).then_inc(act_done, act.tick(("row", m)))

            def dve_():
                dve.wait_ge(*at(("turned", 11)))
                b0 = VEC["b_mod"] + 48 * l
                bias = vec[:, b0:b0 + 48].unsqueeze(2).to_broadcast([P, 48, 2])
                dve.step(vadd(mod[:], ps[0][:, 0:96].rearrange("p (m s) -> p m s", s=2), bias))
                g = [vec[:, VEC["norm_g"] + (4 * l + a) * 8:][:, 0:8].unsqueeze(2).to_broadcast([P, 8, 2])
                     for a in range(4)]
                one = nc.vector.scalar_tensor_tensor
                one(moda[:, 0], mod[:, 8:16], 1.0, g[0], ALU.add, ALU.mult).then_inc(dve_done, dve.tick())
                one(moda[:, 2], mod[:, 32:40], 1.0, g[2], ALU.add, ALU.mult).then_inc(dve_done, dve.tick())
                vmul(moda[:, 1], mod[:, 16:24], g[1]).then_inc(dve_done, dve.tick())
                vmul(moda[:, 3], mod[:, 40:48], g[3]).then_inc(dve_done, dve.tick())

            block(pe_, act_, dve_, last=("mod", l, 11))

        def rms_block(tag, src, n, cols, dim, use, sq_at, pool_=None):
            sq = region(sq_at, 2, T)
            inv = region(sq_at + 2 * T, T)[:, 0:cols]

            def pe_():
                for k in range(n):
                    pe.wait_ge(*at((tag, "square", k)))
                    nc.tensor.matmul(ps[0][:, 0:cols], ones[:], sq[:, k % 2, 0:cols],
                                             start=k == 0, stop=k == n - 1).then_inc(pe_done, pe.tick((tag, "summed", k)))

            def act_():
                for k in range(n):
                    if k >= 2:
                        act.wait_ge(*at((tag, "summed", k - 2)))
                    nc.scalar.activation(sq[:, k % 2, 0:cols], src(k), ACT.Square).then_inc(act_done, act.tick((tag, "square", k)))
                act.wait_ge(*at((tag, "summed", n - 1)))
                nc.scalar.activation(inv, ps[0][:, 0:cols], ACT.Sqrt, bias=epsc[:], scale=1.0 / dim).then_inc(act_done, act.tick((tag, "root")))
                if use[1]:
                    use[1](inv)

            def dve_():
                dve.wait_ge(*at((tag, "root")))
                dve.step(nc.vector.reciprocal(inv, inv), (tag, "inv"))
                use[0](inv)

            block(pe_, act_, dve_, pool_)

        def segments(c0):
            return [(s, slice(s * 256, s * 256 + 256), slice(s * 256 - c0, s * 256 + 256 - c0))
                    for s in range(2) if s * 256 >= c0]

        def modulated(tag, a, shift, dst, sq_at, c0=0):
            def dve_(inv):
                for k in range(KD):
                    for s, c, ci in segments(c0):
                        nc.vector.scalar_tensor_tensor(dst[:, k, c], h[:, k, c], moda[:, a, k, s:s + 1],
                                                                inv[:, ci], ALU.mult, ALU.mult).then_inc(dve_done, dve.tick((tag, "scaled", k, s)))

            def act_(inv):
                for k in range(KD):
                    for s, c, _ in segments(c0):
                        act.wait_ge(*at((tag, "scaled", k, s)))
                        nc.scalar.activation(dst[:, k, c], dst[:, k, c], ACT.Identity,
                                                      bias=mod[:, shift + k, s:s + 1]).then_inc(act_done, act.tick())

            rms_block(tag, lambda k: h[:, k, c0:T], KD, T - c0, D, (dve_, act_), sq_at)

        def residual(tag, a, y, sq_at, c0=0):
            def dve_(inv):
                for k in range(KD):
                    for s, c, ci in segments(c0):
                        nc.vector.scalar_tensor_tensor(y[:, k, c], y[:, k, c], moda[:, a, k, s:s + 1],
                                                       inv[:, ci], ALU.mult, ALU.mult).then_inc(dve_done, dve.tick((tag, "scaled", k, s)))

            def pool_():
                for k in range(KD):
                    for s, c, _ in segments(c0):
                        pool.wait_ge(*at((tag, "scaled", k, s)))
                        nc.gpsimd.tensor_tensor(h[:, k, c], h[:, k, c], y[:, k, c], ALU.add).then_inc(pool_done, pool.tick())

            rms_block(tag, lambda k: y[:, k, c0:T], KD, T - c0, D, (dve_, None), sq_at, pool_)

        a_mask = region(0, 2, 512)
        a_oz = region(1024, 16, T)
        a_q, a_k = region(9216, 4, T), region(11264, 4, T)
        a_v = region(13312, TT, D)
        a_xbc = region(17408, 10, 2, 260)
        a_u = region(22608, KD, T)
        a_e = region(26704, 2, 4, T)
        a_gates = region(30800, 3, T, rows=32)
        a_cb = region(9216, 2, 4, T)
        a_rows = region(30800, 7, T, rows=32)
        a_cols = region(34400, 600)
        a_bias = a_cols[0:32, 0:8]

        def halves_of(x):
            return x.rearrange("p (s t) -> p s t", s=2)

        def xs(f, c0, c1):
            if c1 - c0 == T:
                return a_xbc[:, f, :, 2:258]
            s0 = c0 // 256
            return a_xbc[:, f, s0, 2 + c0 - 256 * s0:2 + c1 - 256 * s0]

        def project_gates():
            def pe_():
                j = 0
                w = weights("gates")
                for i in range(2):
                    mms(bank("pg", j)[0:8, :], [(w[:, k, 8 * i:8 * i + 8], a_u[:, k, :]) for k in range(8)]).then_inc(pe_done, pe.tick(("pg", j), *((let_go("gates"),) if i == 1 else ())))
                    j += 1
                for i in (2, 0, 1):
                    w = weights(("x", i))
                    if i == 2:
                        mms(bank("pg", j)[0:32, :], [(w[:, k, 256:288], a_u[:, k, :]) for k in range(8)]).then_inc(pe_done, pe.tick(("pg", j)))
                        j += 1
                    last = 3 if i < 2 else 1
                    for f in range(last + 1):
                        mms(bank("pg", j), [(w[:, k, f * P:(f + 1) * P], a_u[:, k, :]) for k in range(8)]).then_inc(pe_done, pe.tick(("pg", j), *((let_go(("x", i)),) if f == last else ())))
                        j += 1

            def dve_():
                for j in range(13):
                    dve.wait_ge(*at(("pg", j)))
                    if j < 2:
                        i = nc.vector.tensor_copy(a_gates[0:8, j, :], ps[j][0:8, :])
                    elif j == 2:
                        i = nc.vector.tensor_copy(a_gates[:, 2, :], ps[j][0:32, :])
                    else:
                        f = j + 5 if j < 5 else j - 5
                        i = nc.vector.tensor_copy(xs(f, 0, T), halves_of(ps[j % 8]))
                    i.then_inc(dve_done, dve.tick(("pg", "read", j)))

            def pool_():
                nc.gpsimd.memset(a_xbc[:, :, :, 0:2], 0.0).then_inc(pool_done, pool.tick())
                nc.gpsimd.memset(a_xbc[:, :, :, 258:260], 0.0).then_inc(pool_done, pool.tick())

            def sp_():
                load(nc.sync, a_mask, A["maskneg"])
                for i, (n_, m) in enumerate((("ml_i_bias", 8), ("ml_f_bias", 8), ("ssd_dt_bias", 32), ("ssd_a_log", 32))):
                    load(nc.sync, a_bias[0:m, i:i + 1], A[n_].rearrange("l a (h o) -> (l a h) o", o=1))
                with nc.allow_non_contiguous_dma(reason="a few words"):
                    for hf in range(2):
                        load(nc.sync, a_cols[64 * hf:64 * hf + 64, 16:24],
                             A["ssd_d"][0:1, hf::2].to_broadcast([64, 8]))

            block(pe_, None, dve_, pool_, sp_, last=("x", 1))

        def soft(x, tmp, out, sign, tag):
            v = nc.vector
            dve.step(v.scalar_tensor_tensor(tmp[0], x, -1.0, x, ALU.mult, ALU.max), (tag, "abs"))
            dve.wait_ge(*at((tag, "exp")))
            dve.step(v.tensor_scalar(tmp[2], tmp[1], 1.0, None, ALU.add), (tag, "1+e"))
            dve.step(v.tensor_scalar(tmp[0], tmp[2], -1.0, 1e-30, ALU.add, ALU.max))
            dve.step(v.reciprocal(tmp[3], tmp[0]))
            dve.step(vmul(tmp[3], tmp[3], tmp[1]))
            dve.wait_ge(*at((tag, "ln")))
            dve.step(vmul(tmp[3], tmp[3], tmp[5]))
            dve.step(v.scalar_tensor_tensor(tmp[0], tmp[0], 1e-30, tmp[1], ALU.is_equal, ALU.mult))
            dve.step(vadd(tmp[3], tmp[3], tmp[0]))
            dve.step(v.tensor_scalar(tmp[0], x, 0.0, None, ALU.max if sign > 0 else ALU.min))
            dve.step(nc.vector.tensor_tensor(out, tmp[0], tmp[3], ALU.add if sign > 0 else ALU.subtract))

        def soft_act(tmp, tag):
            act.wait_ge(*at((tag, "abs")))
            nc.scalar.activation(tmp[1], tmp[0], ACT.Exp, scale=-1.0).then_inc(act_done, act.tick((tag, "exp")))
            act.wait_ge(*at((tag, "1+e")))
            nc.scalar.activation(tmp[5], tmp[2], ACT.Ln).then_inc(act_done, act.tick((tag, "ln")))

        def scans(src, dst_f, dst_b, op, first):
            n = src[0].shape[0]
            unit = (ones if op == ALU.add else zeros)[0:n, 0:1]
            how = (ALU.mult, ALU.add) if op == ALU.add else (ALU.add, ALU.max)
            dve.step(nc.vector.tensor_tensor_scan(dst_f, unit.to_broadcast([n, T]), src[0], first, *how))
            dve.step(nc.vector.tensor_tensor_scan(dst_b[:, 0:NC_][:, ::-1], unit.to_broadcast([n, NC_]),
                                                  src[1][:, 0:NC_][:, ::-1], first, *how))
            dve.step(nc.vector.tensor_tensor_scan(dst_b[:, NC_:T][:, ::-1], unit.to_broadcast([n, NL]),
                                                  src[1][:, NC_:T][:, ::-1], dst_b[:, 0:1], *how))

        a_negm = a_rows[0:8, 3:5]
        a_em = a_rows[0:8, 5:7]
        a_brow = a_rows[:, 0:3:2]
        c_g = a_cols[:, 64:128].rearrange("p (d t r) -> p d t r", d=2, t=TT)
        c_b = a_cols[:, 128:384].rearrange("p (d t r) -> p d t r", d=2, t=TT)
        c_dt = a_cols[:, 384:512].rearrange("p (t r) -> p t r", t=TT)

        def project_rest():
            slots = a_e.rearrange("p a b c -> p (a b) c")
            tmp = [slots[0:8, i, :] for i in range(8)]
            tmp32 = [slots[0:32, i, :] for i in range(8)]
            x, lf, bf, bb, gf, gb = a_gates[0:8, 0, :], tmp[4], tmp[5], tmp[6], tmp[7], a_gates[0:8, 1, :]
            raw, dt, la, dt_rows = a_gates[:, 2, :], tmp32[4], tmp32[5], tmp32[6]
            columns = ps[7]

            def mlstm_rows():
                dve.step(nc.vector.memset(zeros[:], 0.0))
                dve.step(nc.vector.tensor_scalar(x, x, a_bias[0:8, 0:1], None, ALU.add))
                f = a_gates[0:8, 1, :]
                dve.step(nc.vector.tensor_scalar(f, f, a_bias[0:8, 1:2], None, ALU.add))
                soft(f, tmp, lf, -1, "lf")
                scans((lf, lf), bf, bb, ALU.add, 0.0)
                dve.step(vsub(gf, x, bf))
                dve.step(vsub(gb, x, bb), "g rows")
                mf, mb = a_negm[:, 0], a_negm[:, 1]
                scans((gf, gb), mf, mb, ALU.max, 0.0)
                for b, m, e in ((bf, mf, 0), (bb, mb, 1)):
                    dve.step(vadd(tmp[0], b, m))
                    dve.step(nc.vector.tensor_scalar(a_em[:, e], tmp[0], -87.0, None, ALU.max), ("m", e))
                dve.step(nc.vector.tensor_scalar(a_negm, a_negm, -1.0, None, ALU.mult))

            def ssd_rows():
                dve.step(nc.vector.tensor_scalar(raw, raw, a_bias[:, 2:3], None, ALU.add))
                soft(raw, tmp32, dt, 1, "dt")
                dve.wait_ge(*at("A"))
                dve.step(nc.vector.tensor_scalar(la, dt, a_bias[:, 4:5], -1.0, ALU.mult, ALU.mult))
                scans((la, la), a_brow[:, 0], a_brow[:, 1], ALU.add, 0.0)
                dve.step(nc.vector.tensor_copy(dt_rows, dt), "B rows")

            def convolution():
                for f in range(10):
                    o = halves_of(slots[:, f % 2, :])
                    if f >= 2:
                        dve.wait_ge(*at(("conv silu", f - 2)))
                    for t in range(CONV):
                        w = col("ssd_conv_w", 10 * t + f)
                        if t == 0:
                            dve.step(nc.vector.tensor_scalar(o, a_xbc[:, f, :, t:t + 256], w, col("ssd_conv_b", f), ALU.mult, ALU.add))
                        else:
                            dve.step(nc.vector.scalar_tensor_tensor(o, a_xbc[:, f, :, t:t + 256], w, o, ALU.mult, ALU.add), ("conv", f, t))

            def dve_():
                mlstm_rows()
                ssd_rows()
                convolution()
                dve.wait_ge(*at("columns"))
                nc.vector.tensor_copy(a_cols[:, 64:128], columns[:, 0:64]).then_inc(dve_done, dve.tick())
                nc.vector.tensor_scalar(a_cols[:, 128:384], columns[:, 64:320], -1.0, None, ALU.mult).then_inc(dve_done, dve.tick())
                nc.vector.tensor_copy(a_cols[:, 384:512], columns[:, 320:448]).then_inc(dve_done, dve.tick())

            def turn_rows():
                pe.wait_ge(*at("g rows"))
                pe.wait_ge(*at("B rows"))
                for d, g in enumerate((gf, gb)):
                    for tt in range(TT):
                        c0 = (d * TT + tt) * 8
                        nc.tensor.transpose(columns[:, c0:c0 + 8], g[:, tt * P:(tt + 1) * P], ident[0:8, 0:8])
                for i, r in enumerate((a_brow[:, 0], a_brow[:, 1], dt_rows)):
                    for tt in range(TT):
                        c0 = 64 + (i * TT + tt) * 32
                        m = nc.tensor.transpose(columns[:, c0:c0 + 32], r[:, tt * P:(tt + 1) * P], ident[0:32, 0:32])
                m.then_inc(pe_done, pe.tick("columns"))

            jobs = [(key, f) for key in ("q", "k", ("v", 0), ("v", 1), ("o", 0), ("o", 1), ("z", 0), ("z", 1)) for f in range(4)]

            def pe_():
                for j, (key, f) in enumerate(jobs):
                    w = weights(key)
                    if j >= 7:
                        pe.wait_ge(*at(("pr", "read", j - 7)))
                    c = slice(f * P, (f + 1) * P)
                    pairs = [(a_u[:, k, c], w[:, k, :]) if key[0] == "v" else (w[:, k, c], a_u[:, k, :]) for k in range(8)]
                    mms(ps[j % 7], pairs).then_inc(pe_done, pe.tick(("pr", j), *((let_go(key),) if f == 3 else ())))
                    if j == 9:
                        turn_rows()

            def act_():
                soft_act(tmp, "lf")
                nc.scalar.activation(a_bias[:, 4:5], a_bias[:, 3:4], ACT.Exp).then_inc(act_done, act.tick("A"))
                for e in range(2):
                    act.wait_ge(*at(("m", e)))
                    nc.scalar.activation(a_em[:, e], a_em[:, e], ACT.Exp, scale=-1.0).then_inc(act_done, act.tick())
                soft_act(tmp32, "dt")
                for j, (key, f) in enumerate(jobs):
                    act.wait_ge(*at(("pr", j)))
                    o = ps[j % 7]
                    if key == "q":
                        m = nc.scalar.activation(a_q[:, f, :], o, ACT.Copy, scale=MLQK ** -0.5)
                    elif key == "k":
                        m = nc.scalar.activation(a_k[:, f, :], o, ACT.Copy)
                    elif key[0] == "v":
                        m = nc.scalar.activation(a_v[:, f, key[1] * 512:(key[1] + 1) * 512], o, ACT.Copy)
                    else:
                        m = nc.scalar.activation(a_oz[:, 8 * (key[0] == "z") + 4 * key[1] + f, :], o,
                                                 ACT.Sigmoid if key[0] == "o" else ACT.Silu)
                    m.then_inc(act_done, act.tick(("pr", "read", j)))
                    if 8 <= j < 18:
                        t = j - 8
                        act.wait_ge(*at(("conv", t, CONV - 1)))
                        nc.scalar.activation(xs(t, 0, T), halves_of(slots[:, t % 2, :]), ACT.Silu).then_inc(act_done, act.tick(("conv silu", t)))

            block(pe_, act_, dve_, last=("z", 1))

        def exponent_tiles(it, d, n_rows, row, rows_d, off_bank, diag_bank):
            sel = ident[0:n_rows, row:row + 1].to_broadcast([n_rows, P])
            nc.tensor.matmul(off_bank, sel, rows_d, start=True, stop=True)
            nc.tensor.matmul(diag_bank, sel, rows_d, start=True, stop=False)
            nc.tensor.matmul(diag_bank, ident[:], a_mask[:, d], start=False, stop=True).then_inc(pe_done, pe.tick(("expo", it)))

        def exponentials(it, d, e, off_bank, diag_bank, bias):
            act.wait_ge(*at(("expo", it)))
            for s, _ in SPAN[d]:
                c = slice(s * P, s * P + P)
                m = nc.scalar.activation(e[:, s, c], diag_bank[:, c], ACT.Exp, bias=bias(s))
                for c0, c1 in OFF[d][s]:
                    m.then_inc(act_done, act.tick())
                    m = nc.scalar.activation(e[:, s, c0:c1], off_bank[:, c0:c1], ACT.Exp, bias=bias(s))
                m.then_inc(act_done, act.tick(("E", it, s)))

        def mlstm():
            qk = [ps[0], ps[1], ps[2], ps[2]]
            inv, tmp = scratch[:], region(31312, T)

            def qk_cols(s, c0, c1):
                return qk[s][:, c0:c1] if s < 2 else qk[s][:, c0 - 256 + 256 * (s - 2):c1 - 256 + 256 * (s - 2)]

            def prepare(it):
                hd, d = divmod(it, 2)
                if d == 0:
                    for s in range(TT):
                        pe.wait_ge(*at(("sD", it - 1, s)))
                    for s in range(TT):
                        c0 = 0 if s < 2 else 256
                        m = nc.tensor.matmul(qk_cols(s, c0, T), a_k[:, hd, s * P:(s + 1) * P], a_q[:, hd, c0:T],
                                             start=True, stop=True)
                    m.then_inc(pe_done, pe.tick(("qk", hd)))
                pe.wait_ge(*at(("em read", it - 1)))
                for s in range(TT):
                    pe.wait_ge(*at(("E", it - 1, s)))
                exponent_tiles(it, d, 8, d * MLH + hd, a_negm[:, d], ps[3], ps[4])

            def pe_():
                for it in range(2 * MLH):
                    hd, d = divmod(it, 2)
                    prepare(it)
                    pe.wait_ge(*at(("h", it - 1)))
                    for n, (s, spans) in enumerate(SPAN[d]):
                        pe.wait_ge(*at(("sD", it, s)))
                        for half in range(3):
                            w = ones[:] if half == 2 else a_v[:, s, hd * MLV + half * P:hd * MLV + half * P + P]
                            for i, (c0, c1) in enumerate(spans):
                                m = nc.tensor.matmul(ps[5 + half][:, c0:c1], w, a_e[:, it % 2, s, c0:c1], start=n == 0,
                                                     stop=n == TT - 1 and i == len(spans) - 1)
                    m.then_inc(pe_done, pe.tick(("num", it)))
                    for s in range(TT):
                        pe.wait_ge(*at(("E", it, s)))
                    row = d * MLH + hd
                    nc.tensor.matmul(ps[3], ident[0:8, row:row + 1].to_broadcast([8, P]), a_em[:, d],
                                             start=True, stop=True).then_inc(pe_done, pe.tick(("em", it)))

            def act_():
                for it in range(2 * MLH):
                    hd, d = divmod(it, 2)
                    if it >= 2:
                        act.wait_ge(*at(("num", it - 2)))
                    exponentials(it, d, a_e[:, it % 2], ps[3], ps[4],
                                 lambda s: c_g[:, d, s, d * MLH + hd:d * MLH + hd + 1])

            def dve_():
                for it in range(2 * MLH):
                    hd, d = divmod(it, 2)
                    dve.wait_ge(*at(("qk", hd)))
                    for s, spans in SPAN[d]:
                        dve.wait_ge(*at(("E", it, s)))
                        for c0, c1 in spans:
                            e = a_e[:, it % 2, s, c0:c1]
                            m = vmul(e, e, qk_cols(s, c0, c1))
                            m.then_inc(dve_done, dve.tick(("sD", it, s)))
                    dve.wait_ge(*at(("num", it)))
                    dve.step(nc.vector.tensor_scalar(inv, ps[7], -1.0, None, ALU.mult))
                    dve.step(nc.vector.tensor_tensor(inv, inv, ps[7], ALU.max))
                    dve.wait_ge(*at(("em", it)))
                    dve.step(nc.vector.tensor_tensor(inv, inv, ps[3], ALU.max), ("em read", it))
                    dve.step(nc.vector.reciprocal(inv, inv))
                    for half in range(2):
                        o = a_u[:, 2 * hd + half, :]
                        if d == 0:
                            vmul(o, ps[5 + half], inv).then_inc(dve_done, dve.tick(("h", it)))
                        else:
                            dve.step(vmul(tmp, ps[5 + half], inv), ("h", it))
                            dve.step(vadd(o, o, tmp))

            block(pe_, act_, dve_)

        def mlstm_out():
            sq = a_e.rearrange("p a b c -> p (a b) c")
            inv = a_q

            def act_():
                for k in range(8):
                    nc.scalar.activation(sq[:, k, :], a_u[:, k, :], ACT.Square).then_inc(act_done, act.tick(("hsq", k)))
                for hd in range(MLH):
                    act.wait_ge(*at(("hsum", hd)))
                    nc.scalar.activation(inv[:, hd, :], ps[hd], ACT.Sqrt, bias=epsc[:], scale=1.0 / MLV).then_inc(act_done, act.tick(("hroot", hd)))

            def pe_():
                for hd in range(MLH):
                    pe.wait_ge(*at(("hsq", 2 * hd + 1)))
                    mms(ps[hd], [(ones[:], sq[:, 2 * hd + i, :]) for i in range(2)]).then_inc(pe_done, pe.tick(("hsum", hd)))

            def dve_():
                for hd in range(MLH):
                    dve.wait_ge(*at(("hroot", hd)))
                    dve.step(nc.vector.reciprocal(inv[:, hd, :], inv[:, hd, :]))
                    for k in (2 * hd, 2 * hd + 1):
                        dve.step(nc.vector.scalar_tensor_tensor(a_u[:, k, :], a_u[:, k, :], col("ml_norm", k),
                                                                inv[:, hd, :], ALU.mult, ALU.mult))
                        vmul(a_oz[:, k, :], a_oz[:, k, :], a_u[:, k, :]).then_inc(dve_done, dve.tick())

            block(pe_, act_, dve_)

        a_xt = region(22608, TT, D)

        def ssd_prepare():
            def pe_():
                j = 0
                for tt in range(TT):
                    for half in range(2):
                        o = bank("xt", j)
                        for i in range(4):
                            m = nc.tensor.transpose(o[:, i * P:(i + 1) * P], xs(4 * half + i, tt * P, (tt + 1) * P),
                                                    ident[:])
                        m.then_inc(pe_done, pe.tick(("xt", j)))
                        j += 1
                for g in range(2):
                    r = slice(64 * g, 64 * g + 64)
                    for s in range(TT):
                        c0 = 0 if s < 2 else 256
                        o = bank("xt", j)[:, c0:T]
                        mms(halves_of(o) if c0 == 0 else o, [(xs(8, s * P, (s + 1) * P)[r], xs(9, c0, T)[r])]).then_inc(pe_done, pe.tick(("xt", j)))
                        j += 1

            def read(e, copy, j):
                e.wait_ge(*at(("xt", j)))
                if j < 8:
                    tt, half = divmod(j, 2)
                    i = copy(a_xt[:, tt, 512 * half:512 * half + 512], ps[j % 8])
                else:
                    g, s = divmod(j - 8, 4)
                    c0 = 0 if s < 2 else 256
                    i = copy(a_cb[:, g, s, c0:T], ps[j % 8][:, c0:T])
                i.then_inc(e.sem, e.tick(("xt", "read", j)))

            def act_():
                for j in range(0, 16, 2):
                    read(act, lambda o, i: nc.scalar.activation(o, i, ACT.Copy), j)

            def dve_():
                for j in range(1, 16, 2):
                    read(dve, nc.vector.tensor_copy, j)

            block(pe_, act_, dve_)

        def ssd():
            n = 2 * SSH
            weights_of = [a_e[:, 0], a_e[:, 1], region(14336, 4, T)]

            def head(it):
                hd, d = divmod(it, 2)
                return hd, d, hd // 2, hd % 2

            def pe_():
                def expo(it):
                    hd, d, _, _ = head(it)
                    if it >= 4:
                        for s in range(TT):
                            pe.wait_ge(*at(("E", it - 4, s)))
                        pe.wait_ge(*at(("masked", it - 4)))
                    row = d * SSH + hd
                    nc.tensor.matmul(ps[it % 4], ident[0:32, row:row + 1].to_broadcast([32, P]), a_brow[:, d],
                                     start=True, stop=True).then_inc(pe_done, pe.tick(("expo", it)))

                expo(0)
                expo(1)
                for it in range(n):
                    hd, d, p, hf = head(it)
                    if it + 2 < n:
                        expo(it + 2)
                    if hf == 0 and d == 0 and p >= 2:
                        pe.wait_ge(*at(("y read", p - 2)))
                    o = ps[4 + p % 2][64 * hf:64 * hf + 64]
                    for k, (s, spans) in enumerate(SPAN[d]):
                        pe.wait_ge(*at(("W", it, s)))
                        for i, (c0, c1) in enumerate(spans):
                            m = nc.tensor.matmul(o[:, c0:c1], a_xt[:, s, hd * SSP:(hd + 1) * SSP], weights_of[it % 3][:, s, c0:c1],
                                                 start=d == 0 and k == 0,
                                                 stop=d == 1 and k == TT - 1 and i == len(spans) - 1)
                    m.then_inc(pe_done, pe.tick(("y", it)))

            def act_():
                for it in range(n):
                    hd, d, _, _ = head(it)
                    if it >= 3:
                        act.wait_ge(*at(("y", it - 3)))
                    act.wait_ge(*at(("masked", it)))
                    exponentials(it, d, weights_of[it % 3], ps[it % 4], masked[:, it % 2],
                                 lambda s: c_b[:, d, s, d * SSH + hd:d * SSH + hd + 1])

            masked = region(13312, 2, T)

            def dve_():
                def mask(it):
                    dve.wait_ge(*at(("expo", it)))
                    if it >= 2:
                        for s in range(TT):
                            dve.wait_ge(*at(("E", it - 2, s)))
                    vadd(masked[:, it % 2], ps[it % 4], a_mask[:, it % 2]).then_inc(dve_done, dve.tick(("masked", it)))

                mask(0)
                for it in range(n):
                    hd, d, p, hf = head(it)
                    if it + 1 < n:
                        mask(it + 1)
                    for s, spans in SPAN[d]:
                        dve.wait_ge(*at(("E", it, s)))
                        for c0, c1 in spans:
                            e = weights_of[it % 3][:, s, c0:c1]
                            nc.vector.scalar_tensor_tensor(
                                e, e, c_dt[:, s, d * SSH + hd:d * SSH + hd + 1], a_cb[:, hd // 8, s, c0:c1],
                                ALU.mult, ALU.mult).then_inc(dve_done, dve.tick(("W", it, s)))
                    if hf == 1 and d == 1:
                        dve.wait_ge(*at(("y", it)))
                        x = xs(p, 0, T)
                        dve.step(nc.vector.scalar_tensor_tensor(x, x, a_cols[:, 16 + p:17 + p], halves_of(ps[4 + p % 2]),
                                                                ALU.mult, ALU.add), ("y read", p))
                        z = halves_of(a_oz[:, 8 + p, :])
                        vmul(z, z, x).then_inc(dve_done, dve.tick())

            block(pe_, act_, dve_)

        def ssd_norm():
            def dve_(inv):
                for k in range(8):
                    nc.vector.scalar_tensor_tensor(a_oz[:, 8 + k, :], a_oz[:, 8 + k, :], col("ssd_norm", k),
                                                            inv, ALU.mult, ALU.mult).then_inc(dve_done, dve.tick())

            rms_block("sn", lambda k: a_oz[:, 8 + k, :], 8, T, D, (dve_, None), 26704)

        def out_projection(l, mix, kt, c0, y, high_at, low_at, w_at):
            n, kq = T - c0, kt // 4
            mix_high, mix_low = parts_region(high_at - PARTS, kt, n), parts_region(low_at - PARTS, kt, n)
            w_high = parts_region(w_at - PARTS, 2, kq, 256)
            w_low = parts_region(w_at - PARTS + 512 * kq, 2, kq, 256)

            def landed(t):
                i = piece_at[("out", l, t // 4)]
                return slot_view(i, *pieces[i][1:])[:, (t % 4) * kq:(t % 4 + 1) * kq, :]

            def pe_():
                for t in range(16):
                    j, q = divmod(t, 4)
                    pe.wait_ge(*at(("w low", t)))
                    for f in range(2):
                        c = slice(f * P, (f + 1) * P)
                        pairs = []
                        for k in range(kq):
                            pe.wait_ge(*at(("mix low", q * kq + k)))
                            pairs += three(w_high[:, t % 2, k, c], w_low[:, t % 2, k, c], mix_high[:, q * kq + k, :], mix_low[:, q * kq + k, :])
                        m = mms(ps[2 * j + f][:, 0:n], pairs, q == 0, q == 3)
                        if q == 3:
                            m.then_inc(pe_done, pe.tick(("op", 2 * j + f), *([("used", t)] if f else [])))
                        elif f:
                            m.then_inc(pe_done, pe.tick(("used", t)))

            def act_():
                def split_high(t):
                    i = piece_at[("out", l, t // 4)]
                    act.wait_ge(weights_landed[i % NSLOT], 16 * (i // NSLOT + 1))
                    act.wait_ge(*at(("used", t - 2)))
                    nc.scalar.activation(w_high[:, t % 2], landed(t), ACT.Copy).then_inc(act_done, act.tick(("w high", t)))

                split_high(0)
                split_high(1)
                for k in range(kt):
                    nc.scalar.activation(mix_high[:, k, :], mix[:, k, :], ACT.Copy).then_inc(act_done, act.tick(("mix high", k)))
                for t in range(2, 16):
                    split_high(t)

            def pool_():
                for t in range(16):
                    pool.wait_ge(*at(("w high", t)))
                    nc.gpsimd.tensor_tensor(w_low[:, t % 2], landed(t), whole(w_high[:, t % 2]), ALU.subtract).then_inc(pool_done, pool.tick(("w low", t), *((let_go(("out", l, t // 4)),) if t % 4 == 3 else ())))

            def dve_():
                for k in range(kt):
                    dve.wait_ge(*at(("mix high", k)))
                    vsub(mix_low[:, k, :], mix[:, k, :], whole(mix_high[:, k, :])).then_inc(dve_done, dve.tick(("mix low", k)))
                for j in range(8):
                    dve.wait_ge(*at(("op", j)))
                    nc.vector.tensor_copy(y[:, j, c0:T], ps[j][:, 0:T - c0]).then_inc(dve_done, dve.tick(("op", "read", j)))

            block(pe_, act_, dve_, pool_, last=("out", l, 3))

        m_v = m_y = region(0, KD, T)
        m_gate = region(4096, NE, T)
        m_silu = region(12288, 4, T)
        m_small = region(4096, 24 * 64)
        m_rw = region(5632, KD, NE)
        p_vh, p_vl = parts_region(0, KD, T), parts_region(4096, KD, T)
        p_hh, p_hl = parts_region(8192, 4, T), parts_region(10240, 4, T)
        p_wh, p_wl = parts_region(12288, 4, 1024), parts_region(16384, 4, 1024)

        def router(c0, pe_shared, act_shared, dve_shared, pool_shared, sp_shared):
            nt = (T - c0) // P
            t_ = [m_small[:, i * 64:i * 64 + 16 * nt] for i in range(16)]
            aff, bias, sel = t_[0], t_[1][:, 0:16], t_[2]
            grp = [t_[i].rearrange("p (t g e) -> p t g e", t=nt, g=4) for i in range(16)]
            tiny = m_small[:, 1024:1536].rearrange("p (i t g) -> p i t g", i=32, t=4)[:, :, 0:nt, :]

            def sp_():
                load(nc.sync, m_rw, A["router_w"].rearrange("(k p) e -> p k e", p=P))
                load(nc.sync, bias, A["router_bias"].rearrange("(o e) -> o e", o=1).to_broadcast([P, NE]))
                sp_shared()

            def pe_():
                pe.wait_ge(loads_landed, loads[0] + 32)
                for t in range(nt):
                    c = slice(c0 + t * P, c0 + t * P + P)
                    mms(ps[0][:, t * NE:(t + 1) * NE], [(m_v[:, k, c], m_rw[:, k, :]) for k in range(KD)]).then_inc(pe_done, pe.tick("logits"))
                pe.wait_ge(*at(("low part", KD - 1)))
                pe.wait_ge(*at("affinities"))
                pe_shared()
                pe.wait_ge(*at("gates"))
                pe.wait_ge(*at(("out read", 1)))
                for t in range(nt):
                    m = nc.tensor.transpose(ps[1][0:NE, t * P:(t + 1) * P], grp[4].rearrange("p t g e -> p t (g e)")[:, t, :],
                                            ident[:])
                m.then_inc(pe_done, pe.tick("gates turned"))
                pe.wait_ge(*at("gate rows"))
                for e in range(NE):
                    if e >= 6:
                        pe.wait_ge(*at(("gate read", e - 6)))
                    else:
                        pe.wait_ge(*at(("out read", 2 + e)))
                    nc.tensor.matmul(ps[2 + e % 6][:, 0:T - c0], ident[0:NE, e:e + 1].to_broadcast([NE, P]),
                                             gate_rows[:, c0:T], start=True, stop=True).then_inc(pe_done, pe.tick(("gate spread", e)))

            def act_():
                for k in range(KD):
                    nc.scalar.activation(p_vh[:, k, c0:T], m_v[:, k, c0:T], ACT.Copy).then_inc(act_done, act.tick(("high part", k)))
                act.wait_ge(*at("logits"))
                nc.scalar.activation(aff, ps[0][:, 0:NE * nt], ACT.Sigmoid).then_inc(act_done, act.tick("affinities"))
                act_shared()
                for e in range(0, NE, 2):
                    act.wait_ge(*at(("gate spread", e)))
                    nc.scalar.activation(m_gate[:, e, c0:T], ps[2 + e % 6][:, 0:T - c0], ACT.Copy).then_inc(act_done, act.tick(("gate read", e)))

            def rank(x, out, tmp):
                dve.step(nc.vector.memset(out, 0.0))
                for i in range(4):
                    for j in range(i + 1, 4):
                        a, b = x[:, :, :, i:i + 1], x[:, :, :, j:j + 1]
                        dve.step(nc.vector.tensor_tensor(tmp, b, a, ALU.is_gt))
                        dve.step(vadd(out[:, :, :, i:i + 1], out[:, :, :, i:i + 1], tmp))
                        dve.step(nc.vector.tensor_scalar(tmp, tmp, -1.0, 1.0, ALU.mult, ALU.add))
                        dve.step(vadd(out[:, :, :, j:j + 1], out[:, :, :, j:j + 1], tmp))

            def dve_():
                v = nc.vector
                dve.wait_ge(*at("affinities"))
                dve.step(vadd(grp[2].rearrange("p t g e -> p t (g e)"), grp[0].rearrange("p t g e -> p t (g e)"),
                              bias.unsqueeze(1).to_broadcast([P, nt, NE])))
                rank(grp[2], grp[3], tiny[:, 0].unsqueeze(3))
                dve.step(v.tensor_scalar(t_[3], t_[3], 2.0, None, ALU.is_lt))
                dve.step(vmul(t_[5], t_[3], sel))
                dve.step(v.tensor_reduce(tiny[:, 1], grp[5], AX.X, ALU.add))
                rank(tiny[:, 1].unsqueeze(2), tiny[:, 2].unsqueeze(2), tiny[:, 3, :, 0:1].unsqueeze(3))
                dve.step(v.tensor_scalar(tiny[:, 2], tiny[:, 2], 1.0, None, ALU.is_lt))
                dve.step(vmul(grp[3], grp[3], tiny[:, 2].unsqueeze(3).to_broadcast([P, nt, 4, 4])))
                dve.step(vmul(t_[3], t_[3], aff))
                dve.step(v.tensor_reduce(tiny[:, 4, :, 0:1], grp[3].rearrange("p t g e -> p t (g e)"), AX.X, ALU.add))
                dve.step(v.reciprocal(tiny[:, 5, :, 0:1], tiny[:, 4, :, 0:1]))
                dve.step(vmul(grp[4].rearrange("p t g e -> p t (g e)"), grp[3].rearrange("p t g e -> p t (g e)"),
                              tiny[:, 5, :, 0:1].to_broadcast([P, nt, NE])), "gates")
                dve_shared()
                dve.wait_ge(*at("gates turned"))
                dve.step(v.tensor_copy(gate_rows[:, c0:T], ps[1][0:NE, 0:T - c0]), "gate rows")
                for e in range(1, NE, 2):
                    dve.wait_ge(*at(("gate spread", e)))
                    v.tensor_copy(m_gate[:, e, c0:T], ps[2 + e % 6][:, 0:T - c0]).then_inc(dve_done, dve.tick(("gate read", e)))

            def pool_():
                for k in range(KD):
                    pool.wait_ge(*at(("high part", k)))
                    nc.gpsimd.tensor_tensor(p_vl[:, k, c0:T], m_v[:, k, c0:T], whole(p_vh[:, k, c0:T]), ALU.subtract).then_inc(pool_done, pool.tick(("low part", k)))
                pool_shared()

            block(pe_, act_, dve_, pool_, sp_)

        def experts(l, c0):
            n = T - c0
            first = piece_at[("experts", l)]
            key = ("expert loop", l)

            def quarter(x, q):
                return x[:, q % 4, :].rearrange("p (k n) -> p k n", k=8 if q < 8 else 4)

            def landed_quarter(w, q):
                n_ = 128 if q < 8 else 256
                return w(q // 4)[:, :, (q % 4) * n_:(q % 4 + 1) * n_]

            def pe_ffn():
                for q in range(8):
                    pe.wait_ge(*at(("split", q)))
                    pe.wait_ge(*at(("out read", q), back=1))
                    wh, wl = quarter(p_wh, q), quarter(p_wl, q)
                    pairs = []
                    for k in range(KD):
                        pairs += three(wh[:, k, :], wl[:, k, :], p_vh[:, k, c0:T], p_vl[:, k, c0:T])
                    mms(ps[q][:, 0:n], pairs).then_inc(pe_done, pe.tick(("g" if q < 4 else "u", q % 4), ("used", q)))
                pe.wait_ge(*at(("silu", 3)))
                for q in range(8, 12):
                    pe.wait_ge(*at(("split", q)))
                    wh, wl = quarter(p_wh, q), quarter(p_wl, q)
                    for k in range(4):
                        pe.wait_ge(*at(("hidden", k)))
                        for i in range(2):
                            j, c = 2 * (q - 8) + i, slice(i * P, (i + 1) * P)
                            for x, (a, b) in enumerate(three(wh[:, k, c], wl[:, k, c], p_hh[:, k, 0:n], p_hl[:, k, 0:n])):
                                m = nc.tensor.matmul(ps[j][:, 0:n], a, b, start=k == 0 and x == 0, stop=k == 3 and x == 2)
                            if k == 3:
                                m.then_inc(pe_done, pe.tick(("out", j), *([("used", q)] if i else [])))

            def act_ffn(w, landed):
                def split_high(q):
                    if q % 4 == 0:
                        act.wait_ge(*landed(q // 4))
                    if q >= 4:
                        act.wait_ge(*at(("used", q - 4)))
                    else:
                        act.wait_ge(*at(("used", q + 8), back=1))
                    nc.scalar.activation(quarter(p_wh, q), landed_quarter(w, q), ACT.Copy).then_inc(act_done, act.tick(("high", q)))

                for q in range(4):
                    split_high(q)
                for f in range(4):
                    act.wait_ge(*at(("g", f)))
                    nc.scalar.activation(m_silu[:, f, 0:n], ps[f][:, 0:n], ACT.Silu).then_inc(act_done, act.tick(("silu", f)))
                    split_high(4 + f)
                for q in range(8, 12):
                    split_high(q)

            def pool_ffn(w, freed):
                for q in range(12):
                    pool.wait_ge(*at(("high", q)))
                    nc.gpsimd.tensor_tensor(quarter(p_wl, q), landed_quarter(w, q), whole(quarter(p_wh, q)), ALU.subtract).then_inc(pool_done, pool.tick(("split", q), *([freed(q // 4)] if q % 4 == 3 else [])))

            def dve_ffn(gate):
                for f in range(4):
                    dve.wait_ge(*at(("silu", f)))
                    dve.wait_ge(*at(("u", f)))
                    t_ = m_silu[:, f, 0:n]
                    dve.step(vmul(t_, ps[4 + f][:, 0:n], t_))
                    if gate is not None:
                        dve.step(vmul(t_, t_, gate))
                    dve.step(nc.vector.tensor_copy(p_hh[:, f, 0:n], t_))
                    vsub(p_hl[:, f, 0:n], t_, whole(p_hh[:, f, 0:n])).then_inc(dve_done, dve.tick(("hidden", f)))
                for j in range(8):
                    dve.wait_ge(*at(("out", j)))
                    y = m_y[:, j, c0:T]
                    if gate is None:
                        nc.vector.tensor_copy(y, ps[j][:, 0:n]).then_inc(dve_done, dve.tick(("out read", j)))
                    else:
                        vadd(y, y, ps[j][:, 0:n]).then_inc(dve_done, dve.tick(("out read", j)))

            shapes = [(8, 512), (8, 512), (4, 1024)]
            names = ("exp_w_gate", "exp_w_up", "exp_w_down")

            def load_expert(e, k):
                src = A[names[k]][l, bass.ds(e, 1)].rearrange("o (k p) n -> p (o k) n", p=P)
                s = (first + k) % NSLOT
                nc.sync.dma_start(slot_view(s, *shapes[k]), src).then_inc(weights_landed[s], 16)

            def sp_first():
                stream_weights(piece_at[("sh", l, 2)])
                for k in range(3):
                    sp.wait_ge(*at(("let go", first + k - NSLOT)))
                    load_expert(0, k)
                issued[0] += 3 * NE

            def shared_w(k):
                return slot_view(first - 3 + k, *shapes[k])

            def shared_landed(k):
                i = first - 3 + k
                return weights_landed[i % NSLOT], 16 * (i // NSLOT + 1)

            router(c0, pe_ffn, lambda: act_ffn(shared_w, shared_landed), lambda: dve_ffn(None),
                   lambda: pool_ffn(shared_w, lambda k: let_go(("sh", l, k))), sp_first)

            def looped(engine, lo, body):
                with engine.e.Fori(lo, NE) as e:
                    engine.start_loop(e, key, NE)
                    body(e)
                    engine.end_loop()

            def expert_w(k):
                return slot_view(first + k, *shapes[k])

            def act_loop(e):
                act_ffn(expert_w, lambda k: (weights_landed[(first + k) % NSLOT], e * 16 + 16 * ((first + k) // NSLOT + 1)))

            def pool_loop(e):
                pool_ffn(expert_w, lambda k: ("let go", first + 3 * NE - NSLOT + k))

            def sp_loop(e):
                for k in range(3):
                    sp.wait_ge(*at(("let go", first + 3 * NE - NSLOT + k), back=1))
                    load_expert(e, k)

            def sp_all():
                looped(sp, 1, sp_loop)
                if issued[0] < len(pieces):
                    stream_weights(issued[0] - 1)

            block(lambda: looped(pe, 0, lambda e: pe_ffn()), lambda: looped(act, 0, act_loop),
                  lambda: looped(dve, 0, lambda e: dve_ffn(m_gate[:, bass.ds(e, 1), c0:T].rearrange("p o t -> p (o t)"))),
                  lambda: looped(pool, 0, pool_loop), sp_all)

        def moe(l, c0):
            modulated("v", 2, 24, m_v, 12288, c0)
            experts(l, c0)
            residual("r", 3, m_y, 12288, c0)

        b_rope = region(0, 2, NL)
        b_rmask = region(512, 2, 6, L)
        b_restart = region(1280, 2, 8 * L)
        b_w2, b_a2, b_g2 = region(2304, D), region(3328, D), region(4352, D)
        b_r, b_k, b_v = region(5376, KD, NL), region(7424, KD, T), region(11520, KD, T)
        b_kk = region(15616, KD, T)
        b_mix = region(19712, 12, NL)
        b_att, b_y = b_mix[:, 0:4, :], b_mix[:, 4:12, :]
        b_tw, b_al, b_gl = region(22784, T), region(23296, T), region(23808, NL)
        b_u = region(28416, KD, T)
        n_q, n_kv = region(5376, 3, NL), region(6144, 2, T)
        n_kr = region(7168, 2, T)
        n_uq, n_uqs, n_ukv = region(8192, 3, AH * HD), region(10496, 3, AH * ROPE), region(11264, 2, D)
        n_kh, n_vt = region(13312, AH, T), region(17408, TT, AH * AV)
        n_qh = region(24064, AH, NL)
        n_p, n_pt = region(26112, 2, T), region(27136, 2, T)
        n_krs = region(28160, KD, ROPE)
        n_stat = region(34600, 4, 16)
        lat = slice(NC_, T)

        def swap(dst, src, e, label):
            nc.gpsimd.tensor_copy(dst[..., 0:16], src[..., 16:32]).then_inc(e.sem, e.tick())
            return nc.gpsimd.tensor_copy(dst[..., 16:32], src[..., 0:16]).then_inc(e.sem, e.tick(label))

        def project_mla():
            i_kv = piece_at["mkv"]

            def pe_():
                w = weights("mq")
                for f in range(3):
                    mms(ps[f][:, 0:NL], [(w[:, k, f * P:(f + 1) * P], b_u[:, k, lat]) for k in range(KD)]).then_inc(pe_done, pe.tick(("q", f), *((let_go("mq"),) if f == 2 else ())))
                w = weights("mkv")
                for f in range(2):
                    mms(ps[3 + f], [(w[:, k, f * P:(f + 1) * P], b_u[:, k, :]) for k in range(KD)]).then_inc(pe_done, pe.tick(("kv", f)))
                mms(ps[5][64:96, :], [(w[:, k, 256:288], b_u[:, k, :]) for k in range(KD)])
                pe.wait_ge(*at("kr swapped"))
                mms(ps[6][64:96, :], [(n_krs[:, k, :], b_u[:, k, :]) for k in range(KD)]).then_inc(pe_done, pe.tick("kr", let_go("mkv")))

            def pool_():
                _, kt, n = pieces[i_kv]
                pool.wait_ge(weights_landed[i_kv % NSLOT], 16 * (i_kv // NSLOT + 1))
                swap(n_krs, slot_view(i_kv, kt, n)[:, :, 256:288], pool, "kr swapped")
                pool.wait_ge(loads_landed, loads[0] + 16 * 5)
                for k in range(3):
                    dst = n_uqs[:, k, :].rearrange("p (h r) -> p h r", h=AH)
                    src = n_uq[:, k, :].rearrange("p (h x) -> p h x", h=AH)[:, :, NOPE:HD]
                    swap(dst, src, pool, "uq swapped")

            def act_():
                for f in range(3):
                    act.wait_ge(*at(("q", f)))
                    nc.scalar.activation(n_q[:, f, :], ps[f][:, 0:NL], ACT.Copy).then_inc(act_done, act.tick())

            def dve_():
                for f in range(2):
                    dve.wait_ge(*at(("kv", f)))
                    nc.vector.tensor_copy(n_kv[:, f, :], ps[3 + f]).then_inc(dve_done, dve.tick())
                dve.wait_ge(*at("kr"))
                dve.wait_ge(loads_landed, loads[0] + 16 * 5)
                r = slice(64, 96)
                nc.vector.tensor_copy(n_kr[r, 0, 0:NC_], ps[5][r, 0:NC_]).then_inc(dve_done, dve.tick())
                vmul(n_kr[r, 0, lat], ps[5][r, lat], b_rope[r, 0, :]).then_inc(dve_done, dve.tick())
                dve.step(vmul(n_kr[r, 1, lat], ps[6][r, lat], b_rope[r, 1, :]))
                vadd(n_kr[r, 0, lat], n_kr[r, 0, lat], n_kr[r, 1, lat]).then_inc(dve_done, dve.tick())

            def sp_():
                load(nc.sync, b_rope[64:96], A["rope"])
                load(nc.sync, n_uq, A["mla_w_uq"][0].rearrange("(k p) n -> p k n", p=P))
                load(nc.sync, n_ukv, A["mla_w_ukv"][0].rearrange("(k p) n -> p k n", p=P))
                load(nc.sync, b_rmask, A["rmask"])
                load(nc.sync, b_restart, A["restart"])

            block(pe_, act_, dve_, pool_, sp_, last="mkv")

        def norm_latent(tag, x, n, cols, dim, gain):
            def dve_(inv):
                for k in range(n):
                    nc.vector.scalar_tensor_tensor(x[:, k, :], x[:, k, :], col(gain, k), inv, ALU.mult,
                                                            ALU.mult).then_inc(dve_done, dve.tick())

            rms_block(tag, lambda k: x[:, k, :], n, cols, dim, (dve_, None), 13312)

        def attention_heads():
            r = slice(64, 96)
            ukv = n_ukv.rearrange("p k (h x) -> p k h x", h=AH)
            tmp = n_p

            def pe_():
                for hd in range(AH):
                    o = bank("ah", 2 * hd)
                    mms(o[0:HD, 0:NL], [(n_uq[:, k, hd * HD:(hd + 1) * HD], n_q[:, k, :]) for k in range(3)])
                    mms(o[r, NL:T], [(n_uqs[:, k, hd * ROPE:(hd + 1) * ROPE], n_q[:, k, :]) for k in range(3)]).then_inc(pe_done, pe.tick(("ah", 2 * hd)))
                    mms(bank("ah", 2 * hd + 1)[0:64, :], [(ukv[:, k, hd, 0:64], n_kv[:, k, :]) for k in range(2)]).then_inc(pe_done, pe.tick(("ah", 2 * hd + 1)))
                for tt in range(TT):
                    mms(bank("ah", 16 + tt), [(n_kv[:, k, tt * P:(tt + 1) * P], ukv[:, k, :, 64:128]) for k in range(2)]).then_inc(pe_done, pe.tick(("ah", 16 + tt)))

            def dve_():
                for hd in range(AH):
                    dve.wait_ge(*at(("ah", 2 * hd)))
                    o, t = ps[(2 * hd) % 8], tmp[r, hd % 2, 0:NL]
                    one = nc.vector.scalar_tensor_tensor
                    nc.vector.tensor_scalar(n_qh[0:64, hd, :], o[0:64, 0:NL], ASCALE, None, ALU.mult).then_inc(dve_done, dve.tick())
                    one(t, o[r, 0:NL], ASCALE, b_rope[r, 0, :], ALU.mult, ALU.mult).then_inc(dve_done, dve.tick())
                    dve.step(one(n_qh[r, hd, :], o[r, NL:T], ASCALE, b_rope[r, 1, :], ALU.mult, ALU.mult),
                             ("ah", "read", 2 * hd))
                    vadd(n_qh[r, hd, :], n_qh[r, hd, :], t).then_inc(dve_done, dve.tick())

            def act_():
                for hd in range(AH):
                    act.wait_ge(*at(("ah", 2 * hd + 1)))
                    nc.scalar.activation(n_kh[0:64, hd, :], ps[(2 * hd + 1) % 8][0:64, :], ACT.Copy).then_inc(act_done, act.tick(("ah", "read", 2 * hd + 1)))
                for tt in range(TT):
                    act.wait_ge(*at(("ah", 16 + tt)))
                    nc.scalar.activation(n_vt[:, tt, :], ps[(16 + tt) % 8], ACT.Copy).then_inc(act_done, act.tick(("ah", "read", 16 + tt)))

            def pool_():
                for hd in range(AH):
                    nc.gpsimd.tensor_copy(n_kh[r, hd, :], n_kr[r, 0, :]).then_inc(pool_done, pool.tick())

            block(pe_, act_, dve_, pool_)

        def attention():
            n = 2 * AH
            neg, total, inv = n_stat[:, 0], n_stat[:, 1], n_stat[:, 2]

            def pe_():
                def scores(j):
                    hd, jt = divmod(j, 2)
                    pe.wait_ge(*at(("P", j - 2)))
                    mms(ps[j % 2], [(n_qh[0:HD, hd, jt * P:(jt + 1) * P], n_kh[0:HD, hd, :])]).then_inc(pe_done, pe.tick(("scores", j)))

                scores(0)
                for j in range(n):
                    hd, jt = divmod(j, 2)
                    if j + 1 < n:
                        scores(j + 1)
                    pe.wait_ge(*at(("Pn", j)))
                    pe.wait_ge(*at(("PT", j - 2)))
                    for s in range(TT):
                        m = nc.tensor.transpose(ps[2 + j % 2][:, s * P:(s + 1) * P], n_p[:, j % 2, s * P:(s + 1) * P],
                                                ident[:])
                    m.then_inc(pe_done, pe.tick(("turned", j)))
                    pe.wait_ge(*at(("PT", j)))
                    if hd % 2 == 0 and jt == 0:
                        pe.wait_ge(*at(("att read", hd // 2 - 2)))
                    rows = slice(64 * (hd % 2), 64 * (hd % 2) + 64)
                    mms(ps[4 + (hd // 2) % 2][rows, jt * P:(jt + 1) * P], [(n_vt[:, s, hd * AV:(hd + 1) * AV], n_pt[:, j % 2, s * P:(s + 1) * P]) for s in range(TT)]).then_inc(pe_done, pe.tick(("O", j)))

            def dve_():
                for j in range(n):
                    dve.wait_ge(*at(("scores", j)))
                    nc.vector.tensor_reduce(neg[:, j:j + 1], ps[j % 2], AX.X, ALU.max, negate=True).then_inc(dve_done, dve.tick(("max", j)))
                    dve.wait_ge(*at(("P", j)))
                    dve.step(nc.vector.reciprocal(inv[:, j:j + 1], total[:, j:j + 1]))
                    nc.vector.tensor_scalar(n_p[:, j % 2, :], n_p[:, j % 2, :], inv[:, j:j + 1], None, ALU.mult).then_inc(dve_done, dve.tick(("Pn", j)))
                    if j % 4 == 3:
                        dve.wait_ge(*at(("O", j)))
                        nc.vector.tensor_copy(b_att[:, j // 4, :], ps[4 + (j // 4) % 2][:, 0:NL]).then_inc(dve_done, dve.tick(("att read", j // 4)))

            def act_():
                def turn(j):
                    act.wait_ge(*at(("turned", j)))
                    act.wait_ge(*at(("O", j - 2)))
                    nc.scalar.activation(n_pt[:, j % 2, :], ps[2 + j % 2], ACT.Copy).then_inc(act_done, act.tick(("PT", j)))

                for j in range(n):
                    act.wait_ge(*at(("max", j)))
                    act.wait_ge(*at(("turned", j - 2)))
                    nc.scalar.activation(n_p[:, j % 2, :], ps[j % 2], ACT.Exp, bias=neg[:, j:j + 1],
                                                  accum_out=total[:, j:j + 1]).then_inc(act_done, act.tick(("P", j)))
                    turn(j)

            block(pe_, act_, dve_)

        def project_rwkv():
            raw = region(32512, 2, 2, 258)
            tmp = region(33544, T)
            u_high, u_low = parts_region(15616 - PARTS, KD, T), parts_region(28416 - PARTS, KD, T)
            w_high = parts_region(24064 - PARTS, 2, KD, P)
            w_low = parts_region(26112 - PARTS, 2, KD, P)
            jobs = [(("r", j // 4), j % 4, b_r[:, j, :], j) for j in range(8)]
            jobs += [(("rk", j // 4), j % 4, b_k[:, j, :], 8 + j) for j in range(8)]
            jobs += [(("rv", j // 4), j % 4, b_v[:, j, :], 16 + j) for j in range(8)]
            jobs += [("low", 0, b_tw, 24), ("low", 1, b_al, 25), ("low", 2, b_gl, 26)]

            def pe_():
                pe.wait_ge(*at(("u low", KD - 1)))
                for j, (_, _, dst, _) in enumerate(jobs):
                    c0 = T - dst.shape[-1]
                    pe.wait_ge(*at(("w low", j)))
                    pairs = []
                    for k in range(KD):
                        pairs += three(w_high[:, j % 2, k, :], w_low[:, j % 2, k, :], u_high[:, k, c0:T], u_low[:, k, c0:T])
                    mms(bank("rw", j)[:, c0:T], pairs).then_inc(pe_done, pe.tick(("rw", j)))

            def landed(j):
                key, f, _, _ = jobs[j]
                i = piece_at[key]
                return slot_view(i, *pieces[i][1:])[:, :, f * P:(f + 1) * P]

            def pool_():
                nc.gpsimd.memset(raw[:, :, :, 0:1], 0.0).then_inc(pool_done, pool.tick("pads"))
                nc.gpsimd.memset(raw[:, :, :, 257:258], 0.0).then_inc(pool_done, pool.tick("pads"))
                for j, (key, f, _, _) in enumerate(jobs):
                    pool.wait_ge(*at(("w high", j)))
                    last = f == (2 if key == "low" else 3)
                    nc.gpsimd.tensor_tensor(w_low[:, j % 2], landed(j), whole(w_high[:, j % 2]), ALU.subtract).then_inc(pool_done, pool.tick(("w low", j), *((let_go(key),) if last else ())))

            def act_():
                def split_high(j):
                    i = piece_at[jobs[j][0]]
                    act.wait_ge(weights_landed[i % NSLOT], 16 * (i // NSLOT + 1))
                    act.wait_ge(*at(("rw", j - 2)))
                    nc.scalar.activation(w_high[:, j % 2], landed(j), ACT.Copy).then_inc(act_done, act.tick(("w high", j)))

                split_high(0)
                split_high(1)
                for k in range(KD):
                    nc.scalar.activation(u_high[:, k, :], b_u[:, k, :], ACT.Copy).then_inc(act_done, act.tick(("u high", k)))
                for j, (_, _, dst, _) in enumerate(jobs):
                    if j + 2 < len(jobs):
                        split_high(j + 2)
                    act.wait_ge(*at(("rw", j)))
                    act.wait_ge(*at(("mixed", j - 2)))
                    s = slice(1, 2) if dst.shape[-1] == NL else slice(0, 2)
                    nc.scalar.activation(raw[:, j % 2, s, 1:257], ps[j % 8].rearrange("p (s t) -> p s t", s=2)[:, s],
                                                  ACT.Copy).then_inc(act_done, act.tick(("rw", "read", j)))
                act.wait_ge(*at(("mixed", 26)))
                nc.scalar.activation(b_tw, b_tw, ACT.Tanh).then_inc(act_done, act.tick())
                nc.scalar.activation(b_gl, b_gl, ACT.Sigmoid).then_inc(act_done, act.tick())

            def dve_():
                for k in range(KD):
                    dve.wait_ge(*at(("u high", k)))
                    vsub(u_low[:, k, :], b_u[:, k, :], whole(u_high[:, k, :])).then_inc(dve_done, dve.tick(("u low", k)))
                dve.wait_ge(*at("pads"))
                for j, (_, _, dst, m) in enumerate(jobs):
                    dve.wait_ge(*at(("rw", "read", j)))
                    s = slice(1, 2) if dst.shape[-1] == NL else slice(0, 2)
                    x, n = raw[:, j % 2, s], s.stop - s.start
                    t, o = (y.rearrange("p (s t) -> p s t", s=n) for y in (tmp[:, 0:256 * n], dst))
                    one = nc.vector.scalar_tensor_tensor
                    dve.step(vadd(t, x[:, :, 0:256], x[:, :, 2:258]))
                    dve.step(one(t, t, 0.5, x[:, :, 1:257], ALU.mult, ALU.subtract))
                    dve.step(one(o, t, col("rw_mu", m), x[:, :, 1:257], ALU.mult, ALU.add), ("mixed", j))

            def sp_():
                load(nc.sync, b_w2, A["rw_w2"].rearrange("l a r n -> (l a r) n"))
                load(nc.sync, b_a2, A["rw_a2"].rearrange("l a r n -> (l a r) n"))
                load(nc.sync, b_g2, A["rw_g2"].rearrange("l r n -> (l r) n"))

            def sp_all():
                sp_()
                stream_weights(piece_at["low"] - NSLOT)

            block(pe_, act_, dve_, pool_, sp_all)

        def key_norms():
            sq, root = region(24064, 2, T), region(25088, 2, T)

            def act_():
                for k in range(KD):
                    act.wait_ge(*at(("kx", k)))
                    act.wait_ge(*at(("ksum", k - 2)))
                    nc.scalar.activation(sq[:, k % 2, :], b_kk[:, k, :], ACT.Square).then_inc(act_done, act.tick(("ksq", k)))
                    act.wait_ge(*at(("ksum", k)))
                    act.wait_ge(*at(("kn", k - 2)))
                    nc.scalar.activation(root[:, k % 2, :], ps[k % 2], ACT.Sqrt).then_inc(act_done, act.tick(("kroot", k)))

            def pe_():
                for k in range(KD):
                    pe.wait_ge(*at(("ksq", k)))
                    pe.wait_ge(*at(("kroot", k - 2)))
                    mms(ps[k % 2], [(blockones[:], sq[:, k % 2, :])]).then_inc(pe_done, pe.tick(("ksum", k)))

            def dve_():
                for k in range(KD):
                    nc.vector.tensor_scalar(b_kk[:, k, :], b_k[:, k, :], col("rw_kk", k), None, ALU.mult).then_inc(dve_done, dve.tick(("kx", k)))
                for k in range(KD):
                    dve.wait_ge(*at(("kroot", k)))
                    x = root[:, k % 2, :]
                    dve.step(nc.vector.tensor_scalar(x, x, 1e-12, None, ALU.max))
                    dve.step(nc.vector.reciprocal(x, x))
                    vmul(b_kk[:, k, :], b_kk[:, k, :], x).then_inc(dve_done, dve.tick(("kn", k)))
                nc.vector.tensor_scalar(ka1, vec[:, VEC["rw_ka"]:VEC["rw_ka"] + 8], -1.0, 1.0, ALU.mult, ALU.add).then_inc(dve_done, dve.tick())

            def pool_():
                nc.gpsimd.memset(b_y, 0.0).then_inc(pool_done, pool.tick())
                for d in range(2):
                    nc.gpsimd.memset(st[d]["S"], 0.0).then_inc(pool_done, pool.tick())

            block(pe_, act_, dve_, pool_)

        ringflat = ring[:].rearrange("p s n -> p (s n)")


        def staging(d):
            def at(i, n=8 * L):
                if d == 0 and i >= 20:
                    return h[:, :, (i - 20) * L:(i - 19) * L]
                a = 512 * i
                flat = arena[:, 24064 + a:24064 + a + n] if d == 0 else ringflat[:, a:a + n]
                return flat.rearrange("p (h t) -> p h t", t=L)

            s = {n_: at(i) for i, n_ in enumerate(
                ("a", "r", "vt", "Ot", "RB", "RK", "D", "Dt", "D2", "D2t", "T", "S",
                 "sw", "G", "A", "t", "Pinv", "bend", "v", "AK", "bt", "kt"))}
            s.update(Pexc=s["sw"], next_a=s["sw"], Pinc=s["G"], next_r=s["G"], b=s["A"], k=s["t"], kend=s["Pinv"])
            s.update(D4=s["D"], D4t=s["Dt"], D8t=s["D2t"], W=s["Dt"], N=s["D"], V1=s["D2"], V2=s["D2t"],
                     V3=s["Dt"], U=s["D2t"])
            flat = arena[:, 34304:34448] if d == 0 else ringflat[:, 11776:11920]
            s["low"] = flat[:, 0:2 * L].rearrange("p (h t) -> p h t", t=L)
            s["end"], s["next_end"] = flat[:, 2 * L:2 * L + 8], flat[:, 2 * L + 8:2 * L + 16]
            return s

        st = [staging(0), staging(1)]

        def products(seg, main, front):
            p = []
            if main:
                p += [("bt", (), ("bend",), "bend"), ("kt", (), ("kend",), "kend"), ("vt", (), ("v",), "v"),
                      ("X", ("a",), ("b",), [("b", "a")]), ("Xt", (), (), [("a", "b")]), ("AK", (), ("k",), [("k", "a")])]
                if seg == 1:
                    p += [("RB", ("r",), (), [("b", "r")]), ("RK", (), (), [("k", "r")])]
            if front:
                p += [("z", ("low",), (), None), ("za", (), (), None)]
            if main:
                p += [("D2", ("D", "Dt"), (), [("Dt", "D")]), ("D2t", (), (), [("D", "Dt")]),
                      ("T2", ("T1", "D2", "D2t"), (), [("D2t", "T")]), ("D4", (), (), [("D2t", "D2")]),
                      ("D4t", (), (), [("D2", "D2t")]), ("T4", ("T2", "D4t", "D4"), (), [("D4t", "T")]),
                      ("D8t", (), (), [("D4", "D4t")]), ("T8", ("T4", "D8t"), (), [("D8t", "T")]),
                      ("W", ("AK", "vt"), ("S",), [("a", "S"), ("AK", "vt")]), ("N", ("T8", "Ot"), (), [("Ot", "T")]),
                      ("V1", ("W",), (), [("T", "W")]), ("V2", ("V1", "N"), (), [("N", "V1")]),
                      ("V3", ("V2",), (), [("N", "V2")]), ("U", ("V3",), (), [("N", "V3")])]
                if seg == 1:
                    p += [("Y", ("U", "RB", "RK"), (), [("S", "r"), ("U", "RB"), ("vt", "RK")])]
                p += [("S", ("U", "bt", "kt"), (), [("bt", "U"), ("kt", "vt")])]
            return p

        def rwkv(key, main, front, rounds=1):
            seg, main_chunk = main or (None, None)
            next_seg, front_chunk = front or (None, None)
            prods = products(seg, main is not None, front is not None)
            order = [x[0] for x in prods]

            def bank_of(d, n_):
                return ps[4 * d + order.index(n_) % 4]

            def view(d, n_):
                return bank_of(d, n_).rearrange("p (h t) -> p h t", t=L)

            def chunk(x, seg, j, d, base=0):
                first_col = seg * 256 + (j * L if d == 0 else 192 - j * L) - base
                return x[:, :, bass.ds(first_col, L)]

            def pe_round(i):
                for j, (n_, now, last, pairs) in enumerate(prods):
                    for d in range(2):
                        now_, last_ = [(x, d) for x in now], [(x, d) for x in last]
                        if j >= 4:
                            now_.append((order[j - 4] + " read", d))
                        else:
                            last_.append(([x for k, x in enumerate(order) if k % 4 == j][-1] + " read", d))
                        pe.wait_ge(*latest("act", now_, last_))
                        pe.wait_ge(*latest("dve", now_, last_))
                        pe.settle()
                        o = bank_of(d, n_)
                        if pairs is None:
                            w = b_w2 if n_ == "z" else b_a2
                            rows = slice(64 * d, 64 * d + 64)
                            for f in range(KD):
                                m = nc.tensor.matmul(o[:, f * L:(f + 1) * L], w[rows, f * P:(f + 1) * P],
                                                     st[d]["low"][rows, 0 if n_ == "z" else 1, :], start=True, stop=True)
                        elif isinstance(pairs, str):
                            for p in range(4):
                                m = nc.tensor.transpose(o[:, p * P:(p + 1) * P],
                                                        st[d][pairs][:, 2 * p:2 * p + 2, :].rearrange("p h t -> p (h t)"), ident[:])
                        else:
                            for p in range(8):
                                for hf in range(2):
                                    rows = slice(64 * hf, 64 * hf + 64)
                                    for q, (a, b) in enumerate(pairs):
                                        m = nc.tensor.matmul(o[rows, p * L:(p + 1) * L], st[d][a][rows, p, :], st[d][b][rows, p, :],
                                                             start=q == 0, stop=q == len(pairs) - 1)
                        m.then_inc(pe_done, pe.tick((n_ + " product", d)))

            def act_round(i):
                def fn(d, label, o, x, f=ACT.Copy, **kw):
                    nc.scalar.activation(o, x, f, **kw).then_inc(act_done, act.tick((label, d)))

                def turn(n_, last=None):
                    for d in range(2):
                        act.wait_ge(*at(((last or n_) + " product", d)))
                        nc.scalar.activation(st[d][n_], view(d, n_), ACT.Copy).then_inc(
                            act_done, act.tick((n_, d), (n_ + " read", d)))

                def regroup(n_):
                    for d in range(2):
                        act.wait_ge(*at((n_ + " product", d)))
                        o = bank_of(d, n_).rearrange("p (q h t) -> p q h t", q=4, h=2)
                        dst = st[d][n_].rearrange("p (q h) t -> p q h t", h=2)
                        for odd in range(2):
                            for hf in range(2):
                                m = nc.scalar.activation(dst[64 * hf:64 * hf + 64, :, odd, :], o[64 * odd:64 * odd + 64, :, hf, :], ACT.Copy)
                                m.then_inc(act_done, act.tick(*([(n_, d), (n_ + " read", d)] if odd and hf else [])))

                if main:
                    for d in range(2):
                        act.wait_ge(*at(("S read", d), back=1))
                        fn(d, "a", st[d]["a"], st[d]["next_a"])
                        if seg == 1:
                            fn(d, "r", st[d]["r"], st[d]["next_r"])
                        fn(d, "end", st[d]["end"], st[d]["next_end"])
                if front:
                    j = front_chunk(i)
                    for d in range(2):
                        c = next_seg * 256 + (j * L if d == 0 else 192 - j * L)
                        act.wait_ge(*at(("za product", d), back=1))
                        nc.scalar.activation(st[d]["low"][:, 0, :], b_tw[:, bass.ds(c, L)], ACT.Copy).then_inc(act_done, act.tick())
                        fn(d, "low", st[d]["low"][:, 1, :], b_al[:, bass.ds(c, L)])
                if main:
                    regroup("bt")
                    regroup("kt")
                    regroup("vt")
                if front:
                    for d in range(2):
                        fn(d, "v", st[d]["v"], chunk(b_v, next_seg, j, d))
                if main:
                    turn("D2")
                    turn("D2t")
                if front:
                    for d in range(2):
                        s = st[d]
                        act.wait_ge(*at(("z+w0", d)))
                        fn(d, "tanh w", s["sw"], s["sw"], ACT.Tanh, scale=0.5)
                        act.wait_ge(*at(("a+a0", d)))
                        fn(d, "tanh a", s["A"], s["A"], ACT.Tanh, scale=0.5)
                if main:
                    turn("D4", last="D4t")
                    turn("D4t")
                if front:
                    for d in range(2):
                        s = st[d]
                        act.wait_ge(*at(("G-sw", d)))
                        fn(d, "Pinv", s["Pinv"], s["G"], ACT.Exp, scale=LWC)
                        fn(d, "Pinc", s["Pinc"], s["G"], ACT.Exp, scale=-LWC)
                        fn(d, "Pexc", s["Pexc"], s["Pexc"], ACT.Exp, scale=-LWC)
                if main:
                    turn("D8t")
                    turn("W")
                    turn("N")
                    turn("V1")

            def dve_round(i):
                v = nc.vector

                def go(ins, d, *names, settle=False):
                    dve.step(ins, *[(n_, d) for n_ in names])
                    if settle:
                        dve.settle()

                def across(name, k):
                    c = VEC[name] + k
                    return vec[:, c:c + 8].unsqueeze(2).to_broadcast([P, 8, L])

                def mask(d, k):
                    return b_rmask[:, d, k, :].unsqueeze(1).to_broadcast([P, 8, L])

                def front_1():
                    for d in range(2):
                        s = st[d]
                        dve.wait_ge(*at(("z product", d)))
                        go(vadd(s["sw"], view(d, "z"), across("rw_w0", 8 * d)), d, "z+w0", "z read")
                        dve.wait_ge(*at(("za product", d)))
                        go(vadd(s["A"], view(d, "za"), across("rw_a0", 8 * d)), d, "a+a0", "za read")

                def front_2():
                    for d in range(2):
                        s = st[d]
                        dve.wait_ge(*at(("tanh w", d)))
                        go(v.tensor_scalar(s["sw"], s["sw"], 0.5, 0.5, ALU.mult, ALU.add), d, "sw")
                        flat = [x.rearrange("p h t -> p (h t)") for x in (s["G"], b_restart[:, d].rearrange(
                            "p (h t) -> p h t", t=L), s["sw"])]
                        if d:
                            flat = [x[:, ::-1] for x in flat]
                        go(v.tensor_tensor_scan(flat[0], flat[1], flat[2], 0.0, ALU.mult, ALU.add), d, "G")
                        go(vsub(s["Pexc"], s["G"], s["sw"]), d, "G-sw")

                def front_3():
                    for d in range(2):
                        s, j = st[d], front_chunk(i)
                        dve.wait_ge(*at(("tanh a", d)))
                        go(v.tensor_scalar(s["A"], s["A"], 0.5, 0.5, ALU.mult, ALU.add), d, "A")
                        go(vmul(s["t"], s["A"], across("rw_ka", 0)), d)
                        go(vadd(s["t"], s["t"], ka1.unsqueeze(2).to_broadcast([P, 8, L])), d, settle=True)
                        go(vmul(s["t"], s["t"], chunk(b_k, next_seg, j, d)), d, settle=True)
                        go(vmul(s["A"], s["A"], chunk(b_kk, next_seg, j, d)), d)

                def front_4():
                    for d in range(2):
                        s = st[d]
                        dve.wait_ge(*at(("Pexc", d)))
                        go(vmul(s["k"], s["t"], s["Pinv"]), d, "k")
                        go(vmul(s["b"], s["A"], s["Pinv"]), d, "b")
                        go(v.tensor_copy(s["next_end"], s["Pinc"][:, :, (L - 1) * (1 - d)]), d)
                        end = s["next_end"].unsqueeze(2).to_broadcast([P, 8, L])
                        go(vmul(s["bend"], s["b"], end), d, "bend")
                        go(vmul(s["kend"], s["k"], end), d, "kend")

                def front_5():
                    for d in range(2):
                        s, j = st[d], front_chunk(i)
                        go(v.tensor_scalar(s["Pexc"], s["Pexc"], -1.0, None, ALU.mult), d, settle=True)
                        go(vmul(s["next_a"], s["Pexc"], chunk(b_kk, next_seg, j, d)), d, settle=True)
                        if next_seg == 1:
                            go(vmul(s["next_r"], s["Pinc"], chunk(b_r, 1, j, d, NC_)), d)

                def add_power(n_):
                    for d in range(2):
                        s = st[d]
                        dve.wait_ge(*at((n_ + " product", d)))
                        go(vadd(s["T"], s["T"], view(d, n_)), d, n_, n_ + " read")

                if main:
                    sid = stackid[:].unsqueeze(1).to_broadcast([P, 8, L])
                    for d in range(2):
                        s = st[d]
                        dve.wait_ge(*at(("X product", d)))
                        go(vmul(s["D"], view(d, "X"), mask(d, 2)), d, "D", "X read")
                        dve.wait_ge(*at(("Xt product", d)))
                        go(vmul(s["Dt"], view(d, "Xt"), mask(d, 4)), d, "Dt")
                    for d in range(2):
                        s = st[d]
                        go(vadd(s["T"], s["D"], sid), d, "T1")
                        go(vmul(s["Ot"], view(d, "Xt"), mask(d, 5)), d, "Ot", "Xt read")
                    for d in range(2):
                        s = st[d]
                        dve.wait_ge(*at(("AK product", d)))
                        go(vmul(s["AK"], view(d, "AK"), mask(d, 0)), d, "AK", "AK read")
                        if seg == 1:
                            dve.wait_ge(*at(("RB product", d)))
                            go(vmul(s["RB"], view(d, "RB"), mask(d, 1)), d, "RB", "RB read")
                            dve.wait_ge(*at(("RK product", d)))
                            go(vmul(s["RK"], view(d, "RK"), mask(d, 1)), d, "RK", "RK read")
                if front:
                    front_1()
                if main:
                    add_power("T2")
                if front:
                    front_2()
                if main:
                    add_power("T4")
                if front:
                    front_3()
                if main:
                    add_power("T8")
                if front:
                    front_4()
                    front_5()
                if main:
                    for n_ in ("V2", "V3", "U"):
                        for d in range(2):
                            s = st[d]
                            dve.wait_ge(*at(("V1", d)))
                            dve.wait_ge(*at((n_ + " product", d)))
                            go(vadd(s[n_], view(d, n_), s["V1"]), d, n_, n_ + " read")
                if main:
                    for d in range(2):
                        if seg == 1:
                            dve.wait_ge(*at(("Y product", d)))
                            dve.settle()
                            y = chunk(b_y, 1, main_chunk(i), d, NC_)
                            go(vadd(y, y, view(d, "Y")), d, "Y read")
                    for d in range(2):
                        s = st[d]
                        end = s["end"].unsqueeze(2).to_broadcast([P, 8, L])
                        dve.wait_ge(*at(("end", d)))
                        dve.wait_ge(*at(("S product", d)))
                        go(vmul(s["S"], s["S"], end), d)
                        go(vadd(s["S"], s["S"], view(d, "S")), d, "S", "S read")

            def looped(engine, body):
                if rounds == 1:
                    return body(0)
                with engine.e.Fori(0, rounds) as i:
                    engine.start_loop(i, key, rounds)
                    body(i)
                    engine.end_loop()

            block(lambda: looped(pe, pe_round), lambda: looped(act, act_round), lambda: looped(dve, dve_round))

        def rwkv_chunks():
            n = NC_ // L
            rwkv("first front", None, (0, lambda i: 0))
            rwkv("context", (0, lambda i: i), (0, lambda i: i + 1), n - 1)
            rwkv("last of context", (0, lambda i: n - 1), (1, lambda i: 0))
            rwkv("latents", (1, lambda i: i), (1, lambda i: i + 1), n - 1)
            rwkv("last of latents", (1, lambda i: n - 1), None)

        ka1 = region(34584, 8)

        def rwkv_out():
            asum, bonus, inv, sq = (region(24064 + 2048 * i, KD, NL) for i in range(4))

            def pe_():
                for f in range(KD):
                    for d in range(2):
                        r = slice(64 * d, 64 * d + 64)
                        mms(bank("ro", 2 * f + d)[:, 0:NL], [(b_a2[r, f * P:(f + 1) * P], b_al[r, lat])]).then_inc(pe_done, pe.tick(("ro", 2 * f + d)))
                for f in range(KD):
                    pe.wait_ge(*at(("rk sum operand", f)))
                    pe.wait_ge(*at(("y square", f)))
                    o = bank("ro", 16 + f)
                    nc.tensor.matmul(o[:, 0:NL], blockones[:], asum[:, f, :], start=True, stop=True)
                    nc.tensor.matmul(o[:, NL:T], blockones[:], sq[:, f, :], start=True, stop=True).then_inc(pe_done, pe.tick(("ro", 16 + f)))
                for f in range(KD):
                    mms(bank("ro", 24 + f)[:, 0:NL], [(b_g2[:, f * P:(f + 1) * P], b_gl)]).then_inc(pe_done, pe.tick(("ro", 24 + f)))

            def act_():
                for f in range(KD):
                    for d in range(2):
                        j = 2 * f + d
                        act.wait_ge(*at(("ro", j)))
                        nc.scalar.activation((asum, bonus)[d][:, f, :], ps[j % 8][:, 0:NL], ACT.Sigmoid,
                                                      bias=col("rw_a0", 8 * d + f)).then_inc(act_done, act.tick(("ro", "read", j)))
                for f in range(KD):
                    nc.scalar.activation(sq[:, f, :], b_y[:, f, :], ACT.Square).then_inc(act_done, act.tick(("y square", f)))
                for f in range(KD):
                    act.wait_ge(*at(("ro", 16 + f)))
                    nc.scalar.activation(inv[:, f, :], ps[f][:, NL:T], ACT.Sqrt, bias=epsc[:], scale=1.0 / RN).then_inc(act_done, act.tick(("y root", f)))

            def dve_():
                one = nc.vector.scalar_tensor_tensor
                dve.step(nc.vector.tensor_scalar(ka2, ka1, 2.0, None, ALU.mult))
                for f in range(KD):
                    a = asum[:, f, :]
                    dve.wait_ge(*at(("ro", "read", 2 * f + 1)))
                    dve.step(vadd(a, a, bonus[:, f, :]))
                    dve.step(nc.vector.tensor_scalar(a, a, col("rw_ka", f), ka2[:, f:f + 1], ALU.mult, ALU.add))
                    dve.step(vmul(a, a, b_k[:, f, lat]))
                    dve.step(one(a, a, col("rw_rk", f), b_r[:, f, :], ALU.mult, ALU.mult), ("rk sum operand", f))
                for f in range(KD):
                    dve.wait_ge(*at(("ro", 16 + f)))
                    dve.wait_ge(*at(("y root", f)))
                    dve.step(vmul(bonus[:, f, :], b_v[:, f, lat], ps[f][:, 0:NL]))
                    dve.step(nc.vector.reciprocal(inv[:, f, :], inv[:, f, :]), ("ro", "read", 16 + f))
                    dve.step(one(b_y[:, f, :], b_y[:, f, :], col("rw_ln", f), inv[:, f, :], ALU.mult, ALU.mult))
                    dve.step(vadd(b_y[:, f, :], b_y[:, f, :], bonus[:, f, :]))
                for f in range(KD):
                    dve.wait_ge(*at(("ro", 24 + f)))
                    vmul(b_y[:, f, :], b_y[:, f, :], ps[f][:, 0:NL]).then_inc(dve_done, dve.tick(("ro", "read", 24 + f)))

            block(pe_, act_, dve_, None, lambda: stream_weights(piece_at["low"]))

        ka2 = region(34592, 8)

        def write_out():
            o = region(0, 2, D)

            def pe_():
                for tt in range(2):
                    for half in range(2):
                        j = 2 * tt + half
                        for k in range(4):
                            m = nc.tensor.transpose(ps[j][:, k * P:(k + 1) * P],
                                                    h[:, 4 * half + k, NC_ + tt * P:NC_ + (tt + 1) * P], ident[:])
                        m.then_inc(pe_done, pe.tick(("turned", j)))

            def dve_():
                for j in range(4):
                    dve.wait_ge(*at(("turned", j)))
                    nc.vector.tensor_copy(o[:, j // 2, 512 * (j % 2):512 * (j % 2) + 512], ps[j]).then_inc(dve_done, dve.tick(("copied", j)))

            def sp_():
                for tt in range(2):
                    sp.wait_ge(*at(("copied", 2 * tt + 1)))
                    nc.sync.dma_start(out[0, tt * P:(tt + 1) * P, :], o[:, tt, :]).then_inc(output_written, 16)
                sp.wait_ge(output_written, 32)

            block(pe_, None, dve_, None, sp_)

        load_all()
        modulation(0)
        modulated("u", 0, 0, a_u, 26704)
        project_gates()
        project_rest()
        mlstm()
        mlstm_out()
        ssd_prepare()
        ssd()
        ssd_norm()
        a_y = region(9216, KD, T)
        out_projection(0, a_oz, 16, 0, a_y, PARTS, PARTS + 8192, PARTS + 16384)
        residual("r", 1, a_y, 14336)
        moe(0, 0)
        modulation(1)
        modulated("u", 0, 0, b_u, 0)
        project_mla()
        norm_latent("nq", n_q, 3, NL, QR, "mla_qn")
        norm_latent("nkv", n_kv, 2, T, KVR, "mla_kvn")
        attention_heads()
        attention()
        project_rwkv()
        key_norms()
        rwkv_chunks()
        rwkv_out()
        b_out = region(24064, KD, T)
        out_projection(1, b_mix, 12, NC_, b_out, PARTS, 28160, 31232)
        residual("r", 1, b_out, 0, NC_)
        moe(1, NC_)
        write_out()
    return steps.new


_INS = ['x', 'c', 'ctx', 'c_ctx', 'w_mod', 'b_mod', 'norm_g', 'ab_w_in', 'ab_w_out', 'ml_i_bias', 'ml_f_bias', 'ml_norm',
        'ssd_conv_w', 'ssd_conv_b', 'ssd_dt_bias', 'ssd_a_log', 'ssd_d', 'ssd_norm', 'cd_w_in', 'cd_w_out', 'mla_qn',
        'mla_w_uq', 'mla_kvn', 'mla_w_ukv', 'rw_mu', 'rw_w0', 'rw_w2', 'rw_a0', 'rw_a2', 'rw_g2', 'rw_kk', 'rw_ka', 'rw_rk',
        'rw_ln', 'router_w', 'router_bias', 'exp_w_gate', 'exp_w_up', 'exp_w_down', 'sh_w_gate', 'sh_w_up', 'sh_w_down']


def kernel(**inputs):
    import concourse.bacc as _bacc
    from concourse.bass_utils import run_bass_kernel_spmd as _run

    arrays = {f"in_{n}_dram": np.ascontiguousarray(inputs[n]) for n in _INS}
    arrays.update({f"in_{n}_dram": a for n, a in constants().items()})

    def build(known):
        nc = _bacc.Bacc("TRN2", target_bir_lowering=False, num_devices=1)
        args = {n[3:-5]: nc.dram_tensor(n, a.shape, mybir.dt.from_np(a.dtype), kind="ExternalInput").ap()
                for n, a in arrays.items()}
        out = nc.dram_tensor("out_0_dram", (1, NL, D), F32, kind="ExternalOutput").ap()
        return nc, program(nc, args, out, known)

    _, known = build({})
    nc, _ = build(known)
    r = _run(nc, [arrays], core_ids=[0])
    return r.results[0]["out_0_dram"]
```
